# Optimizing a Trainium2 kernel written in Bass

```python
import math
import jax, jax.numpy as jnp
from jax import lax
import numpy as np

D_MODEL = 1024
BATCH = 1
SEQ = 256
DEPTH = 2

DA_HEADS = 4
DA_HEAD_DIM = 64
DA_QK_WIDTH = DA_HEADS * 2 * DA_HEAD_DIM
DA_WIDTH = DA_HEADS * 2 * DA_HEAD_DIM
MLA_HEADS = 8
MLA_Q_RANK = 256
MLA_KV_RANK = 128
MLA_NOPE = 64
MLA_ROPE = 32
MLA_V = 64
MLA_QK = MLA_NOPE + MLA_ROPE
MLA_WIDTH = MLA_HEADS * MLA_V
SSM_D_INNER = D_MODEL
SSM_HEAD_DIM = 64
SSM_HEADS = SSM_D_INNER // SSM_HEAD_DIM
SSM_GROUPS = 4
SSM_STATE = 128
SSM_CONV = 4
SSM_CHUNK = 128
SSM_CONV_DIM = SSM_D_INNER + 2 * SSM_GROUPS * SSM_STATE
FFN_DIM = 2816
FFN_CONV = 3
REL_BUCKETS = 32
REL_MAX_DIST = 128
ROPE_THETA = 10000.0
Q_BLOCK = 128
EPS = 1e-6

_IN_SIZES = (DA_QK_WIDTH, DA_QK_WIDTH, DA_WIDTH, MLA_Q_RANK, MLA_KV_RANK, MLA_ROPE,
             SSM_D_INNER, SSM_CONV_DIM, SSM_HEADS, 3 * D_MODEL)
IN_COLS = sum(_IN_SIZES)
_IN_OFFSETS = tuple(int(v) for v in np.cumsum(_IN_SIZES)[:-1])


f32 = jnp.float32

def _rmsnorm(x, w):
    xf = x.astype(f32)
    y = xf * lax.rsqrt(jnp.mean(xf * xf, axis=-1, keepdims=True) + EPS)
    return (y * w.astype(f32)).astype(x.dtype)

def _causal_dwconv(u, w, b):
    k = w.shape[0]
    out = lax.conv_general_dilated(u, w[:, None, :].astype(u.dtype), window_strides=(1,),
                                   padding=[(k - 1, 0)], dimension_numbers=('NWC', 'WIO', 'NWC'),
                                   feature_group_count=u.shape[-1])
    return out + b.astype(u.dtype)

def _rope(x, cos, sin):
    half = x.shape[-1] // 2
    x1, x2 = x[..., :half], x[..., half:]
    return jnp.concatenate([x1 * cos - x2 * sin, x2 * cos + x1 * sin], axis=-1).astype(x.dtype)

def _t5_bucket(dist):
    max_exact = REL_BUCKETS // 2
    d = jnp.maximum(dist, 0)
    large = max_exact + (jnp.log(jnp.maximum(d, 1).astype(f32) / max_exact)
                         / math.log(REL_MAX_DIST / max_exact) * (REL_BUCKETS - max_exact)).astype(jnp.int32)
    large = jnp.minimum(large, REL_BUCKETS - 1)
    return jnp.where(d < max_exact, d, large)

def _to_blocks(a):
    b, h, s = a.shape[:3]
    return jnp.moveaxis(a.reshape(b, h, s // Q_BLOCK, Q_BLOCK, *a.shape[3:]), 2, 0)

def _from_blocks(a):
    a = jnp.moveaxis(a, 0, 2)
    return a.reshape(a.shape[0], a.shape[1], a.shape[2] * a.shape[3], *a.shape[4:])

def _causal_mask(blk, seq):
    q_idx = blk * Q_BLOCK + jnp.arange(Q_BLOCK)
    return jnp.arange(seq)[None, :] <= q_idx[:, None]

def _diff_attention(q, k, v, positions, rel_table, lam):
    bsz, _, seq = q.shape[:3]
    nb = seq // Q_BLOCK
    scale = DA_HEAD_DIM ** -0.5
    pos_blocks = jnp.moveaxis(positions.reshape(bsz, nb, Q_BLOCK), 1, 0)

    def block(args):
        qb, qpos, blk = args
        s = jnp.einsum('bhqmd,bhkmd->mbhqk', qb, k).astype(f32) * scale
        dist = qpos[:, :, None] - positions[:, None, :]
        bias = jnp.take(rel_table, _t5_bucket(dist), axis=0)
        s = s + jnp.transpose(bias, (0, 3, 1, 2)).astype(f32)[None]
        s = jnp.where(_causal_mask(blk, seq), s, -jnp.inf)
        p = jax.nn.softmax(s, axis=-1)
        w = p[0] - lam * p[1]
        return jnp.einsum('bhqk,bhkv->bhqv', w.astype(v.dtype), v)

    return _from_blocks(lax.map(block, (_to_blocks(q), pos_blocks, jnp.arange(nb))))

def _mla_attention(q, k, v):
    seq = q.shape[2]
    nb = seq // Q_BLOCK
    scale = MLA_QK ** -0.5

    def block(args):
        qb, blk = args
        s = jnp.einsum('bhqd,bhkd->bhqk', qb, k).astype(f32) * scale
        s = jnp.where(_causal_mask(blk, seq), s, -jnp.inf)
        p = jax.nn.softmax(s, axis=-1)
        return jnp.einsum('bhqk,bhkd->bhqd', p.astype(v.dtype), v)

    return _from_blocks(lax.map(block, (_to_blocks(q), jnp.arange(nb))))

def _ssd(xs, dt, a, bm, cm):
    bsz, seq = xs.shape[:2]
    nc, L = seq // SSM_CHUNK, SSM_CHUNK
    G, R = SSM_GROUPS, SSM_HEADS // SSM_GROUPS
    xdt = (xs.astype(f32) * dt[..., None]).reshape(bsz, nc, L, G, R, SSM_HEAD_DIM)
    da = (dt * a).reshape(bsz, nc, L, G, R)
    bm = bm.astype(f32).reshape(bsz, nc, L, G, SSM_STATE)
    cm = cm.astype(f32).reshape(bsz, nc, L, G, SSM_STATE)
    cs = jnp.cumsum(da, axis=2)
    causal = jnp.tril(jnp.ones((L, L), bool))[None, None, :, :, None, None]
    seg = cs[:, :, :, None] - cs[:, :, None, :]
    decay = jnp.exp(jnp.where(causal, seg, -jnp.inf))
    cb = jnp.einsum('bclgn,bcsgn->bclsg', cm, bm)
    y_diag = jnp.einsum('bclsgr,bcsgrp->bclgrp', cb[..., None] * decay, xdt)
    to_end = jnp.exp(cs[:, :, -1:] - cs)
    states = jnp.einsum('bclgn,bclgrp->bcgrpn', bm, xdt * to_end[..., None])
    chunk_decay = jnp.exp(cs[:, :, -1])

    def step(h, inp):
        st, dec = inp
        return dec[..., None, None] * h + st, h

    init = jnp.zeros((bsz, G, R, SSM_HEAD_DIM, SSM_STATE), f32)
    _, prev = lax.scan(step, init, (jnp.moveaxis(states, 1, 0), jnp.moveaxis(chunk_decay, 1, 0)))
    prev = jnp.moveaxis(prev, 0, 1)
    y_off = jnp.einsum('bclgn,bcgrpn->bclgrp', cm, prev) * jnp.exp(cs)[..., None]
    return (y_diag + y_off).reshape(bsz, seq, SSM_HEADS, SSM_HEAD_DIM)

def first_inputs(seed: int = 0) -> dict:
    key = jax.random.key(seed)
    ks = iter(jax.random.split(key, 40))

    def nrm(shape, scale):
        return jax.random.normal(next(ks), shape, f32) * scale

    def gain(shape):
        return 1.0 + nrm(shape, 0.02)

    L = DEPTH
    x = nrm((BATCH, SEQ, D_MODEL), 1.0)
    c = nrm((BATCH, D_MODEL), 1.0)
    positions = jnp.arange(SEQ, dtype=jnp.int32)[None, :] + jax.random.randint(
        next(ks), (BATCH, 1), 0, 1024, dtype=jnp.int32)
    rel_bias = nrm((REL_BUCKETS, DA_HEADS), 0.5)
    ada_w = nrm((L, D_MODEL, 6 * D_MODEL), D_MODEL ** -0.5)
    ada_b = nrm((L, 6 * D_MODEL), 0.02)
    norm_mix = gain((L, D_MODEL))
    norm_ffn = gain((L, D_MODEL))
    w_in = nrm((L, D_MODEL, IN_COLS), D_MODEL ** -0.5)
    da_q_norm = gain((L, DA_HEAD_DIM))
    da_k_norm = gain((L, DA_HEAD_DIM))
    da_lambda = nrm((L, 4, DA_HEAD_DIM), 0.1)
    da_subln = gain((L, 2 * DA_HEAD_DIM))
    mla_q_a_norm = gain((L, MLA_Q_RANK))
    mla_kv_a_norm = gain((L, MLA_KV_RANK))
    mla_w_uq = nrm((L, MLA_Q_RANK, MLA_HEADS * MLA_QK), MLA_Q_RANK ** -0.5)
    mla_w_ukv = nrm((L, MLA_KV_RANK, MLA_HEADS * (MLA_NOPE + MLA_V)), MLA_KV_RANK ** -0.5)
    mla_q_norm = gain((L, MLA_QK))
    mla_k_norm = gain((L, MLA_QK))
    ssm_conv_w = nrm((L, SSM_CONV, SSM_CONV_DIM), SSM_CONV ** -0.5)
    ssm_conv_b = nrm((L, SSM_CONV_DIM), 0.02)
    dt0 = jnp.exp(jax.random.uniform(next(ks), (L, SSM_HEADS), f32, math.log(1e-3), math.log(1e-1)))
    ssm_dt_bias = dt0 + jnp.log(-jnp.expm1(-dt0))
    ssm_a_log = jnp.log(jax.random.uniform(next(ks), (L, SSM_HEADS), f32, 1.0, 16.0))
    ssm_d = 1.0 + nrm((L, SSM_HEADS), 0.1)
    ssm_norm = gain((L, SSM_D_INNER))
    w_branch_a = nrm((L, DA_WIDTH, D_MODEL), DA_WIDTH ** -0.5)
    w_branch_b = nrm((L, MLA_WIDTH, D_MODEL), MLA_WIDTH ** -0.5)
    w_branch_c = nrm((L, SSM_D_INNER, D_MODEL), SSM_D_INNER ** -0.5)
    w_out = nrm((L, D_MODEL, D_MODEL), D_MODEL ** -0.5)
    ffn_w_up = nrm((L, D_MODEL, 2 * FFN_DIM), D_MODEL ** -0.5)
    ffn_conv_w = nrm((L, FFN_CONV, 2 * FFN_DIM), FFN_CONV ** -0.5)
    ffn_conv_b = nrm((L, 2 * FFN_DIM), 0.02)
    ffn_w_down = nrm((L, FFN_DIM, D_MODEL), FFN_DIM ** -0.5)
    return {'x': x, 'c': c, 'positions': positions, 'rel_bias': rel_bias,
            'ada_w': ada_w, 'ada_b': ada_b, 'norm_mix': norm_mix, 'norm_ffn': norm_ffn, 'w_in': w_in,
            'da_q_norm': da_q_norm, 'da_k_norm': da_k_norm, 'da_lambda': da_lambda, 'da_subln': da_subln,
            'mla_q_a_norm': mla_q_a_norm, 'mla_kv_a_norm': mla_kv_a_norm, 'mla_w_uq': mla_w_uq,
            'mla_w_ukv': mla_w_ukv, 'mla_q_norm': mla_q_norm, 'mla_k_norm': mla_k_norm,
            'ssm_conv_w': ssm_conv_w, 'ssm_conv_b': ssm_conv_b, 'ssm_dt_bias': ssm_dt_bias,
            'ssm_a_log': ssm_a_log, 'ssm_d': ssm_d, 'ssm_norm': ssm_norm,
            'w_branch_a': w_branch_a, 'w_branch_b': w_branch_b, 'w_branch_c': w_branch_c, 'w_out': w_out,
            'ffn_w_up': ffn_w_up, 'ffn_conv_w': ffn_conv_w, 'ffn_conv_b': ffn_conv_b, 'ffn_w_down': ffn_w_down}

def first_block(x, c, positions, rel_bias, ada_w, ada_b, norm_mix, norm_ffn, w_in,
              da_q_norm, da_k_norm, da_lambda, da_subln,
              mla_q_a_norm, mla_kv_a_norm, mla_w_uq, mla_w_ukv, mla_q_norm, mla_k_norm,
              ssm_conv_w, ssm_conv_b, ssm_dt_bias, ssm_a_log, ssm_d, ssm_norm,
              w_branch_a, w_branch_b, w_branch_c, w_out,
              ffn_w_up, ffn_conv_w, ffn_conv_b, ffn_w_down):
    bsz, seq, _ = x.shape
    inv_freq = ROPE_THETA ** (-jnp.arange(0, MLA_ROPE, 2, dtype=f32) / MLA_ROPE)
    ang = positions.astype(f32)[..., None] * inv_freq
    cos, sin = jnp.cos(ang), jnp.sin(ang)
    c_act = jax.nn.silu(c)

    for l in range(DEPTH):
        mod = c_act @ ada_w[l] + ada_b[l]
        sh_m, sc_m, g_m, sh_f, sc_f, g_f = jnp.split(mod[:, None, :], 6, axis=-1)

        h = _rmsnorm(x, norm_mix[l]) * (1 + sc_m) + sh_m
        proj = h @ w_in[l]
        qa, ka, va, cq, ckv, kr, z, xbc, dt_raw, gates = jnp.split(proj, _IN_OFFSETS, axis=-1)

        qa = _rmsnorm(qa.reshape(bsz, seq, DA_HEADS, 2, DA_HEAD_DIM), da_q_norm[l]).transpose(0, 2, 1, 3, 4)
        ka = _rmsnorm(ka.reshape(bsz, seq, DA_HEADS, 2, DA_HEAD_DIM), da_k_norm[l]).transpose(0, 2, 1, 3, 4)
        va = va.reshape(bsz, seq, DA_HEADS, 2 * DA_HEAD_DIM).transpose(0, 2, 1, 3)
        lam_init = 0.8 - 0.6 * math.exp(-0.3 * l)
        lp = da_lambda[l].astype(f32)
        lam = jnp.exp(jnp.sum(lp[0] * lp[1])) - jnp.exp(jnp.sum(lp[2] * lp[3])) + lam_init
        oa = _diff_attention(qa, ka, va, positions, rel_bias, lam)
        oa = _rmsnorm(oa, da_subln[l]) * (1.0 - lam_init)
        ya = oa.transpose(0, 2, 1, 3).reshape(bsz, seq, DA_WIDTH)

        cq = _rmsnorm(cq, mla_q_a_norm[l])
        qb = (cq @ mla_w_uq[l]).reshape(bsz, seq, MLA_HEADS, MLA_QK)
        ckv = _rmsnorm(ckv, mla_kv_a_norm[l])
        kv = (ckv @ mla_w_ukv[l]).reshape(bsz, seq, MLA_HEADS, MLA_NOPE + MLA_V)
        k_nope, vb = kv[..., :MLA_NOPE], kv[..., MLA_NOPE:]
        kb = jnp.concatenate([k_nope, jnp.broadcast_to(kr[:, :, None, :], (bsz, seq, MLA_HEADS, MLA_ROPE))], axis=-1)
        qb = _rmsnorm(qb, mla_q_norm[l])
        kb = _rmsnorm(kb, mla_k_norm[l])
        cos_h, sin_h = cos[:, :, None, :], sin[:, :, None, :]
        qb = jnp.concatenate([qb[..., :MLA_NOPE], _rope(qb[..., MLA_NOPE:], cos_h, sin_h)], axis=-1)
        kb = jnp.concatenate([kb[..., :MLA_NOPE], _rope(kb[..., MLA_NOPE:], cos_h, sin_h)], axis=-1)
        ob = _mla_attention(qb.transpose(0, 2, 1, 3), kb.transpose(0, 2, 1, 3), vb.transpose(0, 2, 1, 3))
        yb = ob.transpose(0, 2, 1, 3).reshape(bsz, seq, MLA_WIDTH)

        xbc = jax.nn.silu(_causal_dwconv(xbc, ssm_conv_w[l], ssm_conv_b[l]))
        xs, bm, cm = jnp.split(xbc, [SSM_D_INNER, SSM_D_INNER + SSM_GROUPS * SSM_STATE], axis=-1)
        xs = xs.reshape(bsz, seq, SSM_HEADS, SSM_HEAD_DIM)
        bm = bm.reshape(bsz, seq, SSM_GROUPS, SSM_STATE)
        cm = cm.reshape(bsz, seq, SSM_GROUPS, SSM_STATE)
        dt = jax.nn.softplus(dt_raw.astype(f32) + ssm_dt_bias[l].astype(f32))
        a = -jnp.exp(ssm_a_log[l].astype(f32))
        ys = _ssd(xs, dt, a, bm, cm) + ssm_d[l].astype(f32)[:, None] * xs.astype(f32)
        ys = ys.reshape(bsz, seq, SSM_D_INNER) * jax.nn.silu(z.astype(f32))
        ys = _rmsnorm(ys.reshape(bsz, seq, SSM_GROUPS, -1), ssm_norm[l].reshape(SSM_GROUPS, -1))
        ys = ys.reshape(bsz, seq, SSM_D_INNER).astype(x.dtype)

        ga, gb, gc = jnp.split(jax.nn.sigmoid(gates), 3, axis=-1)
        merged = ga * (ya @ w_branch_a[l]) + gb * (yb @ w_branch_b[l]) + gc * (ys @ w_branch_c[l])
        x = x + g_m * (merged @ w_out[l])

        h = _rmsnorm(x, norm_ffn[l]) * (1 + sc_f) + sh_f
        u = _causal_dwconv(h @ ffn_w_up[l], ffn_conv_w[l], ffn_conv_b[l])
        ua, uv = jnp.split(u, 2, axis=-1)
        x = x + g_f * ((jax.nn.silu(ua) * uv) @ ffn_w_down[l])
    return x


DEPTH_2 = 1

HEAD_DIM = 64
MIX_WIDTH = D_MODEL
A_HEADS = MIX_WIDTH // (2 * HEAD_DIM)
A_KV_HEADS = max(1, A_HEADS // 4)
B_HEADS = MIX_WIDTH // HEAD_DIM - A_HEADS
A_WIDTH = A_HEADS * HEAD_DIM
A_KV_WIDTH = A_KV_HEADS * HEAD_DIM
B_WIDTH = B_HEADS * HEAD_DIM
IN_WIDTH = A_WIDTH + 2 * A_KV_WIDTH + 3 * B_WIDTH
IN_SPLITS = (A_WIDTH, A_WIDTH + A_KV_WIDTH, A_WIDTH + 2 * A_KV_WIDTH,
             A_WIDTH + 2 * A_KV_WIDTH + B_WIDTH, A_WIDTH + 2 * A_KV_WIDTH + 2 * B_WIDTH)
GRID_W = 64
DILATED_PATTERNS = ((128, 1), (512, 4), (2048, 16))
SUBSEQ_BLOCK = 64
N_GROUPS = 4
EXPERTS_PER_GROUP = 8
N_EXPERTS = N_GROUPS * EXPERTS_PER_GROUP
TOP_K = 2
D_EXPERT = D_MODEL // 2
MOE_BLOCK = 512
NEG_INF = -1e30


def _rms_norm(x, g):
    xf = x.astype(jnp.float32)
    y = xf * lax.rsqrt(jnp.mean(xf * xf, axis=-1, keepdims=True) + EPS)
    return (y * g.astype(jnp.float32)).astype(x.dtype)

def _rope_inv_freq(dim):
    return 1.0 / (ROPE_THETA ** (jnp.arange(0, dim, 2, dtype=jnp.float32) / dim))

def _apply_rotary(x, angles):
    cos, sin = jnp.cos(angles), jnp.sin(angles)
    xf = x.astype(jnp.float32)
    x1, x2 = jnp.split(xf, 2, axis=-1)
    return jnp.concatenate([x1 * cos - x2 * sin, x2 * cos + x1 * sin], axis=-1).astype(x.dtype)

def _axial_angles(seq_len):
    rows = seq_len // GRID_W
    row = jnp.repeat(jnp.arange(rows, dtype=jnp.float32), GRID_W)
    col = jnp.tile(jnp.arange(GRID_W, dtype=jnp.float32), rows)
    f = _rope_inv_freq(HEAD_DIM // 2)
    return jnp.concatenate([row[:, None] * f, col[:, None] * f], axis=-1)

def _linear_angles(seq_len):
    t = jnp.arange(seq_len, dtype=jnp.float32)
    return t[:, None] * _rope_inv_freq(HEAD_DIM)

def _global_axial_gqa(q, k, v, q_norm_g, k_norm_g):
    b, s, _ = q.shape
    grp = A_HEADS // A_KV_HEADS
    q = q.reshape(b, s, A_KV_HEADS, grp, HEAD_DIM).transpose(0, 2, 3, 1, 4)
    k = k.reshape(b, s, A_KV_HEADS, HEAD_DIM).transpose(0, 2, 1, 3)
    v = v.reshape(b, s, A_KV_HEADS, HEAD_DIM).transpose(0, 2, 1, 3)
    ang = _axial_angles(s)
    q = _apply_rotary(_rms_norm(q, q_norm_g), ang)
    k = _apply_rotary(_rms_norm(k, k_norm_g), ang)
    nq = s // Q_BLOCK
    qb = jnp.moveaxis(q.reshape(b, A_KV_HEADS, grp, nq, Q_BLOCK, HEAD_DIM), 3, 0)
    scale = HEAD_DIM ** -0.5

    def block(qblk):
        sc = jnp.einsum('bkgqd,bksd->bkgqs', qblk, k, preferred_element_type=jnp.float32) * scale
        p = jax.nn.softmax(sc, axis=-1).astype(v.dtype)
        return jnp.einsum('bkgqs,bksd->bkgqd', p, v)

    o = lax.map(block, qb)
    o = jnp.moveaxis(o, 0, 3).reshape(b, A_KV_HEADS, grp, s, HEAD_DIM)
    return o.transpose(0, 3, 1, 2, 4).reshape(b, s, A_WIDTH)

def _dilated_window(q, k, v, window, dilation):
    b, h, s, d = q.shape
    r = window // (2 * dilation)
    L = s // dilation

    def to_sub(t):
        return t.reshape(b, h, L, dilation, d).transpose(0, 1, 3, 2, 4)

    qs, ks, vs = to_sub(q), to_sub(k), to_sub(v)
    nblk = -(-L // SUBSEQ_BLOCK)
    lp = nblk * SUBSEQ_BLOCK
    pad4 = ((0, 0), (0, 0), (0, 0))
    qs = jnp.pad(qs, pad4 + ((0, lp - L), (0, 0)))
    kpad = jnp.pad(ks, pad4 + ((r, lp - L + r), (0, 0)))
    vpad = jnp.pad(vs, pad4 + ((r, lp - L + r), (0, 0)))
    kwin = SUBSEQ_BLOCK + 2 * r
    kidx = jnp.arange(nblk)[:, None] * SUBSEQ_BLOCK + jnp.arange(kwin)[None, :]
    kb = jnp.take(kpad, kidx, axis=3)
    vb = jnp.take(vpad, kidx, axis=3)
    qb = qs.reshape(b, h, dilation, nblk, SUBSEQ_BLOCK, d)
    sc = jnp.einsum('bhrnqd,bhrnkd->bhrnqk', qb, kb, preferred_element_type=jnp.float32) * (d ** -0.5)
    qpos = jnp.arange(lp).reshape(nblk, SUBSEQ_BLOCK)
    kpos = kidx - r
    mask = (jnp.abs(qpos[:, :, None] - kpos[:, None, :]) <= r) & ((kpos >= 0) & (kpos < L))[:, None, :]
    sc = jnp.where(mask, sc, NEG_INF)
    m = jnp.max(sc, axis=-1, keepdims=True)
    p = jnp.exp(sc - m)
    den = jnp.sum(p, axis=-1, keepdims=True)
    o = jnp.einsum('bhrnqk,bhrnkd->bhrnqd', p.astype(vb.dtype), vb,
                   preferred_element_type=jnp.float32) / den
    lse = (m + jnp.log(den))[..., 0]
    o = o.astype(v.dtype).reshape(b, h, dilation, lp, d)[:, :, :, :L]
    o = o.transpose(0, 1, 3, 2, 4).reshape(b, h, s, d)
    lse = lse.reshape(b, h, dilation, lp)[:, :, :, :L].transpose(0, 1, 3, 2).reshape(b, h, s)
    return o, lse

def _longnet_mixture(q, k, v):
    b, s, _ = q.shape
    q = q.reshape(b, s, B_HEADS, HEAD_DIM).transpose(0, 2, 1, 3)
    k = k.reshape(b, s, B_HEADS, HEAD_DIM).transpose(0, 2, 1, 3)
    v = v.reshape(b, s, B_HEADS, HEAD_DIM).transpose(0, 2, 1, 3)
    ang = _linear_angles(s)
    q = _apply_rotary(q, ang)
    k = _apply_rotary(k, ang)
    outs, lses = [], []
    for window, dilation in DILATED_PATTERNS:
        o, lse = _dilated_window(q, k, v, window, dilation)
        outs.append(o)
        lses.append(lse)
    w = jax.nn.softmax(jnp.stack(lses, axis=0), axis=0).astype(v.dtype)
    o = jnp.einsum('pbhs,pbhsd->bhsd', w, jnp.stack(outs, axis=0))
    return o.transpose(0, 2, 1, 3).reshape(b, s, B_WIDTH)

def _hierarchical_moe(x, router_group_w, router_group_b, router_expert_w, router_expert_b,
                      w_gate, w_up, w_down):
    b, s, dm = x.shape
    n = b * s
    xt = x.reshape(n, dm)
    g_logits = (xt @ router_group_w).astype(jnp.float32) + router_group_b.astype(jnp.float32)
    g_prob = jax.nn.softmax(g_logits, axis=-1)
    g_top_p, g_top = lax.top_k(g_prob, 1)
    e_logits = (xt @ router_expert_w).astype(jnp.float32) + router_expert_b.astype(jnp.float32)
    e_logits = e_logits.reshape(n, N_GROUPS, EXPERTS_PER_GROUP)
    e_in_group = jnp.take_along_axis(e_logits, g_top[:, :, None], axis=1)[:, 0]
    e_top_logit, e_top = lax.top_k(e_in_group, TOP_K)
    gates = g_top_p * jax.nn.softmax(e_top_logit, axis=-1)
    expert_id = g_top * EXPERTS_PER_GROUP + e_top

    nk = n * TOP_K
    flat_e = expert_id.reshape(nk).astype(jnp.int32)
    flat_tok = jnp.arange(nk, dtype=jnp.int32) // TOP_K
    flat_gate = gates.reshape(nk)
    order = jnp.argsort(flat_e)
    se = flat_e[order]
    counts = jnp.bincount(flat_e, length=N_EXPERTS)
    start = jnp.cumsum(counts) - counts
    padded = (counts + MOE_BLOCK - 1) // MOE_BLOCK * MOE_BLOCK
    pend = jnp.cumsum(padded)
    pstart = pend - padded
    dest = pstart[se] + (jnp.arange(nk, dtype=jnp.int32) - start[se])
    n_blocks = -(-nk // MOE_BLOCK) + N_EXPERTS
    rows = n_blocks * MOE_BLOCK
    row_tok = jnp.zeros((rows,), jnp.int32).at[dest].set(flat_tok[order])
    row_gate = jnp.zeros((rows,), x.dtype).at[dest].set(flat_gate[order].astype(x.dtype))
    block_e = jnp.minimum(jnp.searchsorted(pend, jnp.arange(n_blocks) * MOE_BLOCK, side='right'),
                          N_EXPERTS - 1).astype(jnp.int32)

    def expert_block(args):
        e, tok = args
        xb = xt[tok]
        hdn = jax.nn.silu(xb @ w_gate[e]) * (xb @ w_up[e])
        return hdn @ w_down[e]

    yb = lax.map(expert_block, (block_e, row_tok.reshape(n_blocks, MOE_BLOCK)))
    y = jnp.zeros((n, dm), x.dtype).at[row_tok].add(yb.reshape(rows, dm) * row_gate[:, None])
    return y.reshape(b, s, dm)

def second_inputs(seed: int = 0) -> dict:
    key = jax.random.key(seed)
    ks = jax.random.split(key, 20)
    f32 = jnp.float32

    def nrm(k, shape, scale):
        return jax.random.normal(k, shape, f32) * scale

    def gain(k, shape):
        return 1.0 + 0.02 * jax.random.normal(k, shape, f32)

    return {
        "x": jax.random.normal(ks[0], (BATCH, SEQ, D_MODEL), f32),
        "norm1_g": gain(ks[1], (DEPTH_2, D_MODEL)),
        "w_in": nrm(ks[2], (DEPTH_2, D_MODEL, IN_WIDTH), D_MODEL ** -0.5),
        "q_norm_g": gain(ks[3], (DEPTH_2, HEAD_DIM)),
        "k_norm_g": gain(ks[4], (DEPTH_2, HEAD_DIM)),
        "out_norm_a_g": gain(ks[5], (DEPTH_2, A_WIDTH)),
        "out_norm_b_g": gain(ks[6], (DEPTH_2, B_WIDTH)),
        "w_out": nrm(ks[7], (DEPTH_2, MIX_WIDTH, D_MODEL), MIX_WIDTH ** -0.5),
        "norm2_g": gain(ks[8], (DEPTH_2, D_MODEL)),
        "router_group_w": nrm(ks[9], (DEPTH_2, D_MODEL, N_GROUPS), D_MODEL ** -0.5),
        "router_group_b": nrm(ks[10], (DEPTH_2, N_GROUPS), 0.01),
        "router_expert_w": nrm(ks[11], (DEPTH_2, D_MODEL, N_EXPERTS), D_MODEL ** -0.5),
        "router_expert_b": nrm(ks[12], (DEPTH_2, N_EXPERTS), 0.01),
        "w_gate": nrm(ks[13], (DEPTH_2, N_EXPERTS, D_MODEL, D_EXPERT), D_MODEL ** -0.5),
        "w_up": nrm(ks[14], (DEPTH_2, N_EXPERTS, D_MODEL, D_EXPERT), D_MODEL ** -0.5),
        "w_down": nrm(ks[15], (DEPTH_2, N_EXPERTS, D_EXPERT, D_MODEL), D_EXPERT ** -0.5),
        "final_norm_g": gain(ks[16], (D_MODEL,)),
    }

def second_block(x, norm1_g, w_in, q_norm_g, k_norm_g, out_norm_a_g, out_norm_b_g, w_out,
              norm2_g, router_group_w, router_group_b, router_expert_w, router_expert_b,
              w_gate, w_up, w_down, final_norm_g):
    h = x
    for l in range(DEPTH_2):
        u = _rms_norm(h, norm1_g[l])
        proj = u @ w_in[l]
        qa, ka, va, qb, kb, vb = jnp.split(proj, IN_SPLITS, axis=-1)
        oa = _rms_norm(_global_axial_gqa(qa, ka, va, q_norm_g[l], k_norm_g[l]), out_norm_a_g[l])
        ob = _rms_norm(_longnet_mixture(qb, kb, vb), out_norm_b_g[l])
        h = h + jnp.concatenate([oa, ob], axis=-1) @ w_out[l]
        h = h + _hierarchical_moe(_rms_norm(h, norm2_g[l]), router_group_w[l], router_group_b[l],
                                  router_expert_w[l], router_expert_b[l],
                                  w_gate[l], w_up[l], w_down[l])
    return _rms_norm(h, final_norm_g)


def setup_inputs(seed=0):
    out = dict(first_inputs(seed))
    for name, value in second_inputs(seed + 1).items():
        if name != "x":
            out[name + "_2"] = value
    return out


def reference(
    x, c, positions, rel_bias, ada_w, ada_b, norm_mix, norm_ffn, w_in, da_q_norm, da_k_norm,
    da_lambda, da_subln, mla_q_a_norm, mla_kv_a_norm, mla_w_uq, mla_w_ukv, mla_q_norm,
    mla_k_norm, ssm_conv_w, ssm_conv_b, ssm_dt_bias, ssm_a_log, ssm_d, ssm_norm, w_branch_a,
    w_branch_b, w_branch_c, w_out, ffn_w_up, ffn_conv_w, ffn_conv_b, ffn_w_down, norm1_g_2,
    w_in_2, q_norm_g_2, k_norm_g_2, out_norm_a_g_2, out_norm_b_g_2, w_out_2, norm2_g_2,
    router_group_w_2, router_group_b_2, router_expert_w_2, router_expert_b_2, w_gate_2, w_up_2,
    w_down_2, final_norm_g_2,
):
    x = first_block(
        x, c, positions, rel_bias, ada_w, ada_b, norm_mix, norm_ffn, w_in, da_q_norm, da_k_norm,
        da_lambda, da_subln, mla_q_a_norm, mla_kv_a_norm, mla_w_uq, mla_w_ukv, mla_q_norm,
        mla_k_norm, ssm_conv_w, ssm_conv_b, ssm_dt_bias, ssm_a_log, ssm_d, ssm_norm, w_branch_a,
        w_branch_b, w_branch_c, w_out, ffn_w_up, ffn_conv_w, ffn_conv_b, ffn_w_down,
    )
    return second_block(
        x, norm1_g_2, w_in_2, q_norm_g_2, k_norm_g_2, out_norm_a_g_2, out_norm_b_g_2, w_out_2,
        norm2_g_2, router_group_w_2, router_group_b_2, router_expert_w_2, router_expert_b_2,
        w_gate_2, w_up_2, w_down_2, final_norm_g_2,
    )


_drawn_inputs = setup_inputs


def setup_inputs(seed=0):
    import zlib

    import numpy as np

    out = dict(_drawn_inputs(seed))
    spreads = {}
    factors = {'norm_mix': 3.187,
     'da_q_norm': 8.0,
     'da_k_norm': 5.042,
     'da_subln': 3.604,
     'mla_q_a_norm': 6.997,
     'mla_kv_a_norm': 5.219,
     'mla_q_norm': 5.474,
     'mla_k_norm': 8.0,
     'ssm_conv_b': 3.344,
     'ssm_norm': 2.969,
     'q_norm_g_2': 7.758,
     'k_norm_g_2': 4.533,
     'out_norm_a_g_2': 25.531,
     'out_norm_b_g_2': 25.237,
     'router_group_b_2': 33.344,
     'router_expert_b_2': 51.016,
     'final_norm_g_2': 7.548,
     'norm2_g_2': 8.0}
    for name, (base, spread) in spreads.items():
        noise = np.random.default_rng([zlib.crc32(name.encode()), seed]).standard_normal(out[name].shape)
        drawn = base * np.exp(spread * noise) if base else spread * noise
        out[name] = __import__('jax').numpy.asarray(drawn.astype(out[name].dtype))
    for name, factor in factors.items():
        out[name] = (out[name] * factor).astype(out[name].dtype)
    return out
```

```python
from contextlib import ExitStack

import numpy as np

import concourse.bass as bass
from concourse import mybir

F32 = mybir.dt.float32
I32 = mybir.dt.int32
ALU = mybir.AluOpType
ACT = mybir.ActivationFunctionType
AX = mybir.AxisListType.X

P = 128
D = 1024
SEQ = 256
T = SEQ // P
KT = D // P
DEPTH = 2
EPS = 1e-6
NEG = -1e30

DA_H, DA_D = 4, 64
ML_H, ML_N, ML_R, ML_V = 8, 64, 32, 64
ML_QK = ML_N + ML_R
Q_RANK, KV_RANK = 256, 128
SM_H, SM_D, SM_G, SM_N = 16, 64, 4, 128
FFN = 2816
FT = FFN // P
BUCKETS, MAX_DIST = 32, 128
LAM_INIT = [0.8 - 0.6 * float(np.exp(-0.3 * l)) for l in range(DEPTH)]

C_Q, C_K, C_V, C_ML = 0, 512, 1024, 1536
ML_W = Q_RANK + KV_RANK + ML_R
C_Z = C_ML + ML_W
C_XBC = C_Z + D
C_DT = C_XBC + 2048
C_G = C_DT + SM_H

H2, D2 = 8, 64
GROUPS, EPG, DE = 4, 8, 512
GRID_W, THETA = 64, 10000.0

SLOTS = 4
SLOT = 4096

K_ID, K_TRI, K_CM = 0, 128, 256
K_IOTA = K_CM + 384
K_INV = K_IOTA + 128
K_THR = K_INV + 16
K_LAM = K_THR + 32
K_TIE = K_LAM + 4
K_AC, K_AS = K_TIE + 8, K_TIE + 72
K_LC, K_LS = K_TIE + 136, K_TIE + 200
K_LNC = K_TIE + 264
K_END = K_LNC + 512

V_FW, V_FB, V_ADA, V_NM, V_NF, V_SN, V_QA, V_KVA, V_SUB = 0, 132, 176, 224, 232, 240, 248, 250, 251
V_SW, V_SB, V_DQ, V_DK, V_END = 256, 320, 336, 337, 338
W_N1, W_OA, W_OB, W_N2, W_FN, W_END = 0, 8, 12, 16, 24, 32
R_MQ, R_MK, R_DTB, R_AL, R_SD, R_LP, R_END = 0, 96, 192, 208, 224, 240, 496


def shape_constants():
    k = np.zeros((P, K_END), np.float32)
    i = np.arange(P)
    k[:, K_ID:K_ID + P] = np.eye(P)
    k[:, K_TRI:K_TRI + P] = i[:, None] <= i[None, :]
    causal = np.where(i[None, :] <= i[:, None], 0.0, NEG)
    k[:, K_CM:K_CM + P] = causal
    k[:, K_CM + 2 * P:K_CM + 3 * P] = causal
    k[:, K_IOTA:K_IOTA + P] = i[None, :]
    k[:, K_INV:K_INV + 16] = np.float32(THETA) ** (-np.arange(0, ML_R, 2, dtype=np.float32) / np.float32(ML_R))
    half = BUCKETS // 2
    thr = list(range(half + 1)) + [
        min(d for d in range(half, MAX_DIST + 1) if (d / half) ** half >= (MAX_DIST / half) ** j * (1 - 1e-12))
        for j in range(1, half)]
    k[:, K_THR:K_THR + BUCKETS] = np.array(thr[:BUCKETS], np.float32)
    k[:, K_LAM:K_LAM + 2] = LAM_INIT
    k[:, K_LAM + 2:K_LAM + 4] = [1.0 - v for v in LAM_INIT]
    k[:, K_TIE:K_TIE + 8] = 8 - np.arange(8)
    t = np.arange(SEQ)
    inv = lambda n: (1.0 / (np.float32(THETA) ** (np.arange(0, n, 2, dtype=np.float32) / np.float32(n)))).astype(np.float32)
    axial = np.concatenate([(t // GRID_W).astype(np.float32)[:, None] * inv(D2 // 2),
                            (t % GRID_W).astype(np.float32)[:, None] * inv(D2 // 2)], 1)
    linear = t.astype(np.float32)[:, None] * inv(D2)
    for a, c, s in ((axial, K_AC, K_AS), (linear, K_LC, K_LS)):
        for n in range(T):
            k[:, c + 32 * n:c + 32 * n + 32] = np.cos(a[n * P:(n + 1) * P])
            k[:, s + 32 * n:s + 32 * n + 32] = np.sin(a[n * P:(n + 1) * P])
    count = np.zeros((SEQ, SEQ))
    for window, dil in ((128, 1), (512, 4), (2048, 16)):
        r = window // (2 * dil)
        same = (t[:, None] % dil) == (t[None, :] % dil)
        count += same & (np.abs(t[:, None] // dil - t[None, :] // dil) <= r)
    lnc = np.where(count > 0, np.log(np.maximum(count, 1)), NEG)
    for n in range(T):
        k[:, K_LNC + SEQ * n:K_LNC + SEQ * (n + 1)] = lnc[n * P:(n + 1) * P]
    return k


LAYER_CHUNKS = (["ada0", "ada1", "ada2", "ada3", "q", "k", "v", "ml", "uqkv", "ga0", "ga1", "gb0", "gb1",
                 "z0", "z1", "ba"] + [f"xbc{i}" for i in range(4)] + ["bb", "gc0", "gc1", "ada4", "ada5", "bc0", "bc1",
                 "wo0", "wo1"] + [f"ada{i}" for i in range(6, 12)] + [f"up{i}" for i in range(11)]
                + [f"dn{i}" for i in range(6)])
MID_CHUNKS = ["m_qa", "m_kva", "m_qb", "m_kb", "m_vb", "m_wo0", "m_wo1"]
PASS_CHUNKS = ["e_g0", "e_u0"] + [x for e in range(1, EPG) for x in (f"e_g{e}", f"e_u{e}", f"e_d{e - 1}")] + [f"e_d{EPG - 1}"]
TWO_DMAS = ("ml", "uqkv", *(f"up{i}" for i in range(11)))
assert len(LAYER_CHUNKS) % SLOTS == 0 and len(PASS_CHUNKS) % SLOTS == 0

LAYER_USES = [("q", 2), ("k", 2), ("v", 2), ("ml", 2), ("uq0", 1), ("uq1", 1), ("ukv0", 1), ("ukv1", 1),
              ("ga0", 4), ("ga1", 4), ("gb0", 4), ("gb1", 4), ("z0", 2), ("z1", 2), ("ba0", 4), ("ba1", 4),
              ("xbc0", 4), ("xbc1", 4), ("xbc2", 4), ("xbc3", 4), ("bb0", 4), ("bb1", 4), ("gc0", 4), ("gc1", 4),
              ("bc0", 4), ("bc1", 4), ("wo0", 4), ("wo1", 4), ("n2", 1)] + [(f"up{i}", 4) for i in range(11)] + [("dn0", 0), ("dn1", 0)]
assert len(LAYER_USES) % 2 == 0


class Use:

    def __init__(self, names, first=(0, 0), free=(1, 1)):
        self.buf, self.full, self.turn = {}, {}, {}
        full, turn = list(first), list(free)
        for i, (name, pieces) in enumerate(names):
            b = i % 2
            self.buf[name], self.full[name], self.turn[name] = b, full[b], turn[b]
            full[b] += pieces
            turn[b] += 1
        self.next_full, self.next_turn = full, turn
        self.per_full = [full[b] - first[b] for b in range(2)]
        self.per_turn = [turn[b] - free[b] for b in range(2)]


LU = Use(LAYER_USES)


MID_USES = [("m_qa", 2), ("m_kva", 2), ("m_qb", 2), ("m_kb", 2), ("m_vb", 2), ("m_wo0", 4), ("m_wo1", 4)]
MU = Use(MID_USES, [DEPTH * n for n in LU.per_full], [1 + DEPTH * n for n in LU.per_turn])


def ring_table(chunks, first_slot, landed):
    where, total = {}, list(landed)
    for i, name in enumerate(chunks):
        s = (first_slot + i) % SLOTS
        total[s] += 16 * (2 if name in TWO_DMAS else 1)
        where[name] = (s, total[s])
    return where, total


LAYER_RING, LAYER_LANDED = ring_table(LAYER_CHUNKS, 0, [0] * SLOTS)
MID_RING, MID_LANDED = ring_table(MID_CHUNKS, len(LAYER_CHUNKS) % SLOTS, [DEPTH * n for n in LAYER_LANDED])
PASS_RING, PASS_TOTAL = ring_table(PASS_CHUNKS, (len(LAYER_CHUNKS) + len(MID_CHUNKS)) % SLOTS, [0] * SLOTS)


def program(nc, a, consts, out):
    ctx = ExitStack()
    with ctx:
        def sb(name, shape, dt=F32):
            return ctx.enter_context(nc.sbuf_tensor(name, [P] + shape, dt))[:]

        def sem(name):
            return ctx.enter_context(nc.semaphore(name))

        def bc(ap, axis, n):
            ap = ap.unsqueeze(axis)
            shape = list(ap.shape)
            shape[axis] = n
            return ap.to_broadcast(shape)

        def shaped(ap, *shape):
            if len(shape) == 1:
                return ap
            names = "abcd"[:len(shape)]
            return ap.rearrange(f"p ({' '.join(names)}) -> p {' '.join(names)}", **dict(zip(names, shape)))

        ring = sb("ring", [SLOTS, SLOT])
        xT = sb("xT", [KT, SEQ])
        hT = sb("hT", [KT, SEQ])
        kc = sb("kc", [K_END])
        ones = sb("ones", [P])
        epsc = sb("epsc", [2])
        cact = sb("cact", [KT])
        cols = sb("cols", [DEPTH, 384])
        cols2 = sb("cols2", [W_END])
        rows = sb("rows", [DEPTH, R_END])
        biasm = sb("biasm", [DA_H, 384])
        rcos = sb("rcos", [T, 16])
        rsin = sb("rsin", [T, 16])
        cc = sb("cc", [V_END])
        rc = sb("rc", [R_END])
        lami = sb("lami", [2])
        mod = sb("mod", [48])
        amix = sb("amix", [KT])
        affn = sb("affn", [KT])
        gmh = sb("gmh", [KT])
        swh = sb("swh", [80])
        wqk = sb("wqk", [1])
        subw = sb("subw", [1])
        anega = sb("anega", [SM_H])
        lamv = sb("lamv", [8])
        lamp = sb("lamp", [128])
        rstd = sb("rstd", [SEQ])
        gates = sb("gates", [2, KT, SEQ])
        zb = sb("zb", [T, D])
        yT = sb("yT", [8, SEQ])
        ysT = sb("ysT", [8, SEQ])
        kv = shaped(ysT.rearrange("p a b -> p (a b)"), T, 1024)
        area = sb("area", [14336])

        def view(offset, *shape):
            return shaped(area[:, offset:offset + int(np.prod(shape))], *shape)

        S = view(0, 1024)
        PT = view(1024, 8, P)
        o = view(2048, T, 512)
        junk = view(3072, 1024)
        qk = view(4096, 2, T, 512)
        sqqk = view(0, 2, T, 512)
        va = view(6144, T, 512)
        qTa = view(7168, DA_H, SEQ)
        kTa = view(8192, DA_H, SEQ)
        kb = view(4096, T, ML_H, ML_QK)
        qTm = view(6144, ML_H, SEQ)
        kTm = view(8192, ML_H, SEQ)
        ml = view(10240, T, ML_W + SM_H)
        cT = view(11104, 3, SEQ)
        qb = view(11872, T, ML_H, ML_QK)
        sqq = view(0, T, ML_H, ML_QK)
        sqk = view(2048, T, ML_H, ML_N)
        xb = view(0, 16, SEQ)
        xdt = view(0, T, D)
        xs = view(4096, T, D)
        bmt = view(6144, SM_G * SM_N)
        cbm = view(6656, SM_G, P)
        tria = view(7168, 8, P)
        E = view(8192, 8, P)
        stT = view(9216, D)
        xe = view(10240, SM_H, SM_D)
        y = view(11264, T, D)
        th = view(13312, 1024)
        sqy = view(7168, T, D)
        act = view(0, FT, SEQ)
        u4 = view(5632, 2, 4, SEQ)
        sl = view(7680, 2, 512)
        sqx = view(8704, KT, SEQ)
        xin = view(0, T, D)
        prow = view(2048, DEPTH, 3, P)
        prow2 = view(2816, P)
        crow = view(2944, P)
        dist = view(3072, 384)
        step = view(3456, 384)
        ang = view(3840, T, 16)
        turns = view(3872, T, 16)
        posf = view(4096, SEQ)
        rel = view(4352, BUCKETS * DA_H)
        drel = view(4480, BUCKETS * DA_H)
        posr = sb("posr", [SEQ], I32)
        posc = sb("posc", [T], I32)
        poscf = sb("poscf", [T])
        iturn = sb("iturn", [T * 16], I32)

        qa2 = view(4096, T, 512)
        ka2 = view(5120, T, P)
        kd2 = view(5376, T, 2, 2, D2)
        va2 = view(5888, T, P)
        qb2 = view(6144, T, 512)
        kb2 = view(7168, T, 512)
        vb2 = view(8192, T, 512)
        rt1, rt2, rr1 = (view(9216 + 512 * i, T, H2, 32) for i in range(3))
        sqa2 = view(0, T, 512)
        sqk2 = view(1024, T, P)
        qTa2 = view(10752, 4, SEQ)
        kTa2 = view(11776, 2, SEQ)
        qTb2 = view(12288, 4, SEQ)
        kTb2 = view(13312, 4, SEQ)
        sqo = view(9216, T, 512)
        o2 = [view(2048 + 1024 * i, T, 512) for i in range(2)]
        S2 = [zb[:, i, :] for i in range(2)]
        PT2 = [shaped(yT[:, 4 * i:4 * i + 4, :].rearrange("p h n -> p (h n)"), 8, P) for i in range(2)]
        late = ysT.rearrange("p h n -> p (h n)")
        rwt = shaped(late[:, 0:KT * 36], KT, 36)
        qn2, kn2 = late[:, 288:352], late[:, 352:416]
        rb2 = late[:, 416:452]
        h2t = view(0, T, D)
        xg = view(2048, KT, P)
        pm = view(3072, T, P)
        pmT = view(3328, SEQ)
        hs = view(3584, 2, 512)
        he = view(4608, 2, 512)
        heT = view(5632, 2, 4, P)
        ygs = view(6656, D)
        fin = view(10752, T, D)
        r = lambda at, *shape: view(7680 + at, *shape)
        lg, og, gv, gm = r(0, T, 36), r(72, T, GROUPS), r(80, T, GROUPS), r(88, T)
        ge, gp, em, ei = r(90, T, GROUPS), r(98, T), r(100, T, GROUPS, EPG), r(164, T, EPG)
        m1, m2, o1, o2nd, ev, vm = r(180, T), r(182, T), r(184, T, EPG), r(200, T, EPG), r(216, T, EPG), r(232, T)
        w1, w2, gate8, psl = r(234, T), r(236, T), r(240, T, EPG), r(256, T, GROUPS + 1)
        over, metaf, gsl, ssq = r(266, GROUPS), r(270, 8), r(278, EPG), r(286, T)
        meta = sb("meta", [8], I32)

        nmx = sb("nmx", [8])
        psums = sb("psums", [8])
        rps = sb("rps", [8])
        nlr = sb("nlr", [4])
        ss = sb("ss", [64])
        rs = sb("rs", [64])
        rsl = sb("rsl", [T, 4])
        sso = sb("sso", [T, 4])
        ssl = sb("ssl", [T, 4])
        krr = sb("krr", [T, 32])
        tmp1 = view(13408, T, ML_H, 16)
        tmp2 = view(13664, T, ML_H, 16)
        rot1 = view(13920, T, ML_H, 16)
        dt = sb("dt", [T, SM_H])
        dtn = sb("dtn", [T, SM_H])
        da = sb("da", [T, SM_H])
        csb = sb("csb", [T, SM_H])
        ecs = sb("ecs", [T, SM_H])

        acc = [ctx.enter_context(nc.psum_tensor(f"acc{b}", [P, 1024], F32))[:] for b in range(2)]
        aux = ctx.enter_context(nc.psum_tensor("aux", [P, 1024], F32))[:]
        aux2 = ctx.enter_context(nc.psum_tensor("aux2", [P, 512], F32))[:]
        pmod = ctx.enter_context(nc.psum_tensor("pmod", [P, 512], F32))[:]
        ident = kc[:, K_ID:K_ID + P]
        tri = kc[:, K_TRI:K_TRI + P]

        landed = [sem(f"landed{s}") for s in range(SLOTS)]
        acc_full = [sem(f"acc_full{b}") for b in range(2)]
        acc_free = [sem(f"acc_free{b}") for b in range(2)]
        dn_done = sem("dn_done")
        ada_done = sem("ada_done")
        x_in, small_in = sem("x_in"), sem("small_in")
        fill = sem("fill")
        pro_t, pro_e = sem("pro_t"), sem("pro_e")
        c_ready, rope_n, rope_ang, rope_done = sem("c_ready"), sem("rope_n"), sem("rope_ang"), sem("rope_done")
        x_sq, x_ss, x_rt, h_ready = sem("x_sq"), sem("x_ss"), sem("x_rt"), sem("h_ready")
        x_new = sem("x_new")
        cur_ready, mod_ready, al_exp, lam_arg, lam_exp = (sem(n) for n in ("cur_ready", "mod_ready", "al_exp", "lam_arg", "lam_exp"))
        qk_sq, qk_ss, qk_rt, qk_n, v_in = (sem(n) for n in ("qk_sq", "qk_ss", "qk_rt", "qk_n", "v_in"))
        qkT, qkT_out = sem("qkT"), sem("qkT_out")
        ml_in, ml_rt, c_n, cT_t, cT_out = (sem(n) for n in ("ml_in", "ml_rt", "c_n", "cT_t", "cT_out"))
        dt_abs, dt_exp, dt_p1, dt_ln, dt_ready = (sem(n) for n in ("dt_abs", "dt_exp", "dt_p1", "dt_ln", "dt_ready"))
        s_full, s_max, p_exp, w_mix = (sem(n) for n in ("s_full", "s_max", "p_exp", "w_mix"))
        t_full, t_out, o_full, o_out = (sem(n) for n in ("t_full", "t_out", "o_full", "o_out"))
        oa_rt, oa_n, yaT_t, yaT_out = (sem(n) for n in ("oa_rt", "oa_n", "yaT_t", "yaT_out"))
        qb_in, m_sq, m_ss, m_rt, m_n, mT_t, mT_out = (sem(n) for n in ("qb_in", "m_sq", "m_ss", "m_rt", "m_n", "mT_t", "mT_out"))
        ybT_t, ybT_out = sem("ybT_t"), sem("ybT_out")
        z_tanh, tap0, conv, c_tanh, xb_ready = (sem(n) for n in ("z_tanh", "tap0", "conv", "c_tanh", "xb_ready"))
        xsT_t, xs_out, xdt_ready, cs_full, cs_out, ecs_out = (sem(n) for n in ("xsT_t", "xs_out", "xdt_ready", "cs_full", "cs_out", "ecs_out"))
        bm_t, bm_out, cb_full, cb_out = (sem(n) for n in ("bm_t", "bm_out", "cb_full", "cb_out"))
        tria_ready, r_full, seg_ready, seg_exp, m_ready, y_full, y_out = (
            sem(n) for n in ("tria_ready", "r_full", "seg_ready", "seg_exp", "m_ready", "y_full", "y_out"))
        st_full, st_out, yo_full, yo_out = (sem(n) for n in ("st_full", "st_out", "yo_full", "yo_out"))
        y_gated, y_sq, y_ss, y_rt, y_n, ysT_t, ysT_out = (
            sem(n) for n in ("y_gated", "y_sq", "y_ss", "y_rt", "y_n", "ysT_t", "ysT_out"))
        g_tanh, merged_b, merged = sem("g_tanh"), sem("merged_b"), sem("merged")
        u_tap, u_conv, u_silu, act_ready = (sem(n) for n in ("u_tap", "u_conv", "u_silu", "act_ready"))

        late_in, a2_n, b2_n, t2, t2_out = (sem(n) for n in ("late_in", "a2_n", "b2_n", "t2", "t2_out"))
        a2_ss, a2_rt = sem("a2_ss"), sem("a2_rt")
        s2_full, s2_max, p2_exp, t3_full, t3_out, o2_full, o2_out = (
            sem(n) for n in ("s2_full", "s2_max", "p2_exp", "t3_full", "t3_out", "o2_full", "o2_out"))
        on_ss, on_n, oT_t, oT_out = (sem(n) for n in ("on_ss", "on_n", "oT_t", "oT_out"))
        h2_t, h2_out, lg_full, lg_sub, lg_exp, top_sub, top_exp = (
            sem(n) for n in ("h2_t", "h2_out", "lg_full", "lg_sub", "lg_exp", "top_sub", "top_exp"))
        og_ready, pos_full, routed = sem("og_ready"), sem("pos_full"), sem("routed")
        pm_ready, gx_full, gx_out, pt_full, pt_out = (sem(n) for n in ("pm_ready", "gx_full", "gx_out", "pt_full", "pt_out"))
        g_full, u_full, d_done, g_silu, he_ready, he_t, he_out = (
            sem(n) for n in ("g_full", "u_full", "d_done", "g_silu", "he_ready", "he_t", "he_out"))
        yg_out, sc_full, x_added = sem("yg_out"), sem("sc_full"), sem("x_added")
        f_t, f_out, stored = sem("f_t"), sem("f_out"), sem("stored")
        def by_row(name, dst):
            return dst, a[name].rearrange("l (k n) -> k l n", n=P)

        def spread(name, c0, c1):
            w = a[name]
            if len(w.shape) == 3:
                w = w.rearrange("l a b -> l (a b)")
            return rows[:, :, c0:c1], w.unsqueeze(0).to_broadcast([P, DEPTH, c1 - c0])

        fw = a["ffn_conv_w"].rearrange("l k (f n) -> (k f) l n", n=P)
        small_dmas = [
            (rel, a["rel_bias"].rearrange("b h -> (b h)").unsqueeze(0).to_broadcast([P, BUCKETS * DA_H])),
            (posr, a["positions"].to_broadcast([P, SEQ])),
            *[(posc[:, t:t + 1], a["positions"][:, P * t:P * t + P].rearrange("b p -> p b")) for t in range(T)],
            (prow[:, :, 0, :], fw[0:P]),
            (prow[0:4, :, 1, :], fw[P:P + 4]),
            by_row("ffn_conv_b", prow[V_FB - P:V_ADA - P, :, 1, :]),
            by_row("ada_b", prow[V_ADA - P:V_NM - P, :, 1, :]),
            by_row("norm_mix", prow[V_NM - P:V_NF - P, :, 1, :]),
            by_row("norm_ffn", prow[V_NF - P:V_SN - P, :, 1, :]),
            by_row("ssm_norm", prow[V_SN - P:V_QA - P, :, 1, :]),
            by_row("mla_q_a_norm", prow[V_QA - P:V_KVA - P, :, 1, :]),
            by_row("mla_kv_a_norm", prow[V_KVA - P:V_SUB - P, :, 1, :]),
            by_row("da_subln", prow[V_SUB - P:V_SUB + 1 - P, :, 1, :]),
            (prow[0:64, :, 2, :], a["ssm_conv_w"].rearrange("l k (f n) -> (k f) l n", n=P)),
            by_row("ssm_conv_b", prow[64:80, :, 2, :]),
            *[(prow[80 + i:81 + i, :, 2, DA_D * m:DA_D * m + DA_D], a[name].unsqueeze(0))
              for i, name in enumerate(("da_q_norm", "da_k_norm")) for m in range(2)],
            *[(prow2[w0:w1, :], (a[name] if len(a[name].shape) == 2 else a[name].unsqueeze(0)).rearrange("l (k n) -> (l k) n", n=P))
              for name, w0, w1 in (("norm1_g_2", W_N1, W_OA), ("out_norm_a_g_2", W_OA, W_OB), ("out_norm_b_g_2", W_OB, W_N2),
                                   ("norm2_g_2", W_N2, W_FN), ("final_norm_g_2", W_FN, W_END))],
            spread("mla_q_norm", R_MQ, R_MK),
            spread("mla_k_norm", R_MK, R_DTB),
            spread("ssm_dt_bias", R_DTB, R_AL),
            spread("ssm_a_log", R_AL, R_SD),
            spread("ssm_d", R_SD, R_LP),
            spread("da_lambda", R_LP, R_END),
        ]
        N_SMALL = len(small_dmas)
        shaped_kv = lambda ap: ap.rearrange("p t (h n) -> p t h n", h=ML_H)
        block = ctx.enter_context(nc.Block())

        def release_of(name):
            if name.startswith("dn"):
                return dn_done, 6 + int(name[2:]) + 1, 6
            if name.startswith("ada"):
                return ada_done, int(name[3:]) + 1, 12
            use = {"uqkv": "ukv1", "ba": "ba1", "bb": "bb1"}.get(name, name)
            b = LU.buf[use]
            return acc_full[b], LU.full[use] + dict(LAYER_USES)[use], LU.per_full[b]

        def layer_source(name, l):
            def rows_of(w, c0, c1, r0=0, r1=D):
                n = (r1 - r0) // P
                return w[bass.ds(l, 1), r0:r1, c0:c1].rearrange("l (k p) n -> p (l k) n", p=P), n * (c1 - c0), n
            w_in = a["w_in"]
            if name.startswith("ada"):
                i = int(name[3:])
                return [rows_of(a["ada_w"], 512 * i, 512 * i + 512)]
            if name in ("q", "k", "v"):
                c = {"q": C_Q, "k": C_K, "v": C_V}[name]
                return [rows_of(w_in, c, c + 512)]
            if name == "uqkv":
                return [rows_of(a["mla_w_uq"], 0, ML_H * ML_QK, 0, Q_RANK), rows_of(a["mla_w_ukv"], 0, 1024, 0, KV_RANK)]
            if name[:2] in ("ga", "gb", "gc"):
                c = C_G + D * "abc".index(name[1]) + 512 * int(name[2])
                return [rows_of(w_in, c, c + 512)]
            if name[0] == "z":
                return [rows_of(w_in, C_Z + 512 * int(name[1]), C_Z + 512 * int(name[1]) + 512)]
            if name.startswith("xbc"):
                return [rows_of(w_in, C_XBC + 512 * int(name[3]), C_XBC + 512 * int(name[3]) + 512)]
            if name == "ba":
                return [rows_of(a["w_branch_a"], 0, D, 0, 512)]
            if name == "bb":
                return [rows_of(a["w_branch_b"], 0, D, 0, 512)]
            if name[:2] in ("bc", "wo"):
                w, i = a["w_branch_c" if name[0] == "b" else "w_out"], int(name[2])
                return [rows_of(w, 512 * i, 512 * i + 512)]
            if name[:2] == "dn":
                i = int(name[2:])
                return [rows_of(a["ffn_w_down"], 0, D, 512 * i, min(512 * i + 512, FFN))]
            raise ValueError(name)

        @block.sync
        def _(sp):
            with sp.Fori(0, DEPTH) as l:
                for i, name in enumerate(LAYER_CHUNKS):
                    s = i % SLOTS
                    if i >= SLOTS:
                        signal, value, per = release_of(LAYER_CHUNKS[i - SLOTS])
                        sp.wait_ge(signal, l * per + value)
                    else:
                        sp.wait_ge(dn_done, l * 6 + 6 - SLOTS + i + 1)
                    if name == "ml":
                        dst = shaped(ring[:, s, 0:8 * (ML_W + SM_H)], 8, ML_W + SM_H)
                        w = a["w_in"][bass.ds(l, 1)].rearrange("l (k p) n -> p (l k) n", p=P)
                        sp.dma_start(dst[:, :, 0:ML_W], w[:, :, C_ML:C_ML + ML_W]).then_inc(landed[s], 16)
                        sp.dma_start(dst[:, :, ML_W:], w[:, :, C_DT:C_DT + SM_H]).then_inc(landed[s], 16)
                    elif name.startswith("up"):
                        n = int(name[2:])
                        w = a["ffn_w_up"][bass.ds(l, 1)].rearrange("l (k p) (h n) -> p (l k) h n", p=P, h=2)
                        dst = shaped(ring[:, s, :], KT, 2, 256)
                        sp.dma_start(dst[:, :, 0, :], w[:, :, 0, 256 * n:256 * n + 256]).then_inc(landed[s], 16)
                        sp.dma_start(dst[:, :, 1, :], w[:, :, 1, 256 * n:256 * n + 256]).then_inc(landed[s], 16)
                    else:
                        at = 0
                        for src, size, k in layer_source(name, l):
                            sp.dma_start(shaped(ring[:, s, at:at + size], k, size // k), src).then_inc(landed[s], 16)
                            at += size

            for i, name in enumerate(MID_CHUNKS):
                s = MID_RING[name][0]
                if i < SLOTS:
                    sp.wait_ge(dn_done, 6 + 6 * (DEPTH - 1) + 6 - SLOTS + i + 1)
                else:
                    prev = MID_CHUNKS[i - SLOTS]
                    sp.wait_ge(acc_full[MU.buf[prev]], MU.full[prev] + 2)
                w, c0, c1 = {"m_qa": ("w_in_2", 0, 512), "m_kva": ("w_in_2", 512, 768), "m_qb": ("w_in_2", 768, 1280),
                             "m_kb": ("w_in_2", 1280, 1792), "m_vb": ("w_in_2", 1792, 2304),
                             "m_wo0": ("w_out_2", 0, 512), "m_wo1": ("w_out_2", 512, 1024)}[name]
                sp.dma_start(shaped(ring[:, s, 0:KT * (c1 - c0)], KT, c1 - c0),
                             a[w].rearrange("l (k p) n -> p (l k) n", p=P)[:, :, c0:c1]).then_inc(landed[s], 16)
            sp.wait_ge(routed, 1)
            passes = sp.value_load(meta[0:1, 5:6], min_val=GROUPS, max_val=GROUPS + 1)
            with sp.Fori(0, passes) as p:
                group = sp.value_load(meta[0:1, bass.ds(p, 1)], min_val=0, max_val=GROUPS - 1)
                for i, name in enumerate(PASS_CHUNKS):
                    s = PASS_RING[name][0]
                    kind, e = PASS_CHUNKS[i - SLOTS][2], int(PASS_CHUNKS[i - SLOTS][3:])
                    sp.wait_ge({"g": g_full, "u": u_full, "d": d_done}[kind], p * EPG + (EPG if i >= SLOTS else 0) + e + 1)
                    w = a[{"g": "w_gate_2", "u": "w_up_2", "d": "w_down_2"}[name[2]]]
                    src = w[0, bass.ds(group * EPG + int(name[3:]), 1)]
                    n = DE if name[2] != "d" else D
                    sp.dma_start(shaped(ring[:, s, :], SLOT // n, n),
                                 src.rearrange("e (k p) n -> p (e k) n", p=P)).then_inc(landed[s], 16)

        @block.tensor
        def _(pe):
            def transposes(ins_outs, signal):
                for src, dst in ins_outs:
                    n = src.shape[0]
                    last = pe.transpose(dst, src, ident[0:n, 0:n])
                last.then_inc(signal, 1)

            pe.wait_ge(x_in, 16 * 3)
            for t in range(T):
                if t:
                    pe.wait_ge(pro_e, t)
                transposes([(xin[:, t, P * k:P * k + P], aux[:, P * k:P * k + P]) for k in range(KT)], pro_t)
            transposes([(crow[0:KT, :], aux2[:, 0:KT])], pro_t)
            pe.wait_ge(small_in, 16 * N_SMALL)
            for l in range(DEPTH):
                for i, n in enumerate((P, V_SUB + 1 - P, V_END - 2 * P)):
                    transposes([(prow[0:n, l, i, :], acc[0][:, 384 * l + P * i:384 * l + P * i + n])], pro_t)
            transposes([(prow2[0:W_END, :], acc[1][:, 0:W_END])], pro_t)
            pe.drain().then_inc(dn_done, 6)
            pe.wait_ge(c_ready, 1)
            pe.wait_ge(fill, 1)

            with pe.Fori(0, DEPTH) as l:
                def arrived(name):
                    s, value = LAYER_RING[name]
                    pe.wait_ge(landed[s], l * LAYER_LANDED[s] + value)
                    return ring[:, s, :]

                def open_acc(use):
                    b = LU.buf[use]
                    pe.wait_ge(acc_free[b], l * LU.per_turn[b] + LU.turn[use])

                def feature_piece(use, j, w, c0, x):
                    n = w.shape[1]
                    for k in range(n):
                        mm = pe.matmul(acc[LU.buf[use]][:, SEQ * j:SEQ * j + SEQ], w[:, k, c0:c0 + P], x[:, k, :],
                                       start=(k == 0), stop=(k == n - 1))
                    mm.then_inc(acc_full[LU.buf[use]], 1)

                def token_piece(use, t, at, w, x, signal=True):
                    n, width = w.shape[1], w.shape[2]
                    for k in range(n):
                        mm = pe.matmul(acc[LU.buf[use]][:, at:at + width], x[:, k, P * t:P * t + P], w[:, k, :],
                                       start=(k == 0), stop=(k == n - 1))
                    if signal:
                        mm.then_inc(acc_full[LU.buf[use]], 1)

                def ada(i):
                    w = shaped(arrived(f"ada{i}"), KT, 512)
                    for j in range(4):
                        for k in range(KT):
                            mm = pe.matmul(pmod[:, 4 * i + j:4 * i + j + 1], w[:, k, P * j:P * j + P], cact[:, k:k + 1],
                                           start=(k == 0), stop=(k == KT - 1))
                    mm.then_inc(ada_done, 1)

                def norm_sum(dst, signal):
                    for k in range(KT):
                        mm = pe.matmul(dst, ones, sqx[:, k, :], start=(k == 0), stop=(k == KT - 1))
                    mm.then_inc(signal, 1)

                def token_chunk(name, width=512):
                    w = shaped(arrived(name)[:, 0:KT * width], KT, width)
                    open_acc(name)
                    for t in range(T):
                        token_piece(name, t, 512 * t, w, hT)

                def gate_pieces(name, first, last):
                    w = shaped(arrived(name), KT, 512)
                    if first == 0:
                        open_acc(name)
                    for j in range(first, last):
                        feature_piece(name, j, w, P * j, hT)

                ada(0)
                ada(1)
                pe.wait_ge(x_sq, 2 * l + 1)
                norm_sum(aux2[:, 0:SEQ], x_ss)
                ada(2)
                ada(3)
                pe.wait_ge(h_ready, 2 * l + 1)
                for name in ("q", "k", "v"):
                    token_chunk(name)
                token_chunk("ml", ML_W + SM_H)

                pe.wait_ge(qk_n, l + 1)
                for i in range(2):
                    if i:
                        pe.wait_ge(qkT_out, 2 * l + 1)
                    transposes([(qk[:, i, t, P * h:P * h + P], aux[:, SEQ * h + P * t:SEQ * h + P * t + P])
                                for h in range(DA_H) for t in range(T)], qkT)
                pe.wait_ge(c_n, l + 1)
                pe.wait_ge(qkT_out, 2 * l + 2)
                transposes([(ml[:, t, P * j:P * j + P], aux[:, SEQ * j + P * t:SEQ * j + P * t + P])
                            for j in range(3) for t in range(T)], cT_t)
                pe.wait_ge(cT_out, l + 1)
                w = arrived("uqkv")
                wq, wkv = shaped(w[:, 0:1536], 2, 768), shaped(w[:, 1536:2560], 1, 1024)
                for t in range(T):
                    open_acc(f"uq{t}")
                    token_piece(f"uq{t}", t, 0, wq[:, :, 0:512], cT, signal=False)
                    token_piece(f"uq{t}", t, 512, wq[:, :, 512:768], cT)
                for t in range(T):
                    open_acc(f"ukv{t}")
                    token_piece(f"ukv{t}", t, 0, wkv[:, :, 0:512], cT[:, 2:3, :], signal=False)
                    token_piece(f"ukv{t}", t, 512, wkv[:, :, 512:1024], cT[:, 2:3, :])
                pe.wait_ge(dt_ready, l + 1)
                for t in range(T):
                    mm = pe.matmul(pmod[:, 48 + SM_H * t:48 + SM_H * (t + 1)], tri, da[:, t, :], start=True, stop=True)
                mm.then_inc(cs_full, 1)

                def da_unit(n):
                    return [(0, 0, 4, 1), (1, 0, 2, 2), (1, 2, 2, 2)][n]

                def ml_unit(n):
                    return [(0, 0, 8, 1), (1, 0, 4, 2), (1, 4, 4, 2)][n]

                def da_scores(n):
                    t, h0, nh, nk = da_unit(n)
                    for i in range(nh):
                        for m in range(2):
                            mm = pe.matmul(aux[:, 512 * m + P * nk * i:512 * m + P * nk * (i + 1)],
                                           qTa[64 * m:64 * m + 64, h0 + i, P * t:P * t + P],
                                           kTa[64 * m:64 * m + 64, h0 + i, 0:P * nk], start=True, stop=True)
                    mm.then_inc(s_full, 1)

                def ml_scores(n):
                    t, h0, nh, nk = ml_unit(n)
                    for i in range(nh):
                        mm = pe.matmul(aux[:, P * nk * i:P * nk * (i + 1)], qTm[0:ML_QK, h0 + i, P * t:P * t + P],
                                       kTm[0:ML_QK, h0 + i, 0:P * nk], start=True, stop=True)
                    mm.then_inc(s_full, 1)

                def prob_transposes(count):
                    transposes([(S[:, P * i:P * i + P], aux[:, P * i:P * i + P]) for i in range(count)], t_full)

                def values(n, unit, width, v):
                    t, h0, nh, nk = unit
                    pe.wait_ge(t_out, l * 6 + n + 1)
                    if n:
                        pe.wait_ge(o_out, l * 6 + n)
                    for i in range(nh):
                        for k in range(nk):
                            mm = pe.matmul(aux2[:, width * i:width * i + width], PT[:, i * nk + k, :], v(h0 + i, k),
                                           start=(k == 0), stop=(k == nk - 1))
                    mm.then_inc(o_full, 1)

                for n, filler in enumerate(("ga0", "ga1", "gb0")):
                    da_scores(n)
                    gate_pieces(filler, 0, 3)
                    pe.wait_ge(w_mix, l * 3 + n + 1)
                    prob_transposes(4)
                    gate_pieces(filler, 3, 4)
                    values(n, da_unit(n), 2 * DA_D, lambda h, k: va[:, k, 2 * DA_D * h:2 * DA_D * (h + 1)])
                gate_pieces("gb1", 0, 4)
                pe.wait_ge(oa_n, l + 1)
                transposes([(o[:, t, P * j:P * j + P], aux[:, SEQ * j + P * t:SEQ * j + P * t + P])
                            for j in range(4) for t in range(T)], yaT_t)
                pe.wait_ge(yaT_out, l + 1)

                pe.wait_ge(m_n, l + 1)
                for i in range(4):
                    if i:
                        pe.wait_ge(mT_out, 4 * l + i)
                    src, t = (qb, kb)[i // 2], i % 2
                    transposes([(src[:, t, h, :], aux[0:ML_QK, P * h:P * h + P]) for h in range(ML_H)], mT_t)
                pe.wait_ge(mT_out, 4 * l + 4)
                v_of = lambda h, k: kv[:, k, P * h + ML_N:P * h + P]
                for n in range(3):
                    ml_scores(n)
                    if n < 2:
                        token_chunk(f"z{n}")
                    else:
                        w = shaped(arrived("ba"), 4, D)
                        for u in range(2):
                            open_acc(f"ba{u}")
                            for j in range(4):
                                feature_piece(f"ba{u}", j, w, 512 * u + P * j, yT[:, 0:4, :])
                    pe.wait_ge(p_exp, l * 6 + 3 + n + 1)
                    prob_transposes(8)
                    values(3 + n, ml_unit(n), ML_V, v_of)

                gate_pieces("xbc0", 0, 4)
                pe.wait_ge(o_out, l * 6 + 6)
                transposes([(o[:, t, P * j:P * j + P], aux[:, SEQ * j + P * t:SEQ * j + P * t + P])
                            for j in range(4) for t in range(T)], ybT_t)
                gate_pieces("xbc1", 0, 4)
                gate_pieces("xbc2", 0, 4)
                pe.wait_ge(xb_ready, 4 * l + 2)
                pe.wait_ge(ybT_out, l + 1)

                def xs_transposes(t):
                    transposes([(xb[:, k, P * t:P * t + P], aux[:, P * k:P * k + P]) for k in range(KT)], xsT_t)

                xs_transposes(0)
                gate_pieces("xbc3", 0, 4)
                pe.wait_ge(xs_out, 2 * l + 1)
                xs_transposes(1)
                pe.wait_ge(xb_ready, 4 * l + 3)
                transposes([(xb[:, 8 + g, 0:P], aux2[:, P * g:P * g + P]) for g in range(SM_G)], bm_t)
                w = shaped(arrived("bb"), 4, D)
                open_acc("bb0")
                for j in range(4):
                    feature_piece("bb0", j, w, P * j, yT[:, 4:8, :])

                def cb(t):
                    for g in range(SM_G):
                        mm = pe.matmul(aux2[:, P * g:P * g + P], xb[:, 8 + g, P * t:P * t + P],
                                       xb[:, 12 + g, P * t:P * t + P], start=True, stop=True)
                    mm.then_inc(cb_full, 1)

                def decays(hc):
                    pe.wait_ge(tria_ready, 4 * l + hc + 1)
                    for i in range(2):
                        mm = pe.matmul(aux[:, 512 * i:512 * i + 512], ones,
                                       tria[:, 4 * i:4 * i + 4, :].rearrange("p h n -> p (h n)"), start=True, stop=True)
                    mm.then_inc(r_full, 1)

                def diagonal(hc):
                    t, h0 = hc // 2, 8 * (hc % 2)
                    pe.wait_ge(m_ready, 4 * l + hc + 1)
                    if hc == 0 or hc == 2:
                        pe.wait_ge(cb_out, 2 * l + t + 1)
                    else:
                        pe.wait_ge(y_out, 4 * l + hc)
                    for h in range(8):
                        mm = pe.matmul(aux2[:, SM_D * h:SM_D * h + SM_D], E[:, h, :],
                                       xdt[:, t, SM_D * (h0 + h):SM_D * (h0 + h + 1)], start=True, stop=True)
                    mm.then_inc(y_full, 1)

                pe.wait_ge(xb_ready, 4 * l + 4)
                pe.wait_ge(bm_out, l + 1)
                cb(0)
                pe.wait_ge(xs_out, 2 * l + 2)
                decays(0)
                open_acc("bb1")
                for j in range(4):
                    feature_piece("bb1", j, w, 512 + P * j, yT[:, 4:8, :])
                diagonal(0)
                decays(1)
                gate_pieces("gc0", 0, 2)
                diagonal(1)
                for g in range(SM_G):
                    mm = pe.matmul(aux[:, SEQ * g:SEQ * g + SEQ], bmt[:, P * g:P * g + P],
                                   xe[:, 4 * g:4 * g + 4, :].rearrange("p h d -> p (h d)"), start=True, stop=True)
                mm.then_inc(st_full, 1)
                pe.wait_ge(y_out, 4 * l + 2)
                cb(1)
                gate_pieces("gc0", 2, 4)
                pe.wait_ge(st_out, l + 1)
                decays(2)
                gate_pieces("gc1", 0, 2)
                diagonal(2)
                decays(3)
                gate_pieces("gc1", 2, 4)
                diagonal(3)
                for g in range(SM_G):
                    mm = pe.matmul(aux[:, SEQ * g:SEQ * g + SEQ], xb[:, 12 + g, P:2 * P], stT[:, SEQ * g:SEQ * g + SEQ],
                                   start=True, stop=True)
                mm.then_inc(yo_full, 1)
                ada(4)
                ada(5)
                pe.wait_ge(y_n, l + 1)
                for t in range(T):
                    if t:
                        pe.wait_ge(ysT_out, 2 * l + t)
                    transposes([(y[:, t, P * k:P * k + P], aux[:, P * k:P * k + P]) for k in range(KT)], ysT_t)
                pe.wait_ge(ysT_out, 2 * l + 2)
                for i in range(2):
                    w = shaped(arrived(f"bc{i}"), KT, 512)
                    open_acc(f"bc{i}")
                    for j in range(4):
                        feature_piece(f"bc{i}", j, w, P * j, ysT)
                pe.wait_ge(merged, l + 1)
                for i in range(2):
                    w = shaped(arrived(f"wo{i}"), KT, 512)
                    open_acc(f"wo{i}")
                    for j in range(4):
                        feature_piece(f"wo{i}", j, w, P * j, gates[:, 0])

                ada(6)
                ada(7)
                ada(8)
                open_acc("n2")
                pe.wait_ge(x_sq, 2 * l + 2)
                norm_sum(acc[LU.buf["n2"]][:, 0:SEQ], acc_full[LU.buf["n2"]])
                for i in range(9, 12):
                    ada(i)
                pe.wait_ge(h_ready, 2 * l + 2)
                for i in range(11):
                    gate_pieces(f"up{i}", 0, 4)
                open_acc("dn0")
                open_acc("dn1")
                pe.wait_ge(act_ready, 11 * l + 10)
                for i in range(6):
                    k0, k1 = 4 * i, min(4 * i + 4, FT)
                    w = shaped(arrived(f"dn{i}")[:, 0:D * (k1 - k0)], k1 - k0, D)
                    if i == 5:
                        pe.wait_ge(act_ready, 11 * l + 11)
                    for k in range(k0, k1):
                        for f in range(KT):
                            dst = acc[LU.buf[f"dn{f // 4}"]][:, SEQ * (f % 4):SEQ * (f % 4) + SEQ]
                            mm = pe.matmul(dst, w[:, k - k0, P * f:P * f + P], act[:, k, :],
                                           start=(k == 0 and f % 2 == 0), stop=(k == FT - 1), skip_group_check=True)
                    mm.then_inc(dn_done, 1)

            def mid_arrived(name):
                s, value = MID_RING[name]
                pe.wait_ge(landed[s], value)
                return ring[:, s, :]

            def mid_token_chunk(name, width):
                w = shaped(mid_arrived(name)[:, 0:KT * width], KT, width)
                b = MU.buf[name]
                pe.wait_ge(acc_free[b], MU.turn[name])
                for t in range(T):
                    for k in range(KT):
                        mm = pe.matmul(acc[b][:, 512 * t:512 * t + width], hT[:, k, P * t:P * t + P], w[:, k, :],
                                       start=(k == 0), stop=(k == KT - 1))
                    mm.then_inc(acc_full[b], 1)

            def sum_squares(n):
                pe.wait_ge(x_sq, 2 * DEPTH + n)
                for k in range(KT):
                    mm = pe.matmul(aux2[:, 0:SEQ], ones, sqx[:, k, :], start=(k == 0), stop=(k == KT - 1))
                mm.then_inc(x_ss, 1)
                pe.wait_ge(h_ready, 2 * DEPTH + n)

            sum_squares(1)
            mid_token_chunk("m_qa", 512)
            mid_token_chunk("m_kva", 256)
            mid_token_chunk("m_qb", 512)
            mid_token_chunk("m_kb", 512)
            pe.wait_ge(a2_n, 1)
            transposes([(qa2[:, t, P * j:P * j + P], aux[:, SEQ * j + P * t:SEQ * j + P * t + P])
                        for j in range(4) for t in range(T)], t2)
            mid_token_chunk("m_vb", 512)
            pe.drain().then_inc(g_full, EPG)
            pe.drain().then_inc(u_full, EPG)
            pe.wait_ge(t2_out, 1)
            transposes([(kd2[:, t, g].rearrange("p a d -> p (a d)"), aux[:, SEQ * g + P * t:SEQ * g + P * t + P])
                        for g in range(2) for t in range(T)], t2)
            for i, src in enumerate((qb2, kb2)):
                pe.wait_ge(t2_out, 2 + i)
                pe.wait_ge(b2_n, 1)
                transposes([(src[:, t, P * j:P * j + P], aux[:, SEQ * j + P * t:SEQ * j + P * t + P])
                            for j in range(4) for t in range(T)], t2)
            pe.wait_ge(t2_out, 4)
            for b in range(2):
                pe.wait_ge(acc_free[b], MU.turn[("m_vb", "m_kb")[b]] + 1)

            def scores(u):
                t, first = u // 2 % 2, 2 * (u % 2)
                for i in range(2):
                    for m in range(2):
                        q, k = (qTa2, kTa2[64 * m:64 * m + 64, u % 2, :]) if u < 4 else (qTb2, kTb2[64 * m:64 * m + 64, first + i, :])
                        mm = pe.matmul(acc[u % 2][:, 512 * m + SEQ * i:512 * m + SEQ * i + SEQ],
                                       q[64 * m:64 * m + 64, first + i, P * t:P * t + P], k, start=True, stop=True)
                mm.then_inc(s2_full, 1)

            scores(0)
            for u in range(8):
                if u < 7:
                    if u >= 1:
                        pe.wait_ge(p2_exp, u)
                    scores(u + 1)
                pe.wait_ge(p2_exp, u + 1)
                if u:
                    pe.wait_ge(t3_out, u)
                transposes([(S2[u % 2][:, P * i:P * i + P], aux[:, P * i:P * i + P]) for i in range(8)], t3_full)
                pe.wait_ge(t3_out, u + 1)
                if u:
                    pe.wait_ge(o2_out, u)
                for i in range(2):
                    for m in range(2):
                        head = 4 * (u % 2) + 2 * i + m
                        for k in range(T):
                            v = va2[:, k, D2 * (head // 4):D2 * (head // 4 + 1)] if u < 4 else vb2[:, k, D2 * head:D2 * head + D2]
                            mm = pe.matmul(aux2[:, D2 * (2 * i + m):D2 * (2 * i + m + 1)], PT2[u % 2][:, 2 * (2 * m + i) + k, :], v,
                                           start=(k == 0), stop=(k == T - 1))
                mm.then_inc(o2_full, 1)
                if u == 4 or u == 7:
                    n = (u - 4) // 3
                    pe.wait_ge(on_n, n + 1)
                    transposes([(o2[n][:, t, P * j:P * j + P], aux[:, SEQ * j + P * t:SEQ * j + P * t + P])
                                for j in range(4) for t in range(T)], oT_t)
                    pe.wait_ge(oT_out, n + 1)
            for i in range(2):
                name = f"m_wo{i}"
                w, b = shaped(mid_arrived(name), KT, 512), MU.buf[name]
                for j in range(4):
                    for k in range(KT):
                        mm = pe.matmul(acc[b][:, SEQ * j:SEQ * j + SEQ], w[:, k, P * j:P * j + P], hT[:, k, :],
                                       start=(k == 0), stop=(k == KT - 1))
                    mm.then_inc(acc_full[b], 1)
            pe.drain().then_inc(d_done, EPG)

            sum_squares(2)
            pe.wait_ge(late_in, 16 * 6)
            for t in range(T):
                for k in range(KT):
                    mm = pe.matmul(pmod[:, 128 + 36 * t:128 + 36 * (t + 1)], hT[:, k, P * t:P * t + P], rwt[:, k, :],
                                   start=(k == 0), stop=(k == KT - 1))
            mm.then_inc(lg_full, 1)
            for t in range(T):
                if t:
                    pe.wait_ge(h2_out, t)
                transposes([(hT[:, k, P * t:P * t + P], aux[:, P * k:P * k + P]) for k in range(KT)], h2_t)
            pe.wait_ge(og_ready, 1)
            pe.matmul(pmod[:, 256:260], tri, og[:, 0, :], start=True, stop=True)
            pe.matmul(pmod[:, 260:264], tri, og[:, 1, :], start=True, stop=False)
            pe.matmul(pmod[:, 260:264], ones, og[:, 0, :], start=False, stop=True)
            pe.matmul(pmod[:, 264:268], ones, og[:, 0, :], start=True, stop=False)
            pe.matmul(pmod[:, 264:268], ones, og[:, 1, :], start=False, stop=True).then_inc(pos_full, 1)
            pe.wait_ge(h2_out, T)
            pe.wait_ge(routed, 1)
            passes = pe.value_load(meta[0:1, 5:6], min_val=GROUPS, max_val=GROUPS + 1)
            with pe.Fori(0, passes) as p:
                def pass_arrived(name):
                    s, value = PASS_RING[name]
                    pe.wait_ge(landed[s], p * PASS_TOTAL[s] + value + MID_LANDED[s])
                    return ring[:, s, :]

                pe.wait_ge(pm_ready, p + 1)
                pe.wait_ge(x_added, p + 1)
                for k in range(KT):
                    for t in range(T):
                        mm = pe.matmul(acc[0][:, P * k:P * k + P], h2t[:, t, P * k:P * k + P], pm[:, t, :],
                                       start=(t == 0), stop=(t == T - 1))
                mm.then_inc(gx_full, 1)
                for t in range(T):
                    pe.transpose(aux2[:, P * t:P * t + P], pm[:, t, :], ident)
                for t in range(T):
                    mm = pe.matmul(pmod[:, 300:300 + EPG], pm[:, t, :], gate8[:, t, :], start=(t == 0), stop=(t == T - 1))
                mm.then_inc(pt_full, 1)
                pe.wait_ge(gx_out, p + 1)

                def gate_up(e):
                    if e >= 2:
                        pe.wait_ge(he_ready, p * EPG + e - 1)
                    for i, (kind, signal) in enumerate((("g", g_full), ("u", u_full))):
                        w = shaped(pass_arrived(f"e_{kind}{e}"), KT, DE)
                        for k in range(KT):
                            mm = pe.matmul(acc[e % 2][:, DE * i:DE * i + DE], xg[:, k, :], w[:, k, :],
                                           start=(k == 0), stop=(k == KT - 1))
                        mm.then_inc(signal, 1)

                def down(e):
                    pe.wait_ge(he_ready, p * EPG + e + 1)
                    if e:
                        pe.wait_ge(he_out, p * EPG + e)
                    else:
                        pe.wait_ge(pt_out, p + 1)
                    transposes([(he[:, e % 2, P * j:P * j + P], aux2[:, P * j:P * j + P]) for j in range(4)], he_t)
                    pe.wait_ge(he_out, p * EPG + e + 1)
                    w = shaped(pass_arrived(f"e_d{e}"), 4, D)
                    for n in range(2):
                        for k in range(4):
                            mm = pe.matmul(aux[:, 512 * n:512 * n + 512], heT[:, e % 2, k, :], w[:, k, 512 * n:512 * n + 512],
                                           start=(e == 0 and k == 0), stop=(e == EPG - 1 and k == 3))
                    mm.then_inc(d_done, 1)

                gate_up(0)
                for e in range(1, EPG):
                    gate_up(e)
                    down(e - 1)
                down(EPG - 1)
                pe.wait_ge(yg_out, p + 1)
                for k in range(KT):
                    mm = pe.matmul(acc[k // 4][:, SEQ * (k % 4):SEQ * (k % 4) + SEQ], ygs[:, P * k:P * k + P], pmT,
                                   start=True, stop=True)
                mm.then_inc(sc_full, 1)
            sum_squares(3)
            for t in range(T):
                if t:
                    pe.wait_ge(f_out, t)
                transposes([(hT[:, k, P * t:P * t + P], aux[:, P * k:P * k + P]) for k in range(KT)], f_t)

        @block.scalar
        def _(act_):
            act = act_
            copy = lambda dst, src: act.activation(dst, src, ACT.Copy)

            act.dma_start(xin, a["x"].rearrange("b (t p) n -> p (b t) n", p=P)).then_inc(x_in, 16)
            act.dma_start(kc, consts).then_inc(x_in, 16)
            act.dma_start(crow[0:KT, :], a["c"].rearrange("b (k n) -> (b k) n", k=KT)).then_inc(x_in, 16)
            for dst, src in small_dmas:
                act.dma_start(dst, src).then_inc(small_in, 16)

            for t in range(T):
                act.wait_ge(pro_t, t + 1)
                copy(xT[:, :, P * t:P * t + P], shaped(aux, KT, P)).then_inc(pro_e, 1)
            act.drain().then_inc(x_new, 1)
            act.wait_ge(fill, 1)
            act.wait_ge(pro_t, 3)
            act.activation(cact, aux2[:, 0:KT], ACT.Silu).then_inc(c_ready, 1)
            act.wait_ge(pro_t, 3 + 3 * DEPTH)
            for l in range(DEPTH):
                copy(cols[:, l, 0:V_SUB + 1], acc[0][:, 384 * l:384 * l + V_SUB + 1])
                last = copy(cols[:, l, V_SW:V_END], acc[0][:, 384 * l + V_SW:384 * l + V_END])
            last.then_inc(acc_free[0], 1)
            act.wait_ge(pro_t, 4 + 3 * DEPTH)
            copy(cols2, acc[1][:, 0:W_END]).then_inc(acc_free[1], 1)
            act.wait_ge(rope_ang, 1)
            act.activation(rsin, ang, ACT.Sin)
            act.activation(rcos, turns, ACT.Sin).then_inc(rope_done, 1)

            with act.Fori(0, DEPTH) as l:
                def full(use, piece):
                    b = LU.buf[use]
                    act.wait_ge(acc_full[b], l * LU.per_full[b] + LU.full[use] + piece + 1)
                    return acc[b]

                def freed(use):
                    b = LU.buf[use]
                    act.wait_ge(acc_free[b], l * LU.per_turn[b] + LU.turn[use] + 1)

                def free(use):
                    return acc_free[LU.buf[use]], 1

                def gate(name, first, last):
                    n, c = {"a": 0, "b": 1, "c": 1}[name[1]], int(name[2])
                    for j in range(first, last):
                        src = full(name, j | 1)
                        i = act.activation(gates[:, n, 4 * c + j, :], src[:, SEQ * j:SEQ * j + SEQ], ACT.Tanh, scale=0.5)
                        if j == 3:
                            i.then_inc(*free(name))

                def exps(n, blocks):
                    act.wait_ge(s_max, l * 6 + n + 1)
                    for i, s in enumerate(blocks):
                        last = act.activation(s, s, ACT.Exp, bias=nmx[:, i:i + 1], accum_out=psums[:, i:i + 1])
                    last.then_inc(p_exp, 1)

                def take_transposes(n, count):
                    act.wait_ge(t_full, l * 6 + n + 1)
                    copy(PT[:, 0:count, :], shaped(aux[:, 0:P * count], count, P)).then_inc(t_out, 1)

                def root(dst, src, n, signal):
                    act.activation(dst, src, ACT.Sqrt, bias=epsc[:, 0:1], scale=1.0 / n).then_inc(*signal)

                act.wait_ge(x_new, 2 * l + 1)
                act.activation(sqx, xT, ACT.Square).then_inc(x_sq, 1)
                act.wait_ge(cur_ready, l + 1)
                act.activation(anega, rc[:, R_AL:R_AL + SM_H], ACT.Exp).then_inc(al_exp, 1)
                act.wait_ge(lam_arg, l + 1)
                act.activation(lamv[:, 4:6], lamv[:, 0:2], ACT.Exp).then_inc(lam_exp, 1)
                act.wait_ge(x_ss, l + 1)
                root(rstd, aux2[:, 0:SEQ], D, (x_rt, 1))

                for i, name in enumerate(("q", "k")):
                    for t in range(T):
                        src = full(name, t)[:, 512 * t:512 * t + 512]
                        copy(qk[:, i, t, :], src)
                        last = act.activation(sqqk[:, i, t, :], src, ACT.Square)
                    last.then_inc(*free(name))
                for t in range(T):
                    last = copy(va[:, t, :], full("v", t)[:, 512 * t:512 * t + 512])
                last.then_inc(*free("v"))
                for t in range(T):
                    src = full("ml", t)[:, 512 * t:512 * t + ML_W + SM_H]
                    copy(ml[:, t, :], src)
                    for i, (c0, c1) in enumerate(((0, Q_RANK), (Q_RANK, Q_RANK + KV_RANK), (Q_RANK + KV_RANK, ML_W))):
                        last = act.activation(junk[:, ML_W * t + c0:ML_W * t + c1], src[:, c0:c1], ACT.Square, accum_out=ssl[:, t, i:i + 1])
                last.then_inc(*free("ml"))
                act.wait_ge(qk_ss, l + 1)
                root(rs[:, 0:32], ss[:, 0:32], DA_D, (qk_rt, 1))
                act.drain()
                act.activation(rsl[:, :, 0], ssl[:, :, 0], ACT.Sqrt, bias=epsc[:, 0:1], scale=1.0 / Q_RANK)
                root(rsl[:, :, 1], ssl[:, :, 1], KV_RANK, (ml_rt, 1))
                act.wait_ge(qkT, 2 * l + 1)
                act.activation(qTa.rearrange("p h n -> p (h n)"), aux, ACT.Copy, scale=wqk).then_inc(qkT_out, 1)
                act.wait_ge(qkT, 2 * l + 2)
                copy(kTa.rearrange("p h n -> p (h n)"), aux).then_inc(qkT_out, 1)
                act.wait_ge(dt_abs, l + 1)
                act.activation(dt, dt, ACT.Exp)
                act.wait_ge(cT_t, l + 1)
                for j, c in enumerate((V_QA, V_QA + 1, V_KVA)):
                    last = act.activation(cT[:, j, :], aux[:, SEQ * j:SEQ * j + SEQ], ACT.Copy, scale=cc[:, c:c + 1])
                last.then_inc(cT_out, 1)
                act.drain()
                act.activation(dt, dt, ACT.Ln, bias=epsc[:, 1:2]).then_inc(dt_ln, 1)
                for t in range(T):
                    copy(qb[:, t].rearrange("p h n -> p (h n)"), full(f"uq{t}", 0)[:, 0:768]).then_inc(*free(f"uq{t}"))
                for t in range(T):
                    copy(kv[:, t, :], full(f"ukv{t}", 0)).then_inc(*free(f"ukv{t}"))
                act.wait_ge(cs_out, l + 1)
                act.activation(ecs, csb, ACT.Exp).then_inc(ecs_out, 1)

                for n, filler in enumerate(("ga0", "ga1", "gb0")):
                    t, h0, nh, nk = [(0, 0, 4, 1), (1, 0, 2, 2), (1, 2, 2, 2)][n]
                    K = P * nk
                    exps(n, [S[:, 512 * m + K * i:512 * m + K * (i + 1)] for m in range(2) for i in range(nh)])
                    gate(filler, 0, 2)
                    take_transposes(n, 4)
                    gate(filler, 2, 4)
                    act.wait_ge(o_full, l * 6 + n + 1)
                    for i in range(nh):
                        act.activation(junk[:, 512 * (n % 2) + P * i:512 * (n % 2) + P * (i + 1)], aux2[:, P * i:P * i + P], ACT.Square, accum_out=sso[:, t, h0 + i:h0 + i + 1])
                    copy(o[:, t, P * h0:P * (h0 + nh)], aux2[:, 0:P * nh]).then_inc(o_out, 1)
                act.drain()
                root(sso, sso, 2 * DA_D, (oa_rt, 1))
                gate("gb1", 0, 4)
                act.wait_ge(yaT_t, l + 1)
                act.activation(yT[:, 0:4, :].rearrange("p h n -> p (h n)"), aux, ACT.Copy, scale=subw).then_inc(yaT_out, 1)

                act.activation(sqq, qb, ACT.Square)
                act.activation(sqk, shaped_kv(kv)[:, :, :, 0:ML_N], ACT.Square).then_inc(m_sq, 1)
                act.wait_ge(m_ss, l + 1)
                root(rs[:, 0:32], ss[:, 0:32], ML_QK, (m_rt, 1))
                for i in range(4):
                    act.wait_ge(mT_t, 4 * l + i + 1)
                    dst, t = (qTm, kTm)[i // 2], i % 2
                    copy(dst[0:ML_QK, :, P * t:P * t + P], shaped(aux, ML_H, P)[0:ML_QK]).then_inc(mT_out, 1)
                for n in range(3):
                    t, h0, nh, nk = [(0, 0, 8, 1), (1, 0, 4, 2), (1, 4, 4, 2)][n]
                    exps(3 + n, [S[:, P * nk * i:P * nk * (i + 1)] for i in range(nh)])
                    if n < 2:
                        for u in range(T):
                            src = full(f"z{n}", u)[:, 512 * u:512 * u + 512]
                            act.activation(zb[:, u, 512 * n:512 * n + 512], src, ACT.Tanh, scale=0.5).then_inc(z_tanh, 1)
                    take_transposes(3 + n, 8)

                def conv_silu(c):
                    for j in range(4):
                        f = 4 * c + j
                        act.activation(xb[:, f, :], full(f"xbc{c}", j | 1)[:, SEQ * j:SEQ * j + SEQ], ACT.Identity,
                                       scale=swh[:, 48 + f:49 + f], bias=swh[:, 64 + f:65 + f]).then_inc(tap0, 1)
                    freed(f"xbc{c}")
                    act.activation(th, xb[:, 4 * c:4 * c + 4, :].rearrange("p h n -> p (h n)"), ACT.Tanh).then_inc(c_tanh, 1)

                def take_xs(t):
                    act.wait_ge(xsT_t, 2 * l + t + 1)
                    copy(xs[:, t, :], aux).then_inc(xs_out, 1)

                conv_silu(0)
                act.wait_ge(ybT_t, l + 1)
                copy(yT[:, 4:8, :].rearrange("p h n -> p (h n)"), aux).then_inc(ybT_out, 1)
                conv_silu(1)
                conv_silu(2)
                take_xs(0)
                conv_silu(3)
                take_xs(1)
                act.wait_ge(bm_t, l + 1)
                copy(bmt, aux2).then_inc(bm_out, 1)

                def seg_exps(hc):
                    act.wait_ge(seg_ready, 4 * l + hc + 1)
                    act.activation(E, E, ACT.Exp).then_inc(seg_exp, 1)

                seg_exps(0)
                seg_exps(1)
                act.wait_ge(merged_b, l + 1)
                gate("gc0", 0, 2)
                act.wait_ge(st_full, l + 1)
                copy(stT, aux).then_inc(st_out, 1)
                gate("gc0", 2, 4)
                seg_exps(2)
                gate("gc1", 0, 2)
                seg_exps(3)
                gate("gc1", 2, 4)
                act.wait_ge(y_gated, l + 1)
                act.activation(sqy, y, ACT.Square).then_inc(y_sq, 1)
                act.wait_ge(y_ss, l + 1)
                root(rs[:, 0:8], ss[:, 0:8], D // SM_G, (y_rt, 1))

                act.wait_ge(x_new, 2 * l + 2)
                act.activation(sqx, xT, ACT.Square).then_inc(x_sq, 1)
                root(rstd, full("n2", 0)[:, 0:SEQ], D, free("n2"))
                for i in range(11):
                    for j in range(4):
                        f = (0, FT)[j // 2] + 2 * i + j % 2
                        act.activation(u4[:, i % 2, j, :], full(f"up{i}", j | 1)[:, SEQ * j:SEQ * j + SEQ], ACT.Identity,
                                       scale=cc[:, V_FW + 4 * FT + f:V_FW + 4 * FT + f + 1],
                                       bias=cc[:, V_FB + f:V_FB + f + 1]).then_inc(u_tap, 1)
                    freed(f"up{i}")
                    act.activation(sl[:, i % 2, :], u4[:, i % 2, 0:2, :].rearrange("p h n -> p (h n)"), ACT.Silu).then_inc(u_silu, 1)

            def square_x(n):
                act.wait_ge(x_new, 2 * DEPTH + n)
                act.activation(sqx, xT, ACT.Square).then_inc(x_sq, 1)

            def root_x(n):
                act.wait_ge(x_ss, DEPTH + n)
                root(rstd, aux2[:, 0:SEQ], D, (x_rt, 1))

            def mid_full(name, piece):
                act.wait_ge(acc_full[MU.buf[name]], MU.full[name] + piece + 1)
                return acc[MU.buf[name]]

            square_x(1)
            act.dma_start(rwt[:, :, 0:GROUPS], a["router_group_w_2"].rearrange("l (k p) n -> p (l k) n", p=P)).then_inc(late_in, 16)
            act.dma_start(rwt[:, :, GROUPS:], a["router_expert_w_2"].rearrange("l (k p) n -> p (l k) n", p=P)).then_inc(late_in, 16)
            for dst, name in ((qn2, "q_norm_g_2"), (kn2, "k_norm_g_2"), (rb2[:, 0:GROUPS], "router_group_b_2"),
                              (rb2[:, GROUPS:], "router_expert_b_2")):
                act.dma_start(dst, a[name].to_broadcast([P, dst.shape[1]])).then_inc(late_in, 16)
            root_x(1)
            for t in range(T):
                src = mid_full("m_qa", t)[:, 512 * t:512 * t + 512]
                copy(qa2[:, t, :], src)
                last = act.activation(sqa2[:, t, :], src, ACT.Square)
            last.then_inc(acc_free[MU.buf["m_qa"]], 1)
            for t in range(T):
                src = mid_full("m_kva", t)[:, 512 * t:512 * t + 256]
                copy(ka2[:, t, :], src[:, 0:P])
                act.activation(sqk2[:, t, :], src[:, 0:P], ACT.Square)
                last = copy(va2[:, t, :], src[:, P:2 * P])
            last.then_inc(acc_free[MU.buf["m_kva"]], 1)
            act.wait_ge(a2_ss, 1)
            root(rs[:, 0:20], ss[:, 0:20], D2, (a2_rt, 1))
            for name, dst in (("m_qb", qb2), ("m_kb", kb2)):
                for t in range(T):
                    last = act.activation(dst[:, t, :], mid_full(name, t)[:, 512 * t:512 * t + 512], ACT.Copy,
                                          scale=D2 ** -0.5 if name == "m_qb" else 1.0)
                last.then_inc(acc_free[MU.buf[name]], 1)
            act.wait_ge(t2, 1)
            copy(qTa2.rearrange("p h n -> p (h n)"), aux).then_inc(t2_out, 1)
            for t in range(T):
                last = copy(vb2[:, t, :], mid_full("m_vb", t)[:, 512 * t:512 * t + 512])
            last.then_inc(acc_free[MU.buf["m_vb"]], 1)
            for i, dst in enumerate((kTa2, qTb2, kTb2)):
                act.wait_ge(t2, 2 + i)
                dst = dst.rearrange("p h n -> p (h n)")
                copy(dst, aux[:, 0:dst.shape[1]]).then_inc(t2_out, 1)
            for u in range(8):
                act.wait_ge(s2_max, u + 1)
                for i in range(4):
                    s = S2[u % 2][:, SEQ * i:SEQ * i + SEQ]
                    last = act.activation(s, acc[u % 2][:, SEQ * i:SEQ * i + SEQ] if u < 4 else s, ACT.Exp,
                                          bias=nmx[:, 4 * (u % 2) + i:4 * (u % 2) + i + 1], accum_out=psums[:, 4 * (u % 2) + i:4 * (u % 2) + i + 1])
                last.then_inc(p2_exp, 1)
                act.wait_ge(t3_full, u + 1)
                copy(PT2[u % 2], shaped(aux, 8, P)).then_inc(t3_out, 1)
                if u == 3 or u == 7:
                    n = u // 4
                    act.wait_ge(on_ss, 2 * n + 1)
                    for t in range(T):
                        act.activation(sqo[:, t, :], o2[n][:, t, :], ACT.Square, accum_out=ssq[:, t:t + 1])
                    act.drain()
                    root(ssq, ssq, 512, (on_ss, 1))
            square_x(2)
            root_x(2)
            for t in range(T):
                act.wait_ge(h2_t, t + 1)
                copy(h2t[:, t, :], aux).then_inc(h2_out, 1)
            act.wait_ge(lg_sub, 1)
            act.activation(ge, ge, ACT.Exp).then_inc(lg_exp, 1)
            act.wait_ge(top_sub, 1)
            act.activation(w2, m2, ACT.Exp).then_inc(top_exp, 1)
            act.wait_ge(routed, 1)
            passes = act.value_load(meta[0:1, 5:6], min_val=GROUPS, max_val=GROUPS + 1)
            with act.Fori(0, passes) as p:
                act.wait_ge(gx_full, p + 1)
                copy(xg, shaped(acc[0], KT, P)).then_inc(gx_out, 1)

                def turn_back(e):
                    act.wait_ge(he_t, p * EPG + e + 1)
                    copy(heT[:, e % 2], shaped(aux2, 4, P)).then_inc(he_out, 1)

                for e in range(EPG):
                    act.wait_ge(g_full, p * EPG + EPG + e + 1)
                    act.activation(hs[:, e % 2, :], acc[e % 2][:, 0:DE], ACT.Silu).then_inc(g_silu, 1)
                    if e:
                        turn_back(e - 1)
                turn_back(EPG - 1)
                act.wait_ge(d_done, p * EPG + 2 * EPG)
                copy(ygs, aux).then_inc(yg_out, 1)
            square_x(3)
            root_x(3)
            for t in range(T):
                act.wait_ge(f_t, t + 1)
                copy(fin[:, t, :], aux).then_inc(f_out, 1)
                act.wait_ge(f_out, t + 1)
                act.dma_start(out[0, P * t:P * t + P, :], fin[:, t, :]).then_inc(stored, 16)
            act.wait_ge(stored, 16 * T)

        @block.gpsimd
        def _(pool):
            pool.memset(ones, 1.0)
            pool.memset(epsc[:, 0:1], EPS)
            pool.memset(epsc[:, 1:2], 1.0).then_inc(fill, 1)

        @block.vector
        def _(dve):
            D_ = dve.drain
            tt, ts, stt = dve.tensor_tensor, dve.tensor_scalar, dve.scalar_tensor_tensor

            dve.wait_ge(x_in, 48)
            dve.wait_ge(small_in, 16 * N_SMALL)
            dve.tensor_copy(posf, posr)
            dve.tensor_copy(poscf, posc)
            tt(drel[:, DA_H:], rel[:, DA_H:], rel[:, 0:(BUCKETS - 1) * DA_H], ALU.subtract)
            for h in range(DA_H):
                ts(biasm[:, h, :], kc[:, K_CM:K_CM + 384], rel[:, h:h + 1], None, ALU.add)
            D_()
            ts(dist[:, 0:P], posf[:, 0:P], -1.0, poscf[:, 0:1], ALU.mult, ALU.add)
            ts(dist[:, P:3 * P], posf, -1.0, poscf[:, 1:2], ALU.mult, ALU.add)
            for t in range(T):
                ts(ang[:, t, :], kc[:, K_INV:K_INV + 16], poscf[:, t:t + 1], None, ALU.mult)
            D_()
            ROUND = 12582912.0
            ts(turns, ang, float(1 / (2 * np.pi)), ROUND, ALU.mult, ALU.add)
            D_()
            ts(turns, turns, ROUND, None, ALU.subtract)
            D_()
            two_pi, parts = 2 * np.pi, []
            for _ in range(2):
                bits = np.array([two_pi], np.float32).view(np.uint32) & np.uint32(0xFFFFE000)
                parts.append(float(bits.view(np.float32)[0]))
                two_pi -= parts[-1]
            for part in (*parts, float(np.float32(two_pi))):
                stt(ang, turns, -part, ang, ALU.mult, ALU.add)
                D_()
            half = 3.1415925
            ts(turns, ang, float(np.pi / 2), None, ALU.add)
            D_()
            ts(step[:, 0:32], turns.rearrange("p a b -> p (a b)"), half, -float(2 * np.pi), ALU.is_gt, ALU.mult)
            ts(ang, ang, half, -half, ALU.min, ALU.max)
            D_()
            tt(turns, turns, shaped(step[:, 0:32], T, 16), ALU.add)
            D_()
            ts(turns, turns, half, -half, ALU.min, ALU.max).then_inc(rope_ang, 1)
            D_()
            with dve.Fori(1, BUCKETS) as b:
                ts(step, dist, kc[:, bass.ds(b + K_THR, 1)], None, ALU.is_ge)
                D_()
                for h in range(DA_H):
                    stt(biasm[:, h, :], step, drel[:, bass.ds(b * DA_H + h, 1)], biasm[:, h, :], ALU.mult, ALU.add)
                D_()
            dve.wait_ge(acc_free[0], 1)
            dve.wait_ge(acc_free[1], 1)
            dve.wait_ge(rope_done, 1)
            dve.wait_ge(fill, 1)

            def rope(x1, x2, cos, sin, t1, t2, r1):
                tt(t1, x1, cos, ALU.mult)
                tt(t2, x2, sin, ALU.mult)
                D_()
                tt(r1, t1, t2, ALU.subtract)
                D_()
                tt(t1, x2, cos, ALU.mult)
                tt(t2, x1, sin, ALU.mult)
                D_()
                dve.tensor_copy(x1, r1)
                tt(x2, t1, t2, ALU.add)
                D_()

            with dve.Fori(0, DEPTH) as l:
                def full(use, piece):
                    b = LU.buf[use]
                    dve.wait_ge(acc_full[b], l * LU.per_full[b] + LU.full[use] + piece + 1)
                    return acc[b]

                def freed(use):
                    b = LU.buf[use]
                    dve.wait_ge(acc_free[b], l * LU.per_turn[b] + LU.turn[use] + 1)

                def free(use):
                    return acc_free[LU.buf[use]], 1

                def modulate(scale, shift):
                    dve.reciprocal(rstd, rstd)
                    D_()
                    tt(hT, xT, bc(rstd, 1, KT), ALU.mult)
                    D_()
                    for k in range(KT):
                        last = ts(hT[:, k, :], hT[:, k, :], scale[:, k:k + 1], shift[:, k:k + 1], ALU.mult, ALU.add)
                    last.then_inc(h_ready, 1)

                def add_to_x(use, k0, gain):
                    for j in range(4):
                        last = stt(xT[:, k0 + j, :], acc[LU.buf[use]][:, SEQ * j:SEQ * j + SEQ], gain[:, k0 + j:k0 + j + 1],
                                   xT[:, k0 + j, :], ALU.mult, ALU.add)
                    last.then_inc(*free(use))

                one = lambda ap: ap[:, bass.ds(l, 1)]
                dve.tensor_copy(cc[:, 0:V_SUB + 1].unsqueeze(1), one(cols)[:, :, 0:V_SUB + 1])
                dve.tensor_copy(cc[:, V_SW:V_END].unsqueeze(1), one(cols)[:, :, V_SW:V_END])
                dve.tensor_copy(rc.unsqueeze(1), one(rows))
                dve.tensor_copy(lami, shaped(kc[:, K_LAM:K_LAM + 4], 2, 2)[:, :, bass.ds(l, 1)].rearrange("p a b -> p (a b)"))
                D_().then_inc(cur_ready, 1)
                ts(swh, cc[:, V_SW:V_SB + 16], 0.5, None, ALU.mult)
                stt(wqk, cc[:, V_DQ:V_DQ + 1], DA_D ** -0.5, cc[:, V_DK:V_DK + 1], ALU.mult, ALU.mult)
                tt(subw, cc[:, V_SUB:V_SUB + 1], lami[:, 1:2], ALU.mult)
                ts(rc[:, R_MQ:R_MQ + ML_QK], rc[:, R_MQ:R_MQ + ML_QK], ML_QK ** -0.5, None, ALU.mult)
                lp = shaped(rc[:, R_LP:R_END], 2, 2, DA_D)
                tt(shaped(lamp, 2, DA_D), lp[:, :, 0, :], lp[:, :, 1, :], ALU.mult)
                D_()
                dve.tensor_reduce(lamv[:, 0:2], shaped(lamp, 2, DA_D), AX, ALU.add).then_inc(lam_arg, 1)
                dve.wait_ge(al_exp, l + 1)
                ts(anega, anega, -1.0, None, ALU.mult)
                dve.wait_ge(lam_exp, l + 1)
                tt(lamv[:, 6:7], lamv[:, 5:6], lamv[:, 4:5], ALU.subtract)
                D_()
                tt(lamv[:, 7:8], lamv[:, 6:7], lami[:, 0:1], ALU.subtract)
                dve.wait_ge(ada_done, 12 * l + 4)
                tt(mod[:, 0:16], pmod[:, 0:16], cc[:, V_ADA:V_ADA + 16], ALU.add)
                D_()
                stt(amix, mod[:, 8:16], 1.0, cc[:, V_NM:V_NM + KT], ALU.add, ALU.mult)
                dve.wait_ge(x_rt, l + 1)
                modulate(amix, mod[:, 0:8])

                freed("q")
                freed("k")
                dve.tensor_reduce(ss[:, 0:32], sqqk.rearrange("p i t (g d) -> p (i t g) d", d=DA_D), AX, ALU.add).then_inc(qk_ss, 1)
                dve.wait_ge(qk_rt, l + 1)
                dve.reciprocal(rs[:, 0:32], rs[:, 0:32])
                D_()
                heads = qk.rearrange("p i t (g d) -> p (i t g) d", d=DA_D)
                tt(heads, heads, bc(rs[:, 0:32], 2, DA_D), ALU.mult).then_inc(qk_n, 1)
                dve.wait_ge(ml_rt, l + 1)
                dve.reciprocal(rsl[:, :, 0:2], rsl[:, :, 0:2])
                D_()
                for t in range(T):
                    ts(ml[:, t, 0:Q_RANK], ml[:, t, 0:Q_RANK], rsl[:, t, 0:1], None, ALU.mult)
                    last = ts(ml[:, t, Q_RANK:Q_RANK + KV_RANK], ml[:, t, Q_RANK:Q_RANK + KV_RANK], rsl[:, t, 1:2], None, ALU.mult)
                last.then_inc(c_n, 1)
                tt(dtn, ml[:, :, ML_W:ML_W + SM_H], bc(rc[:, R_DTB:R_DTB + SM_H], 1, T), ALU.add)
                D_()
                ts(dt, dtn, -1.0, None, ALU.mult)
                D_()
                tt(dt, dt, dtn, ALU.min).then_inc(dt_abs, 1)
                dve.wait_ge(dt_ln, l + 1)
                stt(dt, dtn, 0.0, dt, ALU.max, ALU.add)
                D_()
                tt(da, dt, bc(anega, 1, T), ALU.mult).then_inc(dt_ready, 1)
                dve.wait_ge(cs_full, l + 1)
                dve.tensor_copy(csb, shaped(pmod[:, 48:80], T, SM_H)).then_inc(cs_out, 1)

                for n in range(3):
                    t, h0, nh, nk = [(0, 0, 4, 1), (1, 0, 2, 2), (1, 2, 2, 2)][n]
                    K = P * nk
                    k0 = P if t else 0
                    dve.wait_ge(s_full, l * 6 + n + 1)
                    maps = [shaped(S[:, 512 * m:512 * m + K * nh], nh, K) for m in range(2)]
                    for m in range(2):
                        tt(maps[m], shaped(aux[:, 512 * m:512 * m + K * nh], nh, K), biasm[:, h0:h0 + nh, k0:k0 + K], ALU.add)
                    D_()
                    for m in range(2):
                        last = dve.tensor_reduce(nmx[:, nh * m:nh * m + nh], maps[m], AX, ALU.max, negate=True)
                    last.then_inc(s_max, 1)
                    dve.wait_ge(p_exp, l * 6 + n + 1)
                    dve.reciprocal(rps[:, 0:2 * nh], psums[:, 0:2 * nh])
                    D_()
                    ts(nlr[:, 0:nh], rps[:, nh:2 * nh], lamv[:, 7:8], None, ALU.mult)
                    D_()
                    for i in range(nh):
                        ts(maps[1][:, i, :], maps[1][:, i, :], nlr[:, i:i + 1], None, ALU.mult)
                    D_()
                    for i in range(nh):
                        last = stt(maps[0][:, i, :], maps[0][:, i, :], rps[:, i:i + 1], maps[1][:, i, :], ALU.mult, ALU.add)
                    last.then_inc(w_mix, 1)
                dve.wait_ge(oa_rt, l + 1)
                dve.reciprocal(sso, sso)
                D_()
                heads = o.rearrange("p t (h d) -> p (t h) d", d=2 * DA_D)
                tt(heads, heads, bc(sso.rearrange("p t h -> p (t h)"), 2, 2 * DA_D), ALU.mult).then_inc(oa_n, 1)

                tt(krr, ml[:, :, Q_RANK + KV_RANK:ML_W], bc(rc[:, R_MK + ML_N:R_MK + ML_QK], 1, T), ALU.mult)
                D_()
                rope(krr[:, :, 0:16], krr[:, :, 16:32], rcos, rsin, tmp1[:, :, 0, :], tmp2[:, :, 0, :], rot1[:, :, 0, :])
                dve.wait_ge(m_sq, l + 1)
                dve.tensor_reduce(ss[:, 0:16], sqq.rearrange("p t h n -> p (t h) n"), AX, ALU.add)
                dve.tensor_reduce(ss[:, 16:32], sqk.rearrange("p t h n -> p (t h) n"), AX, ALU.add)
                D_()
                for t in range(T):
                    last = ts(ss[:, 16 + 8 * t:24 + 8 * t], ss[:, 16 + 8 * t:24 + 8 * t], ssl[:, t, 2:3], None, ALU.add)
                last.then_inc(m_ss, 1)
                dve.wait_ge(m_rt, l + 1)
                dve.reciprocal(rs[:, 0:32], rs[:, 0:32])
                D_()
                heads, kheads = qb.rearrange("p t h n -> p (t h) n"), kb.rearrange("p t h n -> p (t h) n")
                tt(heads, heads, bc(rs[:, 0:16], 2, ML_QK), ALU.mult)
                for t in range(T):
                    tt(kb[:, t, :, 0:ML_N], shaped_kv(kv)[:, t, :, 0:ML_N], bc(rs[:, 16 + 8 * t:24 + 8 * t], 2, ML_N), ALU.mult)
                    tt(kb[:, t, :, ML_N:], bc(krr[:, t, :], 1, ML_H), bc(rs[:, 16 + 8 * t:24 + 8 * t], 2, ML_R), ALU.mult)
                D_()
                tt(heads, heads, bc(rc[:, R_MQ:R_MQ + ML_QK], 1, T * ML_H), ALU.mult)
                tt(kheads[:, :, 0:ML_N], kheads[:, :, 0:ML_N], bc(rc[:, R_MK:R_MK + ML_N], 1, T * ML_H), ALU.mult)
                D_()
                rope(qb[:, :, :, ML_N:ML_N + 16], qb[:, :, :, ML_N + 16:], bc(rcos, 2, ML_H), bc(rsin, 2, ML_H), tmp1, tmp2, rot1)
                D_().then_inc(m_n, 1)
                for n in range(3):
                    t, h0, nh, nk = [(0, 0, 8, 1), (1, 0, 4, 2), (1, 4, 4, 2)][n]
                    K = P * nk
                    dve.wait_ge(s_full, l * 6 + 3 + n + 1)
                    mask = kc[:, K_CM + (P if t else 0):K_CM + (P if t else 0) + K]
                    tt(shaped(S, nh, K), shaped(aux, nh, K), bc(mask, 1, nh), ALU.add)
                    D_()
                    dve.tensor_reduce(nmx[:, 0:nh], shaped(S, nh, K), AX, ALU.max, negate=True).then_inc(s_max, 1)
                    if n < 2:
                        for u in range(T):
                            dve.wait_ge(z_tanh, 4 * l + 2 * n + u + 1)
                            part = zb[:, u, 512 * n:512 * n + 512]
                            last = stt(part, part, 1.0, acc[LU.buf[f"z{n}"]][:, 512 * u:512 * u + 512], ALU.add, ALU.mult)
                        last.then_inc(*free(f"z{n}"))
                    else:
                        for u in range(2):
                            part = gates[:, 0, 4 * u:4 * u + 4, :].rearrange("p k n -> p (k n)")
                            stt(part, part, 1.0, full(f"ba{u}", 3), ALU.add, ALU.mult).then_inc(*free(f"ba{u}"))
                    dve.wait_ge(p_exp, l * 6 + 3 + n + 1)
                    dve.reciprocal(rps[:, 0:nh], psums[:, 0:nh])
                    D_()
                    dve.wait_ge(o_full, l * 6 + 3 + n + 1)
                    tt(shaped(o[:, t, ML_V * h0:ML_V * (h0 + nh)], nh, ML_V), shaped(aux2[:, 0:ML_V * nh], nh, ML_V),
                       bc(rps[:, 0:nh], 2, ML_V), ALU.mult).then_inc(o_out, 1)

                for c in range(4):
                    dve.wait_ge(tap0, 16 * l + 4 * c + 4)
                    for k in (2, 1, 0):
                        d = 3 - k
                        for j in range(4):
                            f = 4 * c + j
                            last = stt(xb[:, f, d:], acc[LU.buf[f"xbc{c}"]][:, SEQ * j:SEQ * j + SEQ - d], swh[:, 16 * k + f:16 * k + f + 1],
                                       xb[:, f, d:], ALU.mult, ALU.add)
                        if k:
                            D_()
                    last.then_inc(*free(f"xbc{c}"))
                    dve.wait_ge(c_tanh, 4 * l + c + 1)
                    part = xb[:, 4 * c:4 * c + 4, :].rearrange("p h n -> p (h n)")
                    stt(part, th, 1.0, part, ALU.add, ALU.mult).then_inc(xb_ready, 1)

                def decay_rows(hc):
                    t, h0 = hc // 2, 8 * (hc % 2)
                    tt(tria, bc(tri, 1, 8), bc(da[:, t, h0:h0 + 8], 2, P), ALU.mult).then_inc(tria_ready, 1)

                def take_cb(t):
                    dve.wait_ge(cb_full, 2 * l + t + 1)
                    tt(cbm, shaped(aux2, SM_G, P), bc(tri, 1, SM_G), ALU.mult).then_inc(cb_out, 1)

                def branch_b(u):
                    part = gates[:, 1, 4 * u:4 * u + 4, :].rearrange("p k n -> p (k n)")
                    stt(part, part, 1.0, full(f"bb{u}", 3), ALU.add, ALU.mult).then_inc(*free(f"bb{u}"))

                decay_rows(0)
                dve.wait_ge(xs_out, 2 * l + 2)
                for t in range(T):
                    tt(shaped(xdt[:, t, :], SM_H, SM_D), shaped(xs[:, t, :], SM_H, SM_D), bc(dt[:, t, :], 2, SM_D), ALU.mult)
                branch_b(0)
                take_cb(0)
                for hc in range(4):
                    t, h0 = hc // 2, 8 * (hc % 2)
                    dve.wait_ge(r_full, 4 * l + hc + 1)
                    tt(E, shaped(aux, 8, P), bc(csb[:, t, h0:h0 + 8], 2, P), ALU.subtract)
                    D_()
                    ts(E, E, 0.0, None, ALU.min).then_inc(seg_ready, 1)
                    if hc < 3:
                        decay_rows(hc + 1)
                    if hc == 0:
                        branch_b(1)
                        D_()
                        g0, g1 = (gates[:, n].rearrange("p k n -> p (k n)") for n in range(2))
                        tt(g0, g0, g1, ALU.add).then_inc(merged_b, 1)
                    half_y, half_x = y[:, t, SM_D * h0:SM_D * (h0 + 8)], xs[:, t, SM_D * h0:SM_D * (h0 + 8)]
                    tt(shaped(half_y, 8, SM_D), shaped(half_x, 8, SM_D), bc(rc[:, R_SD + h0:R_SD + h0 + 8], 2, SM_D), ALU.mult)
                    D_()
                    dve.wait_ge(seg_exp, 4 * l + hc + 1)
                    if t == 0:
                        tt(xe[:, h0:h0 + 8, :], shaped(xdt[:, t, SM_D * h0:SM_D * (h0 + 8)], 8, SM_D),
                           E[:, :, P - 1:P].to_broadcast([P, 8, SM_D]), ALU.mult)
                        D_()
                    groups = E.rearrange("p (g r) n -> p g r n", g=2)
                    tt(groups, groups, bc(cbm[:, h0 // 4:h0 // 4 + 2, :], 2, 4), ALU.mult).then_inc(m_ready, 1)
                    dve.wait_ge(y_full, 4 * l + hc + 1)
                    tt(half_y, half_y, aux2, ALU.add).then_inc(y_out, 1)
                    if hc == 1:
                        take_cb(1)
                dve.wait_ge(yo_full, l + 1)
                dve.wait_ge(ecs_out, l + 1)
                off = E.rearrange("p h n -> p (h n)")
                tt(shaped(off, SM_H, SM_D), shaped(aux, SM_H, SM_D), bc(ecs[:, 1, :], 2, SM_D), ALU.mult)
                D_()
                tt(y[:, 1, :], y[:, 1, :], off, ALU.add)
                D_()
                stt(y.rearrange("p t n -> p (t n)"), y.rearrange("p t n -> p (t n)"), 0.5, zb.rearrange("p t n -> p (t n)"),
                    ALU.mult, ALU.mult).then_inc(y_gated, 1)
                dve.wait_ge(y_sq, l + 1)
                dve.tensor_reduce(ss[:, 0:8], sqy.rearrange("p t (g n) -> p (t g) n", g=SM_G), AX, ALU.add).then_inc(y_ss, 1)
                dve.wait_ge(ada_done, 12 * l + 6)
                tt(mod[:, 16:24], pmod[:, 16:24], cc[:, V_ADA + 16:V_ADA + 24], ALU.add)
                D_()
                ts(gmh, mod[:, 16:24], 0.5, None, ALU.mult)
                dve.wait_ge(y_rt, l + 1)
                dve.reciprocal(rs[:, 0:8], rs[:, 0:8])
                D_()
                parts_y = y.rearrange("p t (g n) -> p (t g) n", g=SM_G)
                tt(parts_y, parts_y, bc(rs[:, 0:8], 2, D // SM_G), ALU.mult).then_inc(y_n, 1)
                for t in range(T):
                    dve.wait_ge(ysT_t, 2 * l + t + 1)
                    tt(ysT[:, :, P * t:P * t + P], shaped(aux, KT, P), bc(cc[:, V_SN:V_SN + KT], 2, P), ALU.mult).then_inc(ysT_out, 1)
                freed("gc0")
                freed("gc1")
                for i in range(2):
                    part, total = (gates[:, n, 4 * i:4 * i + 4, :].rearrange("p k n -> p (k n)") for n in (1, 0))
                    stt(part, part, 1.0, full(f"bc{i}", 3), ALU.add, ALU.mult).then_inc(*free(f"bc{i}"))
                    D_()
                    last = tt(total, total, part, ALU.add)
                last.then_inc(merged, 1)
                for i in range(2):
                    full(f"wo{i}", 3)
                    add_to_x(f"wo{i}", 4 * i, gmh)
                D_().then_inc(x_new, 1)

                dve.wait_ge(ada_done, 12 * l + 12)
                tt(mod[:, 24:48], pmod[:, 24:48], cc[:, V_ADA + 24:V_ADA + 48], ALU.add)
                D_()
                stt(affn, mod[:, 32:40], 1.0, cc[:, V_NF:V_NF + KT], ALU.add, ALU.mult)
                freed("n2")
                modulate(affn, mod[:, 24:32])
                for i in range(11):
                    dve.wait_ge(u_tap, 44 * l + 4 * i + 4)
                    for k in (1, 0):
                        d = 2 - k
                        for j in range(4):
                            f = (0, FT)[j // 2] + 2 * i + j % 2
                            last = stt(u4[:, i % 2, j, d:], acc[LU.buf[f"up{i}"]][:, SEQ * j:SEQ * j + SEQ - d],
                                       cc[:, V_FW + 2 * FT * k + f:V_FW + 2 * FT * k + f + 1], u4[:, i % 2, j, d:], ALU.mult, ALU.add)
                        if k:
                            D_()
                    last.then_inc(*free(f"up{i}"))
                    dve.wait_ge(u_silu, 11 * l + i + 1)
                    tt(act[:, 2 * i:2 * i + 2, :].rearrange("p h n -> p (h n)"), sl[:, i % 2, :],
                       u4[:, i % 2, 2:4, :].rearrange("p h n -> p (h n)"), ALU.mult).then_inc(act_ready, 1)
                dve.wait_ge(dn_done, 6 * l + 12)
                for i in range(2):
                    add_to_x(f"dn{i}", 4 * i, mod[:, 40:48])
                D_().then_inc(x_new, 1)

            def norm_x(n, gain):
                dve.wait_ge(x_rt, DEPTH + n)
                dve.reciprocal(rstd, rstd)
                D_()
                tt(hT, xT, bc(rstd, 1, KT), ALU.mult)
                D_()
                for k in range(KT):
                    last = ts(hT[:, k, :], hT[:, k, :], gain[:, k:k + 1], None, ALU.mult)
                last.then_inc(h_ready, 1)

            norm_x(1, cols2[:, W_N1:W_OA])
            dve.wait_ge(late_in, 16 * 6)
            ts(qn2, qn2, D2 ** -0.5, None, ALU.mult)
            for name in ("m_qa", "m_kva"):
                dve.wait_ge(acc_free[MU.buf[name]], MU.turn[name] + 1)
            dve.tensor_reduce(ss[:, 0:16], sqa2.rearrange("p t (h d) -> p (t h) d", d=D2), AX, ALU.add)
            dve.tensor_reduce(ss[:, 16:20], sqk2.rearrange("p t (h d) -> p (t h) d", d=D2), AX, ALU.add).then_inc(a2_ss, 1)
            dve.wait_ge(a2_rt, 1)
            dve.reciprocal(rs[:, 0:20], rs[:, 0:20])
            D_()
            qh, kh = qa2.rearrange("p t (h d) -> p (t h) d", d=D2), ka2.rearrange("p t (h d) -> p (t h) d", d=D2)
            tt(qh, qh, bc(rs[:, 0:16], 2, D2), ALU.mult)
            tt(kh, kh, bc(rs[:, 16:20], 2, D2), ALU.mult)
            D_()
            tt(qh, qh, bc(qn2, 1, 16), ALU.mult)
            tt(kh, kh, bc(kn2, 1, 4), ALU.mult)
            D_()

            def rope2(x, heads, cos, sin):
                v = x.rearrange("p t (h s d) -> p t h s d", s=2, d=32)
                c, s = (bc(shaped(kc[:, at:at + 64], T, 32), 2, heads) for at in (cos, sin))
                rope(v[:, :, :, 0, :], v[:, :, :, 1, :], c, s, rt1[:, :, 0:heads], rt2[:, :, 0:heads], rr1[:, :, 0:heads])

            rope2(qa2, H2, K_AC, K_AS)
            rope2(ka2, 2, K_AC, K_AS)
            for i in range(2):
                for t in range(T):
                    dve.tensor_copy(kd2[:, t, :, i, :], shaped(ka2[:, t, :], 2, D2))
            D_().then_inc(a2_n, 1)
            for name in ("m_qb", "m_kb"):
                dve.wait_ge(acc_free[MU.buf[name]], MU.turn[name] + 1)
            rope2(qb2, H2, K_LC, K_LS)
            rope2(kb2, H2, K_LC, K_LS)
            D_().then_inc(b2_n, 1)

            def take_output(u):
                t, n = u // 2 % 2, u // 4
                dve.wait_ge(o2_full, u + 1)
                dst = o2[n][:, t, 256 * (u % 2):256 * (u % 2) + 256].rearrange("p (i m d) -> p i m d", i=2, m=2)
                r = rps[:, 4 * (u % 2):4 * (u % 2) + 4].rearrange("p (m i) -> p i m", m=2)
                tt(dst, shaped(aux2[:, 0:256], 2, 2, D2), bc(r, 3, D2), ALU.mult).then_inc(o2_out, 1)

            def norm_output(n):
                D_().then_inc(on_ss, 1)
                dve.wait_ge(on_ss, 2 * n + 2)
                dve.reciprocal(ssq, ssq)
                D_()
                for t in range(T):
                    last = ts(o2[n][:, t, :], o2[n][:, t, :], ssq[:, t:t + 1], None, ALU.mult)
                last.then_inc(on_n, 1)

            def output_T(n):
                dve.wait_ge(oT_t, n + 1)
                gain = cols2[:, (W_OA, W_OB)[n]:(W_OA, W_OB)[n] + 4]
                tt(hT[:, 4 * n:4 * n + 4, :], shaped(aux, 4, SEQ), bc(gain, 2, SEQ), ALU.mult).then_inc(oT_out, 1)

            for u in range(8):
                b, t = u % 2, u // 2 % 2
                dve.wait_ge(s2_full, u + 1)
                src = shaped(acc[b], 4, SEQ)
                if u >= 4:
                    dst = shaped(S2[b], 4, SEQ)
                    tt(dst, src, bc(kc[:, K_LNC + SEQ * t:K_LNC + SEQ * (t + 1)], 1, 4), ALU.add)
                    D_()
                    src = dst
                dve.tensor_reduce(nmx[:, 4 * b:4 * b + 4], src, AX, ALU.max, negate=True).then_inc(s2_max, 1)
                if u:
                    take_output(u - 1)
                if u == 4:
                    norm_output(0)
                if u == 5:
                    output_T(0)
                dve.wait_ge(p2_exp, u + 1)
                dve.reciprocal(rps[:, 4 * b:4 * b + 4], psums[:, 4 * b:4 * b + 4])
                D_()
            take_output(7)
            norm_output(1)
            output_T(1)
            for i in range(2):
                name = f"m_wo{i}"
                dve.wait_ge(acc_full[MU.buf[name]], MU.full[name] + 4)
                part = xT[:, 4 * i:4 * i + 4, :].rearrange("p k n -> p (k n)")
                last = tt(part, part, acc[MU.buf[name]], ALU.add)
            last.then_inc(x_new, 1)

            norm_x(2, cols2[:, W_N2:W_FN])

            def first_of(dst, x, best, n):
                dve.tensor_reduce(best, x, AX, ALU.max)
                D_()
                tt(dst, x, bc(best, 2, n), ALU.is_equal)
                D_()
                tt(ev[:, :, 0:n], dst, bc(kc[:, K_TIE:K_TIE + n], 1, T), ALU.mult)
                D_()
                dve.tensor_reduce(vm, ev[:, :, 0:n], AX, ALU.max)
                D_()
                tt(dst, ev[:, :, 0:n], bc(vm, 2, n), ALU.is_equal)
                D_()

            dve.wait_ge(lg_full, 1)
            tt(lg, shaped(pmod[:, 128:200], T, 36), bc(rb2, 1, T), ALU.add)
            D_()
            first_of(og, lg[:, :, 0:GROUPS], gm, GROUPS)
            D_().then_inc(og_ready, 1)
            tt(ge, lg[:, :, 0:GROUPS], bc(gm, 2, GROUPS), ALU.subtract).then_inc(lg_sub, 1)
            tt(em, lg[:, :, GROUPS:].rearrange("p t (g e) -> p t g e", g=GROUPS), bc(og, 3, EPG), ALU.mult)
            D_()
            dve.tensor_reduce(ei, em.rearrange("p t g e -> p t e g"), AX, ALU.add)
            D_()
            first_of(o1, ei, m1, EPG)
            stt(ei, o1, NEG, ei, ALU.mult, ALU.add)
            D_()
            first_of(o2nd, ei, m2, EPG)
            tt(m2, m2, m1, ALU.subtract).then_inc(top_sub, 1)
            dve.wait_ge(lg_exp, 1)
            dve.tensor_reduce(gp, ge, AX, ALU.add)
            D_()
            dve.reciprocal(gp, gp)
            dve.wait_ge(top_exp, 1)
            ts(w1, w2, 1.0, None, ALU.add)
            D_()
            dve.reciprocal(w1, w1)
            D_()
            tt(w1, w1, gp, ALU.mult)
            D_()
            tt(w2, w2, w1, ALU.mult)
            tt(o1, o1, bc(w1, 2, EPG), ALU.mult)
            D_()
            tt(o2nd, o2nd, bc(w2, 2, EPG), ALU.mult)
            D_()
            tt(gate8, o1, o2nd, ALU.add)
            dve.wait_ge(pos_full, 1)
            tt(psl[:, :, 0:GROUPS], shaped(pmod[:, 256:264], T, GROUPS), og, ALU.mult)
            ts(over, pmod[:, 264:268], float(P), None, ALU.is_gt)
            D_()
            ts(psl[:, :, 0:GROUPS], psl[:, :, 0:GROUPS], -1.0, None, ALU.add)
            tt(metaf[:, 0:GROUPS], over, kc[:, K_IOTA:K_IOTA + GROUPS], ALU.mult)
            D_()
            dve.tensor_reduce(psl[:, :, GROUPS], psl[:, :, 0:GROUPS], AX, ALU.max)
            dve.tensor_reduce(metaf[:, 4:5], metaf[:, 0:GROUPS], AX, ALU.add)
            dve.tensor_reduce(metaf[:, 5:6], over, AX, ALU.add)
            D_()
            ts(psl[:, :, GROUPS], psl[:, :, GROUPS], -float(P), None, ALU.add)
            ts(metaf[:, 5:6], metaf[:, 5:6], float(GROUPS), None, ALU.add)
            dve.tensor_copy(metaf[:, 0:GROUPS], kc[:, K_IOTA:K_IOTA + GROUPS])
            D_()
            dve.tensor_copy(meta[:, 0:6], metaf[:, 0:6])
            D_().then_inc(routed, 1)
            D_().then_inc(x_added, 1)
            passes = dve.value_load(meta[0:1, 5:6], min_val=GROUPS, max_val=GROUPS + 1)
            with dve.Fori(0, passes) as p:
                for t in range(T):
                    last = ts(pm[:, t, :], kc[:, K_IOTA:K_IOTA + P], psl[:, t, bass.ds(p, 1)], None, ALU.is_equal)
                last.then_inc(pm_ready, 1)
                dve.wait_ge(pt_full, p + 1)
                dve.tensor_copy(gsl, pmod[:, 300:300 + EPG])
                dve.tensor_copy(pmT, aux2[:, 0:SEQ]).then_inc(pt_out, 1)
                D_()
                for e in range(EPG):
                    dve.wait_ge(g_silu, p * EPG + e + 1)
                    dve.wait_ge(u_full, p * EPG + EPG + e + 1)
                    stt(he[:, e % 2, :], hs[:, e % 2, :], gsl[:, e:e + 1], acc[e % 2][:, DE:2 * DE], ALU.mult, ALU.mult)\
                        .then_inc(he_ready, 1)
                dve.wait_ge(sc_full, p + 1)
                for i in range(2):
                    part = xT[:, 4 * i:4 * i + 4, :].rearrange("p k n -> p (k n)")
                    last = tt(part, part, acc[i], ALU.add)
                last.then_inc(x_added, 1)
            D_().then_inc(x_new, 1)
            norm_x(3, cols2[:, W_FN:W_END])


ARGS = [
    "x", "c", "positions", "rel_bias", "ada_w", "ada_b", "norm_mix", "norm_ffn", "w_in", "da_q_norm", "da_k_norm",
    "da_lambda", "da_subln", "mla_q_a_norm", "mla_kv_a_norm", "mla_w_uq", "mla_w_ukv", "mla_q_norm",
    "mla_k_norm", "ssm_conv_w", "ssm_conv_b", "ssm_dt_bias", "ssm_a_log", "ssm_d", "ssm_norm", "w_branch_a",
    "w_branch_b", "w_branch_c", "w_out", "ffn_w_up", "ffn_conv_w", "ffn_conv_b", "ffn_w_down", "norm1_g_2",
    "w_in_2", "q_norm_g_2", "k_norm_g_2", "out_norm_a_g_2", "out_norm_b_g_2", "w_out_2", "norm2_g_2",
    "router_group_w_2", "router_group_b_2", "router_expert_w_2", "router_expert_b_2", "w_gate_2", "w_up_2",
    "w_down_2", "final_norm_g_2",
]


def kernel(**inputs):
    import numpy as _np
    import concourse.bacc as _bacc
    from concourse.bass_utils import run_bass_kernel_spmd as _run

    nc = _bacc.Bacc("TRN2", target_bir_lowering=False, num_devices=1)
    arrays, args = {}, {}
    for name in ARGS:
        v = _np.ascontiguousarray(inputs[name])
        arrays[f"in_{name}"] = v
        args[name] = nc.dram_tensor(f"in_{name}", v.shape, mybir.dt.from_np(v.dtype), kind="ExternalInput").ap()
    arrays["shape_constants"] = shape_constants()
    consts = nc.dram_tensor("shape_constants", (P, K_END), F32, kind="ExternalInput").ap()
    out = nc.dram_tensor("out", (1, SEQ, D), F32, kind="ExternalOutput").ap()
    program(nc, args, consts, out)
    r = _run(nc, [arrays], core_ids=[0])
    return r.results[0]["out"]
```

```python
from contextlib import ExitStack

import numpy as np

import concourse.bass as bass
from concourse import mybir

F32 = mybir.dt.float32
I32 = mybir.dt.int32
ALU = mybir.AluOpType
ACT = mybir.ActivationFunctionType
AX = mybir.AxisListType.X

P = 128
D = 1024
SEQ = 256
T = SEQ // P
KT = D // P
DEPTH = 2
EPS = 1e-6
NEG = -1e30

DA_H, DA_D = 4, 64
ML_H, ML_N, ML_R, ML_V = 8, 64, 32, 64
ML_QK = ML_N + ML_R
Q_RANK, KV_RANK = 256, 128
SM_H, SM_D, SM_G, SM_N = 16, 64, 4, 128
FFN = 2816
FT = FFN // P
BUCKETS, MAX_DIST = 32, 128
LAM_INIT = [0.8 - 0.6 * float(np.exp(-0.3 * l)) for l in range(DEPTH)]

C_Q, C_K, C_V, C_ML = 0, 512, 1024, 1536
ML_W = Q_RANK + KV_RANK + ML_R
C_Z = C_ML + ML_W
C_XBC = C_Z + D
C_DT = C_XBC + 2048
C_G = C_DT + SM_H

H2, D2 = 8, 64
GROUPS, EPG, DE = 4, 8, 512
GRID_W, THETA = 64, 10000.0

SLOTS = 4
SLOT = 4096

K_ID, K_TRI, K_CM = 0, 128, 256
K_IOTA = K_CM + 384
K_INV = K_IOTA + 128
K_THR = K_INV + 16
K_LAM = K_THR + 32
K_TIE = K_LAM + 4
K_AC, K_AS = K_TIE + 8, K_TIE + 72
K_LC, K_LS = K_TIE + 136, K_TIE + 200
K_LNC = K_TIE + 264
K_END = K_LNC + 512

V_FW, V_FB, V_ADA, V_NM, V_NF, V_SN, V_QA, V_KVA, V_SUB = 0, 132, 176, 224, 232, 240, 248, 250, 251
V_SW, V_SB, V_DQ, V_DK, V_END = 256, 320, 336, 337, 338
W_N1, W_OA, W_OB, W_N2, W_FN, W_END = 0, 8, 12, 16, 24, 32
R_MQ, R_MK, R_DTB, R_AL, R_SD, R_LP, R_END = 0, 96, 192, 208, 224, 240, 496


def shape_constants():
    k = np.zeros((P, K_END), np.float32)
    i = np.arange(P)
    k[:, K_ID:K_ID + P] = np.eye(P)
    k[:, K_TRI:K_TRI + P] = i[:, None] <= i[None, :]
    causal = np.where(i[None, :] <= i[:, None], 0.0, NEG)
    k[:, K_CM:K_CM + P] = causal
    k[:, K_CM + 2 * P:K_CM + 3 * P] = causal
    k[:, K_IOTA:K_IOTA + P] = i[None, :]
    k[:, K_INV:K_INV + 16] = np.float32(THETA) ** (-np.arange(0, ML_R, 2, dtype=np.float32) / np.float32(ML_R))
    half = BUCKETS // 2
    thr = list(range(half + 1)) + [
        min(d for d in range(half, MAX_DIST + 1) if (d / half) ** half >= (MAX_DIST / half) ** j * (1 - 1e-12))
        for j in range(1, half)]
    k[:, K_THR:K_THR + BUCKETS] = np.array(thr[:BUCKETS], np.float32)
    k[:, K_LAM:K_LAM + 2] = LAM_INIT
    k[:, K_LAM + 2:K_LAM + 4] = [1.0 - v for v in LAM_INIT]
    k[:, K_TIE:K_TIE + 8] = 8 - np.arange(8)
    t = np.arange(SEQ)
    inv = lambda n: (1.0 / (np.float32(THETA) ** (np.arange(0, n, 2, dtype=np.float32) / np.float32(n)))).astype(np.float32)
    axial = np.concatenate([(t // GRID_W).astype(np.float32)[:, None] * inv(D2 // 2),
                            (t % GRID_W).astype(np.float32)[:, None] * inv(D2 // 2)], 1)
    linear = t.astype(np.float32)[:, None] * inv(D2)
    for a, c, s in ((axial, K_AC, K_AS), (linear, K_LC, K_LS)):
        for n in range(T):
            k[:, c + 32 * n:c + 32 * n + 32] = np.cos(a[n * P:(n + 1) * P])
            k[:, s + 32 * n:s + 32 * n + 32] = np.sin(a[n * P:(n + 1) * P])
    count = np.zeros((SEQ, SEQ))
    for window, dil in ((128, 1), (512, 4), (2048, 16)):
        r = window // (2 * dil)
        same = (t[:, None] % dil) == (t[None, :] % dil)
        count += same & (np.abs(t[:, None] // dil - t[None, :] // dil) <= r)
    lnc = np.where(count > 0, np.log(np.maximum(count, 1)), NEG)
    for n in range(T):
        k[:, K_LNC + SEQ * n:K_LNC + SEQ * (n + 1)] = lnc[n * P:(n + 1) * P]
    return k


LAYER_CHUNKS = (["q", "k", "ada4", "v", "ml", "ada5", "uqkv", "ada6", "ga0", "ada7", "ga1", "gb0", "ada8", "gb1",
                 "z0", "z1", "ba"] + [f"xbc{i}" for i in range(4)] + ["bb", "gc0", "gc1", "bc0", "ada9", "bc1", "ada10",
                 "wo0", "ada11", "wo1"] + [f"up{i}" for i in range(11)]
                + ["dn0", "dn1", "ada0", "dn2", "ada1", "dn3", "ada2", "dn4", "ada3", "dn5"])
ADA_ORDER = [int(name[3:]) for name in LAYER_CHUNKS if name.startswith("ada")]
ADA_AHEAD = 4
ADA_POOL = 5
assert DEPTH == 2 and ADA_ORDER[-ADA_AHEAD:] == list(range(ADA_AHEAD))
MID_CHUNKS = ["m_qa", "m_kva", "m_qb", "m_kb", "m_vb", "m_wo0", "m_wo1"]
PASS_CHUNKS = ["e_g0", "e_u0"] + [x for e in range(1, EPG) for x in (f"e_g{e}", f"e_u{e}", f"e_d{e - 1}")] + [f"e_d{EPG - 1}"]
TWO_DMAS = ("ml", "uqkv", *(f"up{i}" for i in range(11)))
assert len(LAYER_CHUNKS) % SLOTS == 0 and len(PASS_CHUNKS) % SLOTS == 0

B1, B2, B3, B4 = 17, 20, 24, 28

LAYER_USES = [("q", 2), ("k", 2), ("v", 2), ("ml", 2), ("uq0", 1), ("uq1", 1), ("ukv0", 1), ("ukv1", 1),
              ("ga0", 4), ("ga1", 4), ("gb0", 4), ("gb1", 4), ("z0", 2), ("z1", 2), ("ba0", 4), ("ba1", 4),
              ("xbc0", 4), ("xbc1", 4), ("xbc2", 4), ("xbc3", 4), ("bb0", 4), ("bb1", 4), ("gc0", 4), ("gc1", 4),
              ("bc0", 4), ("bc1", 4), ("wo0", 4), ("wo1", 4)] + [(f"up{i}", 4) for i in range(11)] + [("dn0", 0)]
assert len(LAYER_USES) % 2 == 0


class Use:

    def __init__(self, names, first=(0, 0), free=(1, 1)):
        self.buf, self.full, self.turn = {}, {}, {}
        full, turn = list(first), list(free)
        for i, (name, pieces) in enumerate(names):
            b = i % 2
            self.buf[name], self.full[name], self.turn[name] = b, full[b], turn[b]
            full[b] += pieces
            turn[b] += 1
        self.next_full, self.next_turn = full, turn
        self.per_full = [full[b] - first[b] for b in range(2)]
        self.per_turn = [turn[b] - free[b] for b in range(2)]


LU = Use(LAYER_USES)


MID_USES = [("m_qa", 2), ("m_kva", 2), ("m_qb", 2), ("m_kb", 2), ("m_vb", 2), ("m_wo0", 4), ("m_wo1", 4)]
MU = Use(MID_USES, [DEPTH * n for n in LU.per_full], [1 + DEPTH * n for n in LU.per_turn])


def ring_table(chunks, first_slot, landed):
    where, total = {}, list(landed)
    for i, name in enumerate(chunks):
        s = (first_slot + i) % SLOTS
        total[s] += 16 * (2 if name in TWO_DMAS else 1)
        where[name] = (s, total[s])
    return where, total


LAYER_RING, LAYER_LANDED = ring_table(LAYER_CHUNKS, 0, [16] * SLOTS)
LAYER_LANDED = [n - 16 for n in LAYER_LANDED]
MID_RING, MID_LANDED = ring_table(MID_CHUNKS, len(LAYER_CHUNKS) % SLOTS, [16 + DEPTH * n for n in LAYER_LANDED])
PASS_RING, PASS_TOTAL = ring_table(PASS_CHUNKS, (len(LAYER_CHUNKS) + len(MID_CHUNKS)) % SLOTS, [0] * SLOTS)


def program(nc, a, consts, out):
    ctx = ExitStack()
    with ctx:
        def sb(name, shape, dt=F32):
            return ctx.enter_context(nc.sbuf_tensor(name, [P] + shape, dt))[:]

        def sem(name):
            return ctx.enter_context(nc.semaphore(name))

        def bc(ap, axis, n):
            ap = ap.unsqueeze(axis)
            shape = list(ap.shape)
            shape[axis] = n
            return ap.to_broadcast(shape)

        def shaped(ap, *shape):
            if len(shape) == 1:
                return ap
            names = "abcd"[:len(shape)]
            return ap.rearrange(f"p ({' '.join(names)}) -> p {' '.join(names)}", **dict(zip(names, shape)))

        ring = sb("ring", [SLOTS, SLOT])
        xT = sb("xT", [KT, SEQ])
        hT = sb("hT", [KT, SEQ])
        kc = sb("kc", [K_END])
        ones = sb("ones", [P])
        epsc = sb("epsc", [2])
        cact = sb("cact", [KT])
        cols = sb("cols", [DEPTH, 384])
        cols2 = sb("cols2", [W_END])
        rows = sb("rows", [DEPTH, R_END])
        biasm = sb("biasm", [DA_H, 384])
        rcos = sb("rcos", [T, 16])
        rsin = sb("rsin", [T, 16])
        cc = sb("cc", [V_END])
        rc = sb("rc", [R_END])
        lami = sb("lami", [2])
        mod = sb("mod", [48])
        amix = sb("amix", [KT])
        affn = sb("affn", [KT])
        gmh = sb("gmh", [KT])
        swh = sb("swh", [80])
        wqk = sb("wqk", [1])
        subw = sb("subw", [1])
        anega = sb("anega", [SM_H])
        lamv = sb("lamv", [8])
        lamp = sb("lamp", [128])
        rstd = sb("rstd", [SEQ])
        gates = sb("gates", [2, KT, SEQ])
        zb = sb("zb", [T, D])
        yT = sb("yT", [8, SEQ])
        ysT = sb("ysT", [8, SEQ])
        kv = shaped(ysT.rearrange("p a b -> p (a b)"), T, 1024)
        area = sb("area", [14336])

        def view(offset, *shape):
            return shaped(area[:, offset:offset + int(np.prod(shape))], *shape)

        S = view(0, 1024)
        PT = view(1024, 8, P)
        o = view(2048, T, 512)
        junk = view(3072, 1024)
        qk = view(4096, 2, T, 512)
        sqqk = view(0, 2, T, 512)
        va = view(6144, T, 512)
        qTa = view(7168, DA_H, SEQ)
        kTa = view(8192, DA_H, SEQ)
        kb = view(4096, T, ML_H, ML_QK)
        qTm = view(6144, ML_H, SEQ)
        kTm = view(8192, ML_H, SEQ)
        ml = view(10240, T, ML_W + SM_H)
        cT = view(11104, 3, SEQ)
        qb = view(11872, T, ML_H, ML_QK)
        sqq = shaped(gates[:, 1].rearrange("p k n -> p (k n)")[:, 0:1536], T, ML_H, ML_QK)
        sqk = shaped(yT[:, 0:4].rearrange("p k n -> p (k n)"), T, ML_H, ML_N)
        xb = view(0, 16, SEQ)
        xdt = view(0, T, D)
        xs = view(4096, T, D)
        bmt = view(6144, SM_G * SM_N)
        cbm = view(6656, SM_G, P)
        tria = view(7168, 8, P)
        E = view(8192, 8, P)
        stT = view(9216, D)
        xe = view(10240, SM_H, SM_D)
        y = view(11264, T, D)
        th = view(13312, 1024)
        sqy = view(7168, D)
        act = view(0, FT, SEQ)
        u4 = view(5632, 2, 4, SEQ)
        sl = view(7680, 2, 512)
        sqx = view(8704, KT, SEQ)
        *partial, product = [zb[:, i // 2, 512 * (i % 2):512 * (i % 2) + 512] for i in range(4)]
        xin = view(0, T, D)
        prow = view(2048, DEPTH, 3, P)
        prow2 = view(2816, P)
        crow = view(2944, P)
        early = gates[:, 0].rearrange("p k n -> p (k n)")
        dist, step = early[:, 0:384], early[:, 384:768]
        rel, drel = early[:, 768:896], early[:, 896:1024]
        ang, turns, posf = shaped(early[:, 1024:1056], T, 16), shaped(early[:, 1056:1088], T, 16), early[:, 1088:1344]
        posr = sb("posr", [SEQ], I32)
        posc = sb("posc", [T], I32)
        poscf = sb("poscf", [T])

        qa2 = view(4096, T, 512)
        ka2 = view(5120, T, P)
        kd2 = view(5376, T, 2, 2, D2)
        va2 = view(5888, T, P)
        qb2 = view(6144, T, 512)
        kb2 = view(7168, T, 512)
        vb2 = view(8192, T, 512)
        rt1, rt2, rr1 = (view(9216 + 512 * i, T, H2, 32) for i in range(3))
        sqa2 = view(0, T, 512)
        sqk2 = view(1024, T, P)
        qTa2 = view(10752, 4, SEQ)
        kTa2 = view(11776, 2, SEQ)
        qTb2 = view(12288, 4, SEQ)
        kTb2 = view(13312, 4, SEQ)
        sqo = view(9216, T, 512)
        o2 = [view(2048 + 1024 * i, T, 512) for i in range(2)]
        S2 = [zb[:, i, :] for i in range(2)]
        PT2 = [shaped(yT[:, 4 * i:4 * i + 4, :].rearrange("p h n -> p (h n)"), 8, P) for i in range(2)]
        late = ysT.rearrange("p h n -> p (h n)")
        rwt = shaped(late[:, 0:KT * 36], KT, 36)
        qn2, kn2 = late[:, 288:352], late[:, 352:416]
        rb2 = late[:, 416:452]
        h2t = view(0, T, D)
        xg = view(2048, KT, P)
        pm = view(3072, T, P)
        pmT = view(3328, SEQ)
        hs = view(3584, 2, 512)
        he = view(4608, 2, 512)
        heT = view(5632, 2, 4, P)
        ygs = view(6656, D)
        fin = view(10752, T, D)
        r = lambda at, *shape: view(7680 + at, *shape)
        lg, og, gv, gm = r(0, T, 36), r(72, T, GROUPS), r(80, T, GROUPS), r(88, T)
        ge, gp, em, ei = r(90, T, GROUPS), r(98, T), r(100, T, GROUPS, EPG), r(164, T, EPG)
        m1, m2, o1, o2nd, ev, vm = r(180, T), r(182, T), r(184, T, EPG), r(200, T, EPG), r(216, T, EPG), r(232, T)
        w1, w2, gate8, psl = r(234, T), r(236, T), r(240, T, EPG), r(256, T, GROUPS + 2)
        over, metaf, gsl, ssq = r(268, GROUPS), r(272, 8), r(280, EPG), r(288, T)
        meta = sb("meta", [8], I32)

        nmx = sb("nmx", [8])
        psums = sb("psums", [8])
        rps = sb("rps", [8])
        nlr = sb("nlr", [4])
        ss = sb("ss", [64])
        rs = sb("rs", [64])
        rsl = sb("rsl", [T, 4])
        sso = sb("sso", [T, 4])
        ssl = sb("ssl", [T, 4])
        krr = sb("krr", [T, 32])
        tmp1 = view(13408, T, ML_H, 16)
        tmp2 = view(13664, T, ML_H, 16)
        rot1 = view(13920, T, ML_H, 16)
        dt = sb("dt", [T, SM_H])
        dtn = sb("dtn", [T, SM_H])
        da = sb("da", [T, SM_H])
        csb = sb("csb", [T, SM_H])
        ecs = sb("ecs", [T, SM_H])

        acc = [ctx.enter_context(nc.psum_tensor(f"acc{b}", [P, 1024], F32))[:] for b in range(2)]
        aux = ctx.enter_context(nc.psum_tensor("aux", [P, 1024], F32))[:]
        aux2 = ctx.enter_context(nc.psum_tensor("aux2", [P, 512], F32))[:]
        pmod = ctx.enter_context(nc.psum_tensor("pmod", [P, 512], F32))[:]
        three_banks = [aux[:, 0:512], aux[:, 512:1024], aux2]
        ident = kc[:, K_ID:K_ID + P]
        tri = kc[:, K_TRI:K_TRI + P]

        landed = [sem(f"landed{s}") for s in range(SLOTS)]
        acc_full = [sem(f"acc_full{b}") for b in range(2)]
        acc_free = [sem(f"acc_free{b}") for b in range(2)]
        dn_done = sem("dn_done")
        part_ready, part_pool = sem("part_ready"), sem("part_pool")
        ada_done = sem("ada_done")
        x_in, small_in = sem("x_in"), sem("small_in")
        fill = sem("fill")
        pro_t, pro_e = sem("pro_t"), sem("pro_e")
        c_ready, rope_ang, rope_done = sem("c_ready"), sem("rope_ang"), sem("rope_done")
        x_sq, x_ss, x_rt, h_scaled, h_ready = (sem(n) for n in ("x_sq", "x_ss", "x_rt", "h_scaled", "h_ready"))
        x_new = sem("x_new")
        cur_ready, al_exp, lam_arg, lam_exp = (sem(n) for n in ("cur_ready", "al_exp", "lam_arg", "lam_exp"))
        qk_ss, qk_rt, qk_n = (sem(n) for n in ("qk_ss", "qk_rt", "qk_n"))
        qkT, qkT_out = sem("qkT"), sem("qkT_out")
        ml_rt, c_n, cT_t, cT_out = (sem(n) for n in ("ml_rt", "c_n", "cT_t", "cT_out"))
        dt_abs, dt_ln, dt_ready = (sem(n) for n in ("dt_abs", "dt_ln", "dt_ready"))
        s_full, s_max, p_exp, w_mix = (sem(n) for n in ("s_full", "s_max", "p_exp", "w_mix"))
        t_full, t_out, o_full, o_out = (sem(n) for n in ("t_full", "t_out", "o_full", "o_out"))
        oa_rt, oa_n, yaT_t, yaT_out = (sem(n) for n in ("oa_rt", "oa_n", "yaT_t", "yaT_out"))
        m_sq, m_ss, m_rt, m_n, mT_t, mT_out = (sem(n) for n in ("m_sq", "m_ss", "m_rt", "m_n", "mT_t", "mT_out"))
        ybT_t, ybT_out = sem("ybT_t"), sem("ybT_out")
        z_tanh, tap0, conv, c_tanh, xb_ready = (sem(n) for n in ("z_tanh", "tap0", "conv", "c_tanh", "xb_ready"))
        xsT_t, xs_out, cs_full, cs_out, ecs_out = (sem(n) for n in ("xsT_t", "xs_out", "cs_full", "cs_out", "ecs_out"))
        bm_t, bm_out, cb_full, cb_out = (sem(n) for n in ("bm_t", "bm_out", "cb_full", "cb_out"))
        tria_ready, r_full, seg_ready, seg_exp, m_ready, y_full, y_out = (
            sem(n) for n in ("tria_ready", "r_full", "seg_ready", "seg_exp", "m_ready", "y_full", "y_out"))
        st_full, st_out, yo_full, yo_out = (sem(n) for n in ("st_full", "st_out", "yo_full", "yo_out"))
        y_gated, y_rt, y_n, ysT_t, ysT_out = (sem(n) for n in ("y_gated", "y_rt", "y_n", "ysT_t", "ysT_out"))
        merged_b, merged = sem("merged_b"), sem("merged")
        u_tap, u_silu, act_ready = (sem(n) for n in ("u_tap", "u_silu", "act_ready"))

        late_in, a2_n, b2_n, t2, t2_out = (sem(n) for n in ("late_in", "a2_n", "b2_n", "t2", "t2_out"))
        a2_ss, a2_rt = sem("a2_ss"), sem("a2_rt")
        s2_full, s2_max, p2_exp, t3_full, t3_out, o2_full, o2_out = (
            sem(n) for n in ("s2_full", "s2_max", "p2_exp", "t3_full", "t3_out", "o2_full", "o2_out"))
        on_ss, on_n, oT_t, oT_out = (sem(n) for n in ("on_ss", "on_n", "oT_t", "oT_out"))
        h2_t, h2_out, lg_full, lg_sub, lg_exp, top_sub, top_exp = (
            sem(n) for n in ("h2_t", "h2_out", "lg_full", "lg_sub", "lg_exp", "top_sub", "top_exp"))
        og_ready, pos_full, routed = sem("og_ready"), sem("pos_full"), sem("routed")
        pm_ready, gx_full, gx_out, pt_full, pt_out = (sem(n) for n in ("pm_ready", "gx_full", "gx_out", "pt_full", "pt_out"))
        g_full, u_full, d_done, g_silu, he_ready, he_t, he_out = (
            sem(n) for n in ("g_full", "u_full", "d_done", "g_silu", "he_ready", "he_t", "he_out"))
        yg_out, sc_full, x_added = sem("yg_out"), sem("sc_full"), sem("x_added")
        f_t, f_out, stored = sem("f_t"), sem("f_out"), sem("stored")
        def by_row(name, dst):
            return dst, a[name].rearrange("l (k n) -> k l n", n=P)

        def spread(name, c0, c1):
            w = a[name]
            if len(w.shape) == 3:
                w = w.rearrange("l a b -> l (a b)")
            return rows[:, :, c0:c1], w.unsqueeze(0).to_broadcast([P, DEPTH, c1 - c0])

        fw = a["ffn_conv_w"].rearrange("l k (f n) -> (k f) l n", n=P)
        small_dmas = [
            (rel, a["rel_bias"].rearrange("b h -> (b h)").unsqueeze(0).to_broadcast([P, BUCKETS * DA_H])),
            (posr, a["positions"].to_broadcast([P, SEQ])),
            *[(posc[:, t:t + 1], a["positions"][:, P * t:P * t + P].rearrange("b p -> p b")) for t in range(T)],
            (prow[:, :, 0, :], fw[0:P]),
            (prow[0:4, :, 1, :], fw[P:P + 4]),
            by_row("ffn_conv_b", prow[V_FB - P:V_ADA - P, :, 1, :]),
            by_row("ada_b", prow[V_ADA - P:V_NM - P, :, 1, :]),
            by_row("norm_mix", prow[V_NM - P:V_NF - P, :, 1, :]),
            by_row("norm_ffn", prow[V_NF - P:V_SN - P, :, 1, :]),
            by_row("ssm_norm", prow[V_SN - P:V_QA - P, :, 1, :]),
            by_row("mla_q_a_norm", prow[V_QA - P:V_KVA - P, :, 1, :]),
            by_row("mla_kv_a_norm", prow[V_KVA - P:V_SUB - P, :, 1, :]),
            by_row("da_subln", prow[V_SUB - P:V_SUB + 1 - P, :, 1, :]),
            (prow[0:64, :, 2, :], a["ssm_conv_w"].rearrange("l k (f n) -> (k f) l n", n=P)),
            by_row("ssm_conv_b", prow[64:80, :, 2, :]),
            *[(prow[80 + i:81 + i, :, 2, DA_D * m:DA_D * m + DA_D], a[name].unsqueeze(0))
              for i, name in enumerate(("da_q_norm", "da_k_norm")) for m in range(2)],
            *[(prow2[w0:w1, :], (a[name] if len(a[name].shape) == 2 else a[name].unsqueeze(0)).rearrange("l (k n) -> (l k) n", n=P))
              for name, w0, w1 in (("norm1_g_2", W_N1, W_OA), ("out_norm_a_g_2", W_OA, W_OB), ("out_norm_b_g_2", W_OB, W_N2),
                                   ("norm2_g_2", W_N2, W_FN), ("final_norm_g_2", W_FN, W_END))],
            spread("mla_q_norm", R_MQ, R_MK),
            spread("mla_k_norm", R_MK, R_DTB),
            spread("ssm_dt_bias", R_DTB, R_AL),
            spread("ssm_a_log", R_AL, R_SD),
            spread("ssm_d", R_SD, R_LP),
            spread("da_lambda", R_LP, R_END),
        ]
        N_SMALL = len(small_dmas)
        shaped_kv = lambda ap: ap.rearrange("p t (h n) -> p t h n", h=ML_H)
        block = ctx.enter_context(nc.Block())

        def part_of(i):
            n = ADA_ORDER.index(i)
            return (part_pool, n + 1, ADA_POOL) if n < ADA_POOL else (part_ready, ADA_AHEAD + n + 1 - ADA_POOL, 12 - ADA_POOL)

        def release_of(name):
            if name.startswith("dn"):
                return dn_done, 6 + int(name[2:]) + 1, 6
            if name.startswith("ada"):
                return part_of(int(name[3:]))
            use = {"uqkv": "ukv1", "ba": "ba1", "bb": "bb1"}.get(name, name)
            b = LU.buf[use]
            return acc_full[b], LU.full[use] + dict(LAYER_USES)[use], LU.per_full[b]

        def layer_source(name, l, other):
            def rows_of(w, c0, c1, r0=0, r1=D):
                n = (r1 - r0) // P
                return w[bass.ds(l, 1), r0:r1, c0:c1].rearrange("l (k p) n -> p (l k) n", p=P), n * (c1 - c0), n
            w_in = a["w_in"]
            if name.startswith("ada"):
                i = int(name[3:])
                w = a["ada_w"][bass.ds(other if i < ADA_AHEAD else l, 1), :, 512 * i:512 * i + 512]
                return [(w.rearrange("l (k p) n -> p (l k) n", p=P), KT * 512, KT)]
            if name in ("q", "k", "v"):
                c = {"q": C_Q, "k": C_K, "v": C_V}[name]
                return [rows_of(w_in, c, c + 512)]
            if name == "uqkv":
                return [rows_of(a["mla_w_uq"], 0, ML_H * ML_QK, 0, Q_RANK), rows_of(a["mla_w_ukv"], 0, 1024, 0, KV_RANK)]
            if name[:2] in ("ga", "gb", "gc"):
                c = C_G + D * "abc".index(name[1]) + 512 * int(name[2])
                return [rows_of(w_in, c, c + 512)]
            if name[0] == "z":
                return [rows_of(w_in, C_Z + 512 * int(name[1]), C_Z + 512 * int(name[1]) + 512)]
            if name.startswith("xbc"):
                return [rows_of(w_in, C_XBC + 512 * int(name[3]), C_XBC + 512 * int(name[3]) + 512)]
            if name == "ba":
                return [rows_of(a["w_branch_a"], 0, D, 0, 512)]
            if name == "bb":
                return [rows_of(a["w_branch_b"], 0, D, 0, 512)]
            if name[:2] in ("bc", "wo"):
                w, i = a["w_branch_c" if name[0] == "b" else "w_out"], int(name[2])
                return [rows_of(w, 512 * i, 512 * i + 512)]
            if name[:2] == "dn":
                i = int(name[2:])
                return [rows_of(a["ffn_w_down"], 0, D, 512 * i, min(512 * i + 512, FFN))]
            raise ValueError(name)

        @block.sync
        def _(sp):
            sp.dma_start(xin, a["x"].rearrange("b (t p) n -> p (b t) n", p=P)).then_inc(x_in, 16)
            sp.dma_start(crow[0:KT, :], a["c"].rearrange("b (k n) -> (b k) n", k=KT)).then_inc(x_in, 16)
            sp.dma_start(kc, consts).then_inc(x_in, 16)
            for i in range(ADA_AHEAD):
                if i == 2:
                    for dst, src in small_dmas:
                        sp.dma_start(dst, src).then_inc(small_in, 16)
                sp.dma_start(shaped(ring[:, i, :], KT, 512),
                             a["ada_w"][0:1, :, 512 * i:512 * i + 512].rearrange("l (k p) n -> p (l k) n", p=P)).then_inc(landed[i], 16)
            with sp.Fori(0, DEPTH) as l:
                other = l * -1 + (DEPTH - 1)
                for i, name in enumerate(LAYER_CHUNKS):
                    s = i % SLOTS
                    signal, value, per = release_of(LAYER_CHUNKS[i - SLOTS])
                    if i >= SLOTS:
                        sp.wait_ge(signal, l * per + value)
                    elif signal is dn_done:
                        sp.wait_ge(dn_done, l * per + value - per)
                    else:
                        sp.wait_ge(part_ready, l * per + value - per)
                    if name == "ml":
                        dst = shaped(ring[:, s, 0:8 * (ML_W + SM_H)], 8, ML_W + SM_H)
                        w = a["w_in"][bass.ds(l, 1)].rearrange("l (k p) n -> p (l k) n", p=P)
                        sp.dma_start(dst[:, :, 0:ML_W], w[:, :, C_ML:C_ML + ML_W]).then_inc(landed[s], 16)
                        sp.dma_start(dst[:, :, ML_W:], w[:, :, C_DT:C_DT + SM_H]).then_inc(landed[s], 16)
                    elif name.startswith("up"):
                        n = int(name[2:])
                        w = a["ffn_w_up"][bass.ds(l, 1)].rearrange("l (k p) (h n) -> p (l k) h n", p=P, h=2)
                        dst = shaped(ring[:, s, :], KT, 2, 256)
                        sp.dma_start(dst[:, :, 0, :], w[:, :, 0, 256 * n:256 * n + 256]).then_inc(landed[s], 16)
                        sp.dma_start(dst[:, :, 1, :], w[:, :, 1, 256 * n:256 * n + 256]).then_inc(landed[s], 16)
                    else:
                        at = 0
                        for src, size, k in layer_source(name, l, other):
                            sp.dma_start(shaped(ring[:, s, at:at + size], k, size // k), src).then_inc(landed[s], 16)
                            at += size

            for i, name in enumerate(MID_CHUNKS):
                s = MID_RING[name][0]
                if i < SLOTS:
                    signal, value, per = release_of(LAYER_CHUNKS[i - SLOTS])
                    sp.wait_ge(signal, (DEPTH - 1) * per + value)
                else:
                    prev = MID_CHUNKS[i - SLOTS]
                    sp.wait_ge(acc_full[MU.buf[prev]], MU.full[prev] + 2)
                w, c0, c1 = {"m_qa": ("w_in_2", 0, 512), "m_kva": ("w_in_2", 512, 768), "m_qb": ("w_in_2", 768, 1280),
                             "m_kb": ("w_in_2", 1280, 1792), "m_vb": ("w_in_2", 1792, 2304),
                             "m_wo0": ("w_out_2", 0, 512), "m_wo1": ("w_out_2", 512, 1024)}[name]
                sp.dma_start(shaped(ring[:, s, 0:KT * (c1 - c0)], KT, c1 - c0),
                             a[w].rearrange("l (k p) n -> p (l k) n", p=P)[:, :, c0:c1]).then_inc(landed[s], 16)
            sp.wait_ge(routed, 1)
            passes = sp.value_load(meta[0:1, 5:6], min_val=GROUPS, max_val=GROUPS + 1)
            with sp.Fori(0, passes) as p:
                group = sp.value_load(meta[0:1, bass.ds(p, 1)], min_val=0, max_val=GROUPS - 1)
                for i, name in enumerate(PASS_CHUNKS):
                    s = PASS_RING[name][0]
                    kind, e = PASS_CHUNKS[i - SLOTS][2], int(PASS_CHUNKS[i - SLOTS][3:])
                    sp.wait_ge({"g": g_full, "u": u_full, "d": d_done}[kind], p * EPG + (EPG if i >= SLOTS else 0) + e + 1)
                    w = a[{"g": "w_gate_2", "u": "w_up_2", "d": "w_down_2"}[name[2]]]
                    src = w[0, bass.ds(group * EPG + int(name[3:]), 1)]
                    n = DE if name[2] != "d" else D
                    sp.dma_start(shaped(ring[:, s, :], SLOT // n, n),
                                 src.rearrange("e (k p) n -> p (e k) n", p=P)).then_inc(landed[s], 16)

        @block.tensor
        def _(pe):
            def transposes(ins_outs, signal):
                for src, dst in ins_outs:
                    n = src.shape[0]
                    last = pe.transpose(dst, src, ident[0:n, 0:n])
                last.then_inc(signal, 1)

            pe.wait_ge(x_in, 16 * 3)
            for t in range(T):
                if t:
                    pe.wait_ge(pro_e, t)
                transposes([(xin[:, t, P * k:P * k + P], aux[:, P * k:P * k + P]) for k in range(KT)], pro_t)
            transposes([(crow[0:KT, :], aux2[:, 0:KT])], pro_t)
            pe.wait_ge(small_in, 16 * N_SMALL)
            for l in range(DEPTH):
                for i, n in enumerate((P, V_SUB + 1 - P, V_END - 2 * P)):
                    transposes([(prow[0:n, l, i, :], acc[0][:, 384 * l + P * i:384 * l + P * i + n])], pro_t)
            transposes([(prow2[0:W_END, :], acc[1][:, 0:W_END])], pro_t)
            pe.wait_ge(fill, 1)

            def norm_sum(before):
                for k in range(KT):
                    if k % 4 == 0:
                        pe.wait_ge(x_sq, before + k // 4 + 1)
                    mm = pe.matmul(aux2[:, 0:SEQ], ones, sqx[:, k, :], start=(k == 0), stop=(k == KT - 1))
                mm.then_inc(x_ss, 1)

            def ada_sum(i, signal, value):
                pe.wait_ge(signal, value)
                part = partial[ADA_ORDER.index(i) % 3]
                for j in range(4):
                    mm = pe.matmul(pmod[:, 4 * i + j:4 * i + j + 1], part[:, P * j:P * j + P], ones[:, 0:1], start=True, stop=True)
                mm.then_inc(ada_done, 1)

            for i in range(ADA_AHEAD):
                ada_sum(i, part_ready, i + 1)
                if i % 2:
                    pe.drain().then_inc(dn_done, (5, 1)[i // 2])

            with pe.Fori(0, DEPTH) as l:
                def arrived(name):
                    s, value = LAYER_RING[name]
                    pe.wait_ge(landed[s], l * LAYER_LANDED[s] + value)
                    return ring[:, s, :]

                def open_acc(use):
                    b = LU.buf[use]
                    pe.wait_ge(acc_free[b], l * LU.per_turn[b] + LU.turn[use])

                def feature_piece(use, j, w, c0, x, fresh=None):
                    n = w.shape[1]
                    for k in range(n):
                        if fresh is not None:
                            pe.wait_ge(h_ready, fresh + k + 1)
                        mm = pe.matmul(acc[LU.buf[use]][:, SEQ * j:SEQ * j + SEQ], w[:, k, c0:c0 + P], x[:, k, :],
                                       start=(k == 0), stop=(k == n - 1))
                    mm.then_inc(acc_full[LU.buf[use]], 1)

                def token_piece(use, t, at, w, x, signal=True, fresh=None):
                    n, width = w.shape[1], w.shape[2]
                    for k in range(n):
                        if fresh is not None:
                            pe.wait_ge(h_ready, fresh + k + 1)
                        mm = pe.matmul(acc[LU.buf[use]][:, at:at + width], x[:, k, P * t:P * t + P], w[:, k, :],
                                       start=(k == 0), stop=(k == n - 1))
                    if signal:
                        mm.then_inc(acc_full[LU.buf[use]], 1)

                def ada(i):
                    signal, value, per = part_of(i)
                    ada_sum(i, signal, l * per + value)

                def token_chunk(name, width=512, fresh=None):
                    w = shaped(arrived(name)[:, 0:KT * width], KT, width)
                    open_acc(name)
                    for t in range(T):
                        token_piece(name, t, 512 * t, w, hT, fresh=fresh if t == 0 else None)

                def gate_pieces(name, first, last, fresh=None):
                    w = shaped(arrived(name), KT, 512)
                    if first == 0:
                        open_acc(name)
                    for j in range(first, last):
                        feature_piece(name, j, w, P * j, hT, fresh=fresh if j == 0 else None)

                norm_sum(4 * l)
                token_chunk("q", fresh=2 * KT * l)
                token_chunk("k")
                token_chunk("v")
                token_chunk("ml", ML_W + SM_H)
                ada(4)

                pe.wait_ge(qk_n, l + 1)
                for n in range(4):
                    i, h0 = n // 2, 2 * (n % 2)
                    if n == 3:
                        pe.wait_ge(qkT_out, 4 * l + 1)
                    transposes([(qk[:, i, t, P * (h0 + h):P * (h0 + h) + P], three_banks[n % 3][:, SEQ * h + P * t:SEQ * h + P * t + P])
                                for h in range(2) for t in range(T)], qkT)
                pe.wait_ge(c_n, l + 1)
                pe.wait_ge(qkT_out, 4 * l + 4)
                transposes([(ml[:, t, P * j:P * j + P], aux[:, SEQ * j + P * t:SEQ * j + P * t + P])
                            for j in range(3) for t in range(T)], cT_t)
                pe.wait_ge(cT_out, l + 1)
                w = arrived("uqkv")
                wq, wkv = shaped(w[:, 0:1536], 2, 768), shaped(w[:, 1536:2560], 1, 1024)
                for t in range(T):
                    open_acc(f"uq{t}")
                    token_piece(f"uq{t}", t, 0, wq[:, :, 0:512], cT, signal=False)
                    token_piece(f"uq{t}", t, 512, wq[:, :, 512:768], cT)
                for t in range(T):
                    open_acc(f"ukv{t}")
                    token_piece(f"ukv{t}", t, 0, wkv[:, :, 0:512], cT[:, 2:3, :], signal=False)
                    token_piece(f"ukv{t}", t, 512, wkv[:, :, 512:1024], cT[:, 2:3, :])
                ada(5)
                pe.wait_ge(dt_ready, l + 1)
                for t in range(T):
                    mm = pe.matmul(pmod[:, 48 + SM_H * t:48 + SM_H * (t + 1)], tri, da[:, t, :], start=True, stop=True)
                mm.then_inc(cs_full, 1)

                def da_unit(n):
                    return [(0, 0, 4, 1), (1, 0, 2, 2), (1, 2, 2, 2)][n]

                def ml_unit(n):
                    return [(0, 0, 8, 1), (1, 0, 4, 2), (1, 4, 4, 2)][n]

                def da_scores(n):
                    t, h0, nh, nk = da_unit(n)
                    for i in range(nh):
                        for m in range(2):
                            mm = pe.matmul(aux[:, 512 * m + P * nk * i:512 * m + P * nk * (i + 1)],
                                           qTa[64 * m:64 * m + 64, h0 + i, P * t:P * t + P],
                                           kTa[64 * m:64 * m + 64, h0 + i, 0:P * nk], start=True, stop=True)
                    mm.then_inc(s_full, 1)

                def ml_scores(n):
                    t, h0, nh, nk = ml_unit(n)
                    for i in range(nh):
                        mm = pe.matmul(aux[:, P * nk * i:P * nk * (i + 1)], qTm[0:ML_QK, h0 + i, P * t:P * t + P],
                                       kTm[0:ML_QK, h0 + i, 0:P * nk], start=True, stop=True)
                    mm.then_inc(s_full, 1)

                def prob_transposes(count):
                    transposes([(S[:, P * i:P * i + P], aux[:, P * i:P * i + P]) for i in range(count)], t_full)

                def values(n, unit, width, v):
                    t, h0, nh, nk = unit
                    pe.wait_ge(t_out, l * 6 + n + 1)
                    if n:
                        pe.wait_ge(o_out, l * 6 + n)
                    for i in range(nh):
                        for k in range(nk):
                            mm = pe.matmul(aux2[:, width * i:width * i + width], PT[:, i * nk + k, :], v(h0 + i, k),
                                           start=(k == 0), stop=(k == nk - 1))
                    mm.then_inc(o_full, 1)

                for n, filler in enumerate(("ga0", "ga1", "gb0")):
                    da_scores(n)
                    gate_pieces(filler, 0, 3)
                    pe.wait_ge(w_mix, l * 3 + n + 1)
                    prob_transposes(4)
                    gate_pieces(filler, 3, 4)
                    values(n, da_unit(n), 2 * DA_D, lambda h, k: va[:, k, 2 * DA_D * h:2 * DA_D * (h + 1)])
                    if n < 2:
                        ada((6, 7)[n])
                gate_pieces("gb1", 0, 4)
                ada(8)
                pe.wait_ge(oa_n, l + 1)
                transposes([(o[:, t, P * j:P * j + P], aux[:, SEQ * j + P * t:SEQ * j + P * t + P])
                            for j in range(4) for t in range(T)], yaT_t)
                pe.wait_ge(yaT_out, l + 1)

                pe.wait_ge(m_n, l + 1)
                for i in range(8):
                    if i >= 3:
                        pe.wait_ge(mT_out, 8 * l + i - 2)
                    src, t, h0 = (qb, kb)[i // 4], i // 2 % 2, 4 * (i % 2)
                    transposes([(src[:, t, h0 + h, :], three_banks[i % 3][0:ML_QK, P * h:P * h + P]) for h in range(4)], mT_t)
                pe.wait_ge(mT_out, 8 * l + 8)
                v_of = lambda h, k: kv[:, k, P * h + ML_N:P * h + P]
                for n in range(3):
                    ml_scores(n)
                    w = shaped(arrived(f"z{n}"), KT, 512) if n < 2 else shaped(arrived("ba"), 4, D)
                    for u in range(2):
                        if n < 2:
                            if u == 0:
                                open_acc(f"z{n}")
                            token_piece(f"z{n}", u, 512 * u, w, hT)
                        else:
                            open_acc(f"ba{u}")
                            for j in range(4):
                                feature_piece(f"ba{u}", j, w, 512 * u + P * j, yT[:, 0:4, :])
                        if u == 0:
                            pe.wait_ge(p_exp, l * 6 + 3 + n + 1)
                            prob_transposes(8)
                    values(3 + n, ml_unit(n), ML_V, v_of)

                gate_pieces("xbc0", 0, 4)
                pe.wait_ge(o_out, l * 6 + 6)
                transposes([(o[:, t, P * j:P * j + P], aux[:, SEQ * j + P * t:SEQ * j + P * t + P])
                            for j in range(4) for t in range(T)], ybT_t)
                gate_pieces("xbc1", 0, 4)
                gate_pieces("xbc2", 0, 4)
                pe.wait_ge(xb_ready, 4 * l + 2)
                pe.wait_ge(ybT_out, l + 1)

                def xs_transposes(t):
                    transposes([(xb[:, k, P * t:P * t + P], aux[:, P * k:P * k + P]) for k in range(KT)], xsT_t)

                xs_transposes(0)
                gate_pieces("xbc3", 0, 4)
                pe.wait_ge(xs_out, 2 * l + 1)
                xs_transposes(1)
                pe.wait_ge(xb_ready, 4 * l + 3)
                transposes([(xb[:, 8 + g, 0:P], aux2[:, P * g:P * g + P]) for g in range(SM_G)], bm_t)
                w = shaped(arrived("bb"), 4, D)
                open_acc("bb0")
                for j in range(4):
                    feature_piece("bb0", j, w, P * j, yT[:, 4:8, :])

                def cb(t):
                    for g in range(SM_G):
                        mm = pe.matmul(aux2[:, P * g:P * g + P], xb[:, 8 + g, P * t:P * t + P],
                                       xb[:, 12 + g, P * t:P * t + P], start=True, stop=True)
                    mm.then_inc(cb_full, 1)

                def decays(hc):
                    pe.wait_ge(tria_ready, 4 * l + hc + 1)
                    for i in range(2):
                        mm = pe.matmul(aux[:, 512 * i:512 * i + 512], ones,
                                       tria[:, 4 * i:4 * i + 4, :].rearrange("p h n -> p (h n)"), start=True, stop=True)
                    mm.then_inc(r_full, 1)

                def diagonal(hc):
                    t, h0 = hc // 2, 8 * (hc % 2)
                    pe.wait_ge(m_ready, 4 * l + hc + 1)
                    if hc == 0 or hc == 2:
                        pe.wait_ge(cb_out, 2 * l + t + 1)
                    else:
                        pe.wait_ge(y_out, 4 * l + hc)
                    for h in range(8):
                        mm = pe.matmul(aux2[:, SM_D * h:SM_D * h + SM_D], E[:, h, :],
                                       xdt[:, t, SM_D * (h0 + h):SM_D * (h0 + h + 1)], start=True, stop=True)
                    mm.then_inc(y_full, 1)

                pe.wait_ge(xb_ready, 4 * l + 4)
                pe.wait_ge(bm_out, l + 1)
                cb(0)
                pe.wait_ge(xs_out, 2 * l + 2)
                decays(0)
                open_acc("bb1")
                for j in range(4):
                    feature_piece("bb1", j, w, 512 + P * j, yT[:, 4:8, :])
                diagonal(0)
                decays(1)
                gate_pieces("gc0", 0, 2)
                diagonal(1)
                for g in range(SM_G):
                    mm = pe.matmul(aux[:, SEQ * g:SEQ * g + SEQ], bmt[:, P * g:P * g + P],
                                   xe[:, 4 * g:4 * g + 4, :].rearrange("p h d -> p (h d)"), start=True, stop=True)
                mm.then_inc(st_full, 1)
                pe.wait_ge(y_out, 4 * l + 2)
                cb(1)
                gate_pieces("gc0", 2, 4)
                pe.wait_ge(st_out, l + 1)
                decays(2)
                gate_pieces("gc1", 0, 2)
                diagonal(2)
                decays(3)
                gate_pieces("gc1", 2, 4)
                diagonal(3)
                for g in range(SM_G):
                    mm = pe.matmul(aux[:, SEQ * g:SEQ * g + SEQ], xb[:, 12 + g, P:2 * P], stT[:, SEQ * g:SEQ * g + SEQ],
                                   start=True, stop=True)
                mm.then_inc(yo_full, 1)
                pe.wait_ge(y_n, 2 * l + 1)
                pe.wait_ge(yo_out, l + 1)
                transposes([(y[:, 0, P * k:P * k + P], aux[:, P * k:P * k + P]) for k in range(KT)], ysT_t)
                pe.wait_ge(y_n, 2 * l + 2)
                pe.wait_ge(ysT_out, 3 * l + 1)
                for k0 in (0, 4):
                    transposes([(y[:, 1, P * k:P * k + P], aux[:, P * k:P * k + P]) for k in range(k0, k0 + 4)], ysT_t)
                pe.wait_ge(ysT_out, 3 * l + 3)
                for i in range(2):
                    w = shaped(arrived(f"bc{i}"), KT, 512)
                    open_acc(f"bc{i}")
                    for j in range(4):
                        feature_piece(f"bc{i}", j, w, P * j, ysT)
                ada(9)
                ada(10)
                pe.wait_ge(merged, l + 1)
                for i in range(2):
                    w = shaped(arrived(f"wo{i}"), KT, 512)
                    open_acc(f"wo{i}")
                    for j in range(4):
                        feature_piece(f"wo{i}", j, w, P * j, gates[:, 0])
                    if i == 0:
                        ada(11)

                norm_sum(4 * l + 2)
                for i in range(11):
                    gate_pieces(f"up{i}", 0, 4, fresh=2 * KT * l + KT if i == 0 else None)
                open_acc("dn0")
                pe.wait_ge(act_ready, 11 * l + 10)
                for i in range(6):
                    k0, k1 = 4 * i, min(4 * i + 4, FT)
                    w = shaped(arrived(f"dn{i}")[:, 0:D * (k1 - k0)], k1 - k0, D)
                    if i == 5:
                        pe.wait_ge(act_ready, 11 * l + 11)
                    for k in range(k0, k1):
                        for f in range(KT):
                            dst = (acc[LU.buf["dn0"]], aux)[f // 4][:, SEQ * (f % 4):SEQ * (f % 4) + SEQ]
                            mm = pe.matmul(dst, w[:, k - k0, P * f:P * f + P], act[:, k, :],
                                           start=(k == 0 and f % 2 == 0), stop=(k == FT - 1), skip_group_check=True)
                    mm.then_inc(dn_done, 1)
                    if i >= 4:
                        ada(i - 4)
                ada(2)
                ada(3)

            def mid_arrived(name):
                s, value = MID_RING[name]
                pe.wait_ge(landed[s], value)
                return ring[:, s, :]

            def mid_token_chunk(name, width):
                w = shaped(mid_arrived(name)[:, 0:KT * width], KT, width)
                b = MU.buf[name]
                pe.wait_ge(acc_free[b], MU.turn[name])
                for t in range(T):
                    for k in range(KT):
                        if name == MID_CHUNKS[0] and t == 0:
                            wait_tile(1, k)
                        mm = pe.matmul(acc[b][:, 512 * t:512 * t + width], hT[:, k, P * t:P * t + P], w[:, k, :],
                                       start=(k == 0), stop=(k == KT - 1))
                    mm.then_inc(acc_full[b], 1)

            def sum_squares(n):
                norm_sum(4 * DEPTH + 2 * (n - 1))

            def wait_tile(n, k):
                pe.wait_ge(h_ready, 2 * KT * DEPTH + KT * (n - 1) + k + 1)

            sum_squares(1)
            mid_token_chunk("m_qa", 512)
            mid_token_chunk("m_kva", 256)
            mid_token_chunk("m_qb", 512)
            mid_token_chunk("m_kb", 512)
            pe.wait_ge(a2_n, 1)
            transposes([(qa2[:, t, P * j:P * j + P], aux[:, SEQ * j + P * t:SEQ * j + P * t + P])
                        for j in range(4) for t in range(T)], t2)
            mid_token_chunk("m_vb", 512)
            pe.drain().then_inc(g_full, EPG)
            pe.drain().then_inc(u_full, EPG)
            pe.wait_ge(t2_out, 1)
            transposes([(kd2[:, t, g].rearrange("p a d -> p (a d)"), aux[:, SEQ * g + P * t:SEQ * g + P * t + P])
                        for g in range(2) for t in range(T)], t2)
            for i, src in enumerate((qb2, kb2)):
                pe.wait_ge(t2_out, 2 + i)
                pe.wait_ge(b2_n, 1)
                transposes([(src[:, t, P * j:P * j + P], aux[:, SEQ * j + P * t:SEQ * j + P * t + P])
                            for j in range(4) for t in range(T)], t2)
            pe.wait_ge(t2_out, 4)
            for b in range(2):
                pe.wait_ge(acc_free[b], MU.turn[("m_vb", "m_kb")[b]] + 1)

            def scores(u):
                t, first = u // 2 % 2, 2 * (u % 2)
                for i in range(2):
                    for m in range(2):
                        q, k = (qTa2, kTa2[64 * m:64 * m + 64, u % 2, :]) if u < 4 else (qTb2, kTb2[64 * m:64 * m + 64, first + i, :])
                        mm = pe.matmul(acc[u % 2][:, 512 * m + SEQ * i:512 * m + SEQ * i + SEQ],
                                       q[64 * m:64 * m + 64, first + i, P * t:P * t + P], k, start=True, stop=True)
                mm.then_inc(s2_full, 1)

            scores(0)
            for u in range(8):
                if u < 7:
                    if u >= 1:
                        pe.wait_ge(p2_exp, u)
                    scores(u + 1)
                pe.wait_ge(p2_exp, u + 1)
                if u:
                    pe.wait_ge(t3_out, 2 * u)
                for m in range(2):
                    transposes([(S2[u % 2][:, P * i:P * i + P], aux[:, P * i:P * i + P]) for i in range(4 * m, 4 * m + 4)], t3_full)
                if u:
                    pe.wait_ge(o2_out, u)
                for m in range(2):
                    pe.wait_ge(t3_out, 2 * u + m + 1)
                    for i in range(2):
                        head = 4 * (u % 2) + 2 * i + m
                        for k in range(T):
                            v = va2[:, k, D2 * (head // 4):D2 * (head // 4 + 1)] if u < 4 else vb2[:, k, D2 * head:D2 * head + D2]
                            mm = pe.matmul(aux2[:, D2 * (2 * i + m):D2 * (2 * i + m + 1)], PT2[u % 2][:, 2 * (2 * m + i) + k, :], v,
                                           start=(k == 0), stop=(k == T - 1))
                mm.then_inc(o2_full, 1)
                if u == 4 or u == 7:
                    n = (u - 4) // 3
                    pe.wait_ge(on_n, n + 1)
                    transposes([(o2[n][:, t, P * j:P * j + P], aux[:, SEQ * j + P * t:SEQ * j + P * t + P])
                                for j in range(4) for t in range(T)], oT_t)
                    pe.wait_ge(oT_out, n + 1)
            for i in range(2):
                name = f"m_wo{i}"
                w, b = shaped(mid_arrived(name), KT, 512), MU.buf[name]
                for j in range(4):
                    for k in range(KT):
                        mm = pe.matmul(acc[b][:, SEQ * j:SEQ * j + SEQ], w[:, k, P * j:P * j + P], hT[:, k, :],
                                       start=(k == 0), stop=(k == KT - 1))
                    mm.then_inc(acc_full[b], 1)
            pe.drain().then_inc(d_done, EPG)

            sum_squares(2)
            pe.wait_ge(late_in, 16 * 6)
            for t in range(T):
                for k in range(KT):
                    if t == 0:
                        wait_tile(2, k)
                    mm = pe.matmul(pmod[:, 128 + 36 * t:128 + 36 * (t + 1)], hT[:, k, P * t:P * t + P], rwt[:, k, :],
                                   start=(k == 0), stop=(k == KT - 1))
            mm.then_inc(lg_full, 1)
            for t in range(T):
                if t:
                    pe.wait_ge(h2_out, t)
                transposes([(hT[:, k, P * t:P * t + P], aux[:, P * k:P * k + P]) for k in range(KT)], h2_t)
            pe.wait_ge(og_ready, 1)
            pe.matmul(pmod[:, 256:260], tri, og[:, 0, :], start=True, stop=True)
            pe.matmul(pmod[:, 260:264], tri, og[:, 1, :], start=True, stop=False)
            pe.matmul(pmod[:, 260:264], ones, og[:, 0, :], start=False, stop=True)
            pe.matmul(pmod[:, 264:268], ones, og[:, 0, :], start=True, stop=False)
            pe.matmul(pmod[:, 264:268], ones, og[:, 1, :], start=False, stop=True).then_inc(pos_full, 1)
            pe.wait_ge(h2_out, T)
            pe.wait_ge(routed, 1)
            passes = pe.value_load(meta[0:1, 5:6], min_val=GROUPS, max_val=GROUPS + 1)
            with pe.Fori(0, passes) as p:
                def pass_arrived(name):
                    s, value = PASS_RING[name]
                    pe.wait_ge(landed[s], p * PASS_TOTAL[s] + value + MID_LANDED[s])
                    return ring[:, s, :]

                pe.wait_ge(pm_ready, p + 1)
                for k in range(KT):
                    for t in range(T):
                        mm = pe.matmul(acc[0][:, P * k:P * k + P], h2t[:, t, P * k:P * k + P], pm[:, t, :],
                                       start=(t == 0), stop=(t == T - 1))
                mm.then_inc(gx_full, 1)
                for t in range(T):
                    pe.transpose(aux2[:, P * t:P * t + P], pm[:, t, :], ident)
                for t in range(T):
                    mm = pe.matmul(pmod[:, 300:300 + EPG], pm[:, t, :], gate8[:, t, :], start=(t == 0), stop=(t == T - 1))
                mm.then_inc(pt_full, 1)
                pe.wait_ge(gx_out, p + 1)

                def hidden(e, i):
                    kind, signal = (("g", g_full), ("u", u_full))[i]
                    w = shaped(pass_arrived(f"e_{kind}{e}"), KT, DE)
                    for k in range(KT):
                        mm = pe.matmul(acc[e % 2][:, DE * i:DE * i + DE], xg[:, k, :], w[:, k, :],
                                       start=(k == 0), stop=(k == KT - 1))
                    mm.then_inc(signal, 1)

                def turn(e):
                    pe.wait_ge(he_ready, p * EPG + e + 1)
                    if e:
                        pe.wait_ge(he_out, p * EPG + e)
                    else:
                        pe.wait_ge(pt_out, p + 1)
                    transposes([(he[:, e % 2, P * j:P * j + P], aux2[:, P * j:P * j + P]) for j in range(4)], he_t)

                def down(e):
                    pe.wait_ge(he_out, p * EPG + e + 1)
                    w = shaped(pass_arrived(f"e_d{e}"), 4, D)
                    for n in range(2):
                        for k in range(4):
                            mm = pe.matmul(aux[:, 512 * n:512 * n + 512], heT[:, e % 2, k, :], w[:, k, 512 * n:512 * n + 512],
                                           start=(e == 0 and k == 0), stop=(e == EPG - 1 and k == 3))
                    mm.then_inc(d_done, 1)

                hidden(0, 0)
                hidden(0, 1)
                pe.wait_ge(x_added, p + 1)
                for e in range(1, EPG):
                    hidden(e, 0)
                    turn(e - 1)
                    hidden(e, 1)
                    down(e - 1)
                turn(EPG - 1)
                down(EPG - 1)
                pe.wait_ge(yg_out, p + 1)
                for k in range(KT):
                    mm = pe.matmul((acc[1], aux)[k // 4][:, SEQ * (k % 4):SEQ * (k % 4) + SEQ], ygs[:, P * k:P * k + P], pmT,
                                   start=True, stop=True)
                mm.then_inc(sc_full, 1)
            sum_squares(3)
            wait_tile(3, KT - 1)
            for t in range(T):
                if t:
                    pe.wait_ge(f_out, t)
                transposes([(hT[:, k, P * t:P * t + P], aux[:, P * k:P * k + P]) for k in range(KT)], f_t)

        @block.scalar
        def _(act_):
            act = act_
            copy = lambda dst, src: act.activation(dst, src, ACT.Copy)

            for t in range(T):
                act.wait_ge(pro_t, t + 1)
                copy(xT[:, :, P * t:P * t + P], shaped(aux, KT, P)).then_inc(pro_e, 1)
            act.drain().then_inc(x_new, 2)

            def squares(before):
                for i in range(2):
                    act.wait_ge(x_new, before + i + 1)
                    act.activation(sqx[:, 4 * i:4 * i + 4, :], xT[:, 4 * i:4 * i + 4, :], ACT.Square).then_inc(x_sq, 1)

            act.wait_ge(fill, 1)
            act.wait_ge(pro_t, 3)
            act.activation(cact, aux2[:, 0:KT], ACT.Silu).then_inc(c_ready, 1)
            act.wait_ge(pro_t, 3 + 3 * DEPTH)
            for l in range(DEPTH):
                copy(cols[:, l, 0:V_SUB + 1], acc[0][:, 384 * l:384 * l + V_SUB + 1])
                last = copy(cols[:, l, V_SW:V_END], acc[0][:, 384 * l + V_SW:384 * l + V_END])
            last.then_inc(acc_free[0], 1)
            act.wait_ge(pro_t, 4 + 3 * DEPTH)
            copy(cols2, acc[1][:, 0:W_END]).then_inc(acc_free[1], 1)
            with act.Fori(0, DEPTH) as l:
                def full(use, piece):
                    b = LU.buf[use]
                    act.wait_ge(acc_full[b], l * LU.per_full[b] + LU.full[use] + piece + 1)
                    return acc[b]

                def freed(use):
                    b = LU.buf[use]
                    act.wait_ge(acc_free[b], l * LU.per_turn[b] + LU.turn[use] + 1)

                def free(use):
                    return acc_free[LU.buf[use]], 1

                def gate(name, first, last):
                    n, c = {"a": 0, "b": 1, "c": 1}[name[1]], int(name[2])
                    for j in range(first, last):
                        src = full(name, j | 1)
                        i = act.activation(gates[:, n, 4 * c + j, :], src[:, SEQ * j:SEQ * j + SEQ], ACT.Tanh, scale=0.5)
                        if j == 3:
                            i.then_inc(*free(name))

                def exps(n, blocks):
                    act.wait_ge(s_max, l * 6 + n + 1)
                    for i, s in enumerate(blocks):
                        last = act.activation(s, s, ACT.Exp, bias=nmx[:, i:i + 1], accum_out=psums[:, i:i + 1])
                    last.then_inc(p_exp, 1)

                def take_transposes(n, count):
                    act.wait_ge(t_full, l * 6 + n + 1)
                    copy(PT[:, 0:count, :], shaped(aux[:, 0:P * count], count, P)).then_inc(t_out, 1)

                def root(dst, src, n, signal):
                    act.activation(dst, src, ACT.Sqrt, bias=epsc[:, 0:1], scale=1.0 / n).then_inc(*signal)

                squares(4 * l)
                act.wait_ge(cur_ready, l + 1)
                act.activation(anega, rc[:, R_AL:R_AL + SM_H], ACT.Exp).then_inc(al_exp, 1)
                act.wait_ge(lam_arg, l + 1)
                act.activation(lamv[:, 4:6], lamv[:, 0:2], ACT.Exp).then_inc(lam_exp, 1)
                def norm_root_shift(n, shift):
                    act.wait_ge(x_ss, 2 * l + n + 1)
                    root(rstd, aux2[:, 0:SEQ], D, (x_rt, 1))
                    for k in range(KT):
                        act.wait_ge(h_scaled, 2 * KT * l + KT * n + k + 1)
                        act.activation(hT[:, k, :], hT[:, k, :], ACT.Identity, bias=shift[:, k:k + 1]).then_inc(h_ready, 1)

                norm_root_shift(0, mod[:, 0:8])

                for i, name in enumerate(("q", "k")):
                    for t in range(T):
                        src = full(name, t)[:, 512 * t:512 * t + 512]
                        copy(qk[:, i, t, :], src)
                        last = act.activation(sqqk[:, i, t, :], src, ACT.Square)
                    last.then_inc(*free(name))
                for t in range(T):
                    last = copy(va[:, t, :], full("v", t)[:, 512 * t:512 * t + 512])
                last.then_inc(*free("v"))
                act.wait_ge(qk_ss, l + 1)
                root(rs[:, 0:32], ss[:, 0:32], DA_D, (qk_rt, 1))
                for t in range(T):
                    src = full("ml", t)[:, 512 * t:512 * t + ML_W + SM_H]
                    copy(ml[:, t, :], src)
                    for i, (c0, c1) in enumerate(((0, Q_RANK), (Q_RANK, Q_RANK + KV_RANK), (Q_RANK + KV_RANK, ML_W))):
                        last = act.activation(junk[:, ML_W * t + c0:ML_W * t + c1], src[:, c0:c1], ACT.Square, accum_out=ssl[:, t, i:i + 1])
                last.then_inc(*free("ml"))
                with act.If(l < 1):
                    act.wait_ge(rope_ang, 1)
                    act.activation(rsin, ang, ACT.Sin)
                    act.activation(rcos, turns, ACT.Sin).then_inc(rope_done, 1)
                act.drain()
                act.activation(rsl[:, :, 0], ssl[:, :, 0], ACT.Sqrt, bias=epsc[:, 0:1], scale=1.0 / Q_RANK)
                root(rsl[:, :, 1], ssl[:, :, 1], KV_RANK, (ml_rt, 1))
                for n in range(4):
                    act.wait_ge(qkT, 4 * l + n + 1)
                    dst = (qTa, kTa)[n // 2][:, 2 * (n % 2):2 * (n % 2) + 2, :].rearrange("p h n -> p (h n)")
                    i = act.activation(dst, three_banks[n % 3], ACT.Copy, scale=wqk) if n < 2 else copy(dst, three_banks[n % 3])
                    i.then_inc(qkT_out, 1)
                act.wait_ge(dt_abs, l + 1)
                act.activation(dt, dt, ACT.Exp)
                act.wait_ge(cT_t, l + 1)
                for j, c in enumerate((V_QA, V_QA + 1, V_KVA)):
                    last = act.activation(cT[:, j, :], aux[:, SEQ * j:SEQ * j + SEQ], ACT.Copy, scale=cc[:, c:c + 1])
                last.then_inc(cT_out, 1)
                act.drain()
                act.activation(dt, dt, ACT.Ln, bias=epsc[:, 1:2]).then_inc(dt_ln, 1)
                for t in range(T):
                    copy(qb[:, t].rearrange("p h n -> p (h n)"), full(f"uq{t}", 0)[:, 0:768]).then_inc(*free(f"uq{t}"))
                for t in range(T):
                    copy(kv[:, t, :], full(f"ukv{t}", 0)).then_inc(*free(f"ukv{t}"))
                act.drain()
                act.activation(sqq, qb, ACT.Square)
                act.activation(sqk, shaped_kv(kv)[:, :, :, 0:ML_N], ACT.Square).then_inc(m_sq, 1)
                act.wait_ge(cs_out, l + 1)
                act.activation(ecs, csb, ACT.Exp).then_inc(ecs_out, 1)
                act.wait_ge(m_ss, l + 1)
                root(rs[:, 0:32], ss[:, 0:32], ML_QK, (m_rt, 1))

                for n, filler in enumerate(("ga0", "ga1", "gb0")):
                    t, h0, nh, nk = [(0, 0, 4, 1), (1, 0, 2, 2), (1, 2, 2, 2)][n]
                    K = P * nk
                    exps(n, [S[:, 512 * m + K * i:512 * m + K * (i + 1)] for m in range(2) for i in range(nh)])
                    gate(filler, 0, 2)
                    take_transposes(n, 4)
                    gate(filler, 2, 4)
                    act.wait_ge(o_full, l * 6 + n + 1)
                    for i in range(nh):
                        act.activation(junk[:, 512 * (n % 2) + P * i:512 * (n % 2) + P * (i + 1)], aux2[:, P * i:P * i + P], ACT.Square, accum_out=sso[:, t, h0 + i:h0 + i + 1])
                    copy(o[:, t, P * h0:P * (h0 + nh)], aux2[:, 0:P * nh]).then_inc(o_out, 1)
                act.drain()
                root(sso, sso, 2 * DA_D, (oa_rt, 1))
                gate("gb1", 0, 4)
                act.wait_ge(yaT_t, l + 1)
                act.activation(yT[:, 0:4, :].rearrange("p h n -> p (h n)"), aux, ACT.Copy, scale=subw).then_inc(yaT_out, 1)

                for i in range(8):
                    act.wait_ge(mT_t, 8 * l + i + 1)
                    dst, t, h0 = (qTm, kTm)[i // 4], i // 2 % 2, 4 * (i % 2)
                    copy(dst[0:ML_QK, h0:h0 + 4, P * t:P * t + P], shaped(three_banks[i % 3], 4, P)[0:ML_QK]).then_inc(mT_out, 1)
                for n in range(3):
                    t, h0, nh, nk = [(0, 0, 8, 1), (1, 0, 4, 2), (1, 4, 4, 2)][n]
                    exps(3 + n, [S[:, P * nk * i:P * nk * (i + 1)] for i in range(nh)])
                    for u in range(T):
                        if n < 2:
                            src = full(f"z{n}", u)[:, 512 * u:512 * u + 512]
                            act.activation(zb[:, u, 512 * n:512 * n + 512], src, ACT.Tanh, scale=0.5).then_inc(z_tanh, 1)
                        if u == 0:
                            take_transposes(3 + n, 8)

                def conv_silu(c):
                    for j in range(4):
                        f = 4 * c + j
                        act.activation(xb[:, f, :], full(f"xbc{c}", j | 1)[:, SEQ * j:SEQ * j + SEQ], ACT.Identity,
                                       scale=swh[:, 48 + f:49 + f], bias=swh[:, 64 + f:65 + f]).then_inc(tap0, 1)
                    freed(f"xbc{c}")
                    act.activation(th, xb[:, 4 * c:4 * c + 4, :].rearrange("p h n -> p (h n)"), ACT.Tanh).then_inc(c_tanh, 1)

                def take_xs(t):
                    act.wait_ge(xsT_t, 2 * l + t + 1)
                    copy(xs[:, t, :], aux).then_inc(xs_out, 1)

                conv_silu(0)
                act.wait_ge(ybT_t, l + 1)
                copy(yT[:, 4:8, :].rearrange("p h n -> p (h n)"), aux).then_inc(ybT_out, 1)
                conv_silu(1)
                conv_silu(2)
                take_xs(0)
                conv_silu(3)
                take_xs(1)
                act.wait_ge(bm_t, l + 1)
                copy(bmt, aux2).then_inc(bm_out, 1)

                def seg_exps(hc):
                    act.wait_ge(seg_ready, 4 * l + hc + 1)
                    act.activation(E, E, ACT.Exp).then_inc(seg_exp, 1)

                def squares_y(t):
                    act.wait_ge(y_gated, 2 * l + t + 1)
                    for g in range(SM_G):
                        act.activation((th, sqy)[t][:, 256 * g:256 * g + 256], y[:, t, 256 * g:256 * g + 256], ACT.Square,
                                       accum_out=ss[:, SM_G * t + g:SM_G * t + g + 1])
                    act.drain()

                def root_y(t):
                    root(rs[:, SM_G * t:SM_G * t + SM_G], ss[:, SM_G * t:SM_G * t + SM_G], D // SM_G, (y_rt, 1))

                def take_ysT(turn, k0, k1):
                    t = turn // 2
                    act.wait_ge(ysT_t, 3 * l + turn)
                    for k in range(k0, k1):
                        last = act.activation(ysT[:, k, P * t:P * t + P], aux[:, P * k:P * k + P], ACT.Copy, scale=cc[:, V_SN + k:V_SN + k + 1])
                    last.then_inc(ysT_out, 1)

                seg_exps(0)
                seg_exps(1)
                act.wait_ge(merged_b, l + 1)
                gate("gc0", 0, 2)
                act.wait_ge(st_full, l + 1)
                copy(stT, aux).then_inc(st_out, 1)
                gate("gc0", 2, 4)
                seg_exps(2)
                gate("gc1", 0, 2)
                squares_y(0)
                seg_exps(3)
                gate("gc1", 2, 4)
                root_y(0)
                take_ysT(1, 0, KT)
                squares_y(1)
                root_y(1)
                take_ysT(3, 4, KT)

                squares(4 * l + 2)
                norm_root_shift(1, mod[:, 24:32])
                for i in range(11):
                    for j in range(4):
                        f = (0, FT)[j // 2] + 2 * i + j % 2
                        act.activation(u4[:, i % 2, j, :], full(f"up{i}", j | 1)[:, SEQ * j:SEQ * j + SEQ], ACT.Identity,
                                       scale=cc[:, V_FW + 4 * FT + f:V_FW + 4 * FT + f + 1],
                                       bias=cc[:, V_FB + f:V_FB + f + 1]).then_inc(u_tap, 1)
                    freed(f"up{i}")
                    act.activation(sl[:, i % 2, :], u4[:, i % 2, 0:2, :].rearrange("p h n -> p (h n)"), ACT.Silu).then_inc(u_silu, 1)

            def square_x(n):
                squares(4 * DEPTH + 2 * (n - 1))

            def root_x(n):
                act.wait_ge(x_ss, 2 * DEPTH + n)
                root(rstd, aux2[:, 0:SEQ], D, (x_rt, 1))

            def mid_full(name, piece):
                act.wait_ge(acc_full[MU.buf[name]], MU.full[name] + piece + 1)
                return acc[MU.buf[name]]

            square_x(1)
            act.dma_start(rwt[:, :, 0:GROUPS], a["router_group_w_2"].rearrange("l (k p) n -> p (l k) n", p=P)).then_inc(late_in, 16)
            act.dma_start(rwt[:, :, GROUPS:], a["router_expert_w_2"].rearrange("l (k p) n -> p (l k) n", p=P)).then_inc(late_in, 16)
            for dst, name in ((qn2, "q_norm_g_2"), (kn2, "k_norm_g_2"), (rb2[:, 0:GROUPS], "router_group_b_2"),
                              (rb2[:, GROUPS:], "router_expert_b_2")):
                act.dma_start(dst, a[name].to_broadcast([P, dst.shape[1]])).then_inc(late_in, 16)
            root_x(1)
            for t in range(T):
                src = mid_full("m_qa", t)[:, 512 * t:512 * t + 512]
                copy(qa2[:, t, :], src)
                last = act.activation(sqa2[:, t, :], src, ACT.Square)
            last.then_inc(acc_free[MU.buf["m_qa"]], 1)
            for t in range(T):
                src = mid_full("m_kva", t)[:, 512 * t:512 * t + 256]
                copy(ka2[:, t, :], src[:, 0:P])
                act.activation(sqk2[:, t, :], src[:, 0:P], ACT.Square)
                last = copy(va2[:, t, :], src[:, P:2 * P])
            last.then_inc(acc_free[MU.buf["m_kva"]], 1)
            act.wait_ge(a2_ss, 1)
            root(rs[:, 0:20], ss[:, 0:20], D2, (a2_rt, 1))
            for name, dst in (("m_qb", qb2), ("m_kb", kb2)):
                for t in range(T):
                    last = act.activation(dst[:, t, :], mid_full(name, t)[:, 512 * t:512 * t + 512], ACT.Copy,
                                          scale=D2 ** -0.5 if name == "m_qb" else 1.0)
                last.then_inc(acc_free[MU.buf[name]], 1)
            act.wait_ge(t2, 1)
            copy(qTa2.rearrange("p h n -> p (h n)"), aux).then_inc(t2_out, 1)
            for t in range(T):
                last = copy(vb2[:, t, :], mid_full("m_vb", t)[:, 512 * t:512 * t + 512])
            last.then_inc(acc_free[MU.buf["m_vb"]], 1)
            for i, dst in enumerate((kTa2, qTb2, kTb2)):
                act.wait_ge(t2, 2 + i)
                dst = dst.rearrange("p h n -> p (h n)")
                copy(dst, aux[:, 0:dst.shape[1]]).then_inc(t2_out, 1)
            for u in range(8):
                act.wait_ge(s2_max, u + 1)
                for i in range(4):
                    s = S2[u % 2][:, SEQ * i:SEQ * i + SEQ]
                    last = act.activation(s, acc[u % 2][:, SEQ * i:SEQ * i + SEQ] if u < 4 else s, ACT.Exp,
                                          bias=nmx[:, 4 * (u % 2) + i:4 * (u % 2) + i + 1], accum_out=psums[:, 4 * (u % 2) + i:4 * (u % 2) + i + 1])
                last.then_inc(p2_exp, 1)
                for m in range(2):
                    act.wait_ge(t3_full, 2 * u + m + 1)
                    copy(PT2[u % 2][:, 4 * m:4 * m + 4, :], shaped(aux[:, 512 * m:512 * m + 512], 4, P)).then_inc(t3_out, 1)
                if u == 3 or u == 7:
                    n = u // 4
                    act.wait_ge(on_ss, 2 * n + 1)
                    for t in range(T):
                        act.activation(sqo[:, t, :], o2[n][:, t, :], ACT.Square, accum_out=ssq[:, t:t + 1])
                    act.drain()
                    root(ssq, ssq, 512, (on_ss, 1))
            square_x(2)
            root_x(2)
            for t in range(T):
                act.wait_ge(h2_t, t + 1)
                copy(h2t[:, t, :], aux).then_inc(h2_out, 1)
            act.wait_ge(lg_sub, 1)
            act.activation(ge, ge, ACT.Exp).then_inc(lg_exp, 1)
            act.wait_ge(top_sub, 1)
            act.activation(w2, m2, ACT.Exp).then_inc(top_exp, 1)
            act.wait_ge(routed, 1)
            passes = act.value_load(meta[0:1, 5:6], min_val=GROUPS, max_val=GROUPS + 1)
            with act.Fori(0, passes) as p:
                act.wait_ge(gx_full, p + 1)
                copy(xg, shaped(acc[0], KT, P)).then_inc(gx_out, 1)

                def turn_back(e):
                    act.wait_ge(he_t, p * EPG + e + 1)
                    copy(heT[:, e % 2], shaped(aux2, 4, P)).then_inc(he_out, 1)

                for e in range(EPG):
                    act.wait_ge(g_full, p * EPG + EPG + e + 1)
                    act.activation(hs[:, e % 2, :], acc[e % 2][:, 0:DE], ACT.Silu).then_inc(g_silu, 1)
                    if e:
                        turn_back(e - 1)
                turn_back(EPG - 1)
                act.wait_ge(d_done, p * EPG + 2 * EPG)
                copy(ygs, aux).then_inc(yg_out, 1)
            square_x(3)
            root_x(3)
            for t in range(T):
                act.wait_ge(f_t, t + 1)
                copy(fin[:, t, :], aux).then_inc(f_out, 1)
                act.wait_ge(f_out, t + 1)
                act.dma_start(out[0, P * t:P * t + P, :], fin[:, t, :]).then_inc(stored, 16)
            act.wait_ge(stored, 16 * T)

        @block.gpsimd
        def _(pool):
            pool.memset(ones, 1.0)
            pool.memset(epsc[:, 0:1], EPS)
            pool.memset(epsc[:, 1:2], 1.0).then_inc(fill, 1)

            pool.wait_ge(c_ready, 1)
            with pool.Fori(0, DEPTH) as l:
                for n, i in enumerate(ADA_ORDER[:ADA_POOL]):
                    slot, value = LAYER_RING[f"ada{i}"]
                    pool.wait_ge(landed[slot], l * LAYER_LANDED[slot] + value)
                    pool.wait_ge(ada_done, l * 12 + ADA_AHEAD + n - 2)
                    w, part = shaped(ring[:, slot, :], KT, 512), partial[n % 3]
                    times = lambda dst, k: pool.tensor_tensor(dst, w[:, k, :], cact[:, k:k + 1].to_broadcast([P, 512]), ALU.mult)
                    times(part, 0)
                    for k in range(1, KT):
                        times(product, k)
                        pool.drain()
                        last = pool.tensor_tensor(part, part, product, ALU.add)
                        if k < KT - 1:
                            pool.drain()
                    last.then_inc(part_pool, 1)
                    pool.drain()

        @block.vector
        def _(dve):
            D_ = dve.drain
            tt, ts, stt = dve.tensor_tensor, dve.tensor_scalar, dve.scalar_tensor_tensor

            def positions_and_angles():
                dve.tensor_copy(posf, posr)
                dve.tensor_copy(poscf, posc)
                tt(drel[:, DA_H:], rel[:, DA_H:], rel[:, 0:(BUCKETS - 1) * DA_H], ALU.subtract)
                for h in range(DA_H):
                    ts(biasm[:, h, :], kc[:, K_CM:K_CM + 384], rel[:, h:h + 1], None, ALU.add)
                D_()
                ts(dist[:, 0:P], posf[:, 0:P], -1.0, poscf[:, 0:1], ALU.mult, ALU.add)
                ts(dist[:, P:3 * P], posf, -1.0, poscf[:, 1:2], ALU.mult, ALU.add)
                for t in range(T):
                    ts(ang[:, t, :], kc[:, K_INV:K_INV + 16], poscf[:, t:t + 1], None, ALU.mult)
                D_()
                ROUND = 12582912.0
                ts(turns, ang, float(1 / (2 * np.pi)), ROUND, ALU.mult, ALU.add)
                D_()
                ts(turns, turns, ROUND, None, ALU.subtract)
                D_()
                two_pi, parts = 2 * np.pi, []
                for _ in range(2):
                    bits = np.array([two_pi], np.float32).view(np.uint32) & np.uint32(0xFFFFE000)
                    parts.append(float(bits.view(np.float32)[0]))
                    two_pi -= parts[-1]
                for part in (*parts, float(np.float32(two_pi))):
                    stt(ang, turns, -part, ang, ALU.mult, ALU.add)
                    D_()
                half = 3.1415925
                ts(turns, ang, float(np.pi / 2), None, ALU.add)
                D_()
                ts(step[:, 0:32], turns.rearrange("p a b -> p (a b)"), half, -float(2 * np.pi), ALU.is_gt, ALU.mult)
                ts(ang, ang, half, -half, ALU.min, ALU.max)
                D_()
                tt(turns, turns, shaped(step[:, 0:32], T, 16), ALU.add)
                D_()
                ts(turns, turns, half, -half, ALU.min, ALU.max).then_inc(rope_ang, 1)
                D_()

            def bias_steps(first, last):
                with dve.Fori(first, last) as b:
                    ts(step, dist, kc[:, bass.ds(b + K_THR, 1)], None, ALU.is_ge)
                    D_()
                    for h in range(DA_H):
                        stt(biasm[:, h, :], step, drel[:, bass.ds(b * DA_H + h, 1)], biasm[:, h, :], ALU.mult, ALU.add)
                    D_()

            def ada_partial(i, before, slot, landed_value):
                dve.wait_ge(landed[slot], landed_value)
                if before is not None:
                    dve.wait_ge(ada_done, before - 2)
                w, part = shaped(ring[:, slot, :], KT, 512), partial[ADA_ORDER.index(i) % 3]
                ts(part, w[:, 0, :], cact[:, 0:1], None, ALU.mult)
                for k in range(1, KT):
                    D_()
                    last = stt(part, w[:, k, :], cact[:, k:k + 1], part, ALU.mult, ALU.add)
                last.then_inc(part_ready, 1)

            dve.wait_ge(c_ready, 1)
            for i in range(ADA_AHEAD):
                ada_partial(i, 3 if i == 3 else None, i, 16)
            dve.wait_ge(acc_free[0], 1)
            dve.wait_ge(acc_free[1], 1)
            dve.wait_ge(fill, 1)
            dve.wait_ge(x_in, 48)
            dve.wait_ge(small_in, 16 * N_SMALL)

            def rope(x1, x2, cos, sin, t1, t2, r1):
                tt(t1, x1, cos, ALU.mult)
                tt(t2, x2, sin, ALU.mult)
                D_()
                tt(r1, t1, t2, ALU.subtract)
                D_()
                tt(t1, x2, cos, ALU.mult)
                tt(t2, x1, sin, ALU.mult)
                D_()
                dve.tensor_copy(x1, r1)
                tt(x2, t1, t2, ALU.add)
                D_()

            with dve.Fori(0, DEPTH) as l:
                def full(use, piece):
                    b = LU.buf[use]
                    dve.wait_ge(acc_full[b], l * LU.per_full[b] + LU.full[use] + piece + 1)
                    return acc[b]

                def freed(use):
                    b = LU.buf[use]
                    dve.wait_ge(acc_free[b], l * LU.per_turn[b] + LU.turn[use] + 1)

                def free(use):
                    return acc_free[LU.buf[use]], 1

                def scale_x(n, scale):
                    dve.wait_ge(x_rt, 2 * l + n + 1)
                    dve.reciprocal(rstd, rstd)
                    D_()
                    for k in range(KT):
                        stt(hT[:, k, :], xT[:, k, :], scale[:, k:k + 1], rstd, ALU.mult, ALU.mult).then_inc(h_scaled, 1)

                def add_to_x(src, k0, gain, use=None):
                    for j in range(4):
                        last = stt(xT[:, k0 + j, :], src[:, SEQ * j:SEQ * j + SEQ], gain[:, k0 + j:k0 + j + 1],
                                   xT[:, k0 + j, :], ALU.mult, ALU.add)
                    if use:
                        last.then_inc(*free(use))
                    D_().then_inc(x_new, 1)

                def ada(i):
                    slot, value = LAYER_RING[f"ada{i}"]
                    ada_partial(i, l * 12 + ADA_AHEAD + ADA_ORDER.index(i), slot, l * LAYER_LANDED[slot] + value)

                one = lambda ap: ap[:, bass.ds(l, 1)]
                dve.tensor_copy(cc[:, 0:V_SUB + 1].unsqueeze(1), one(cols)[:, :, 0:V_SUB + 1])
                dve.tensor_copy(cc[:, V_SW:V_END].unsqueeze(1), one(cols)[:, :, V_SW:V_END])
                dve.tensor_copy(rc.unsqueeze(1), one(rows))
                dve.tensor_copy(lami, shaped(kc[:, K_LAM:K_LAM + 4], 2, 2)[:, :, bass.ds(l, 1)].rearrange("p a b -> p (a b)"))
                D_().then_inc(cur_ready, 1)
                ts(swh, cc[:, V_SW:V_SB + 16], 0.5, None, ALU.mult)
                stt(wqk, cc[:, V_DQ:V_DQ + 1], DA_D ** -0.5, cc[:, V_DK:V_DK + 1], ALU.mult, ALU.mult)
                tt(subw, cc[:, V_SUB:V_SUB + 1], lami[:, 1:2], ALU.mult)
                ts(rc[:, R_MQ:R_MQ + ML_QK], rc[:, R_MQ:R_MQ + ML_QK], ML_QK ** -0.5, None, ALU.mult)
                lp = shaped(rc[:, R_LP:R_END], 2, 2, DA_D)
                tt(shaped(lamp, 2, DA_D), lp[:, :, 0, :], lp[:, :, 1, :], ALU.mult)
                D_()
                dve.tensor_reduce(lamv[:, 0:2], shaped(lamp, 2, DA_D), AX, ALU.add).then_inc(lam_arg, 1)
                dve.wait_ge(al_exp, l + 1)
                ts(anega, anega, -1.0, None, ALU.mult)
                dve.wait_ge(lam_exp, l + 1)
                tt(lamv[:, 6:7], lamv[:, 5:6], lamv[:, 4:5], ALU.subtract)
                D_()
                tt(lamv[:, 7:8], lamv[:, 6:7], lami[:, 0:1], ALU.subtract)
                dve.wait_ge(ada_done, 12 * l + ADA_AHEAD)
                tt(mod[:, 0:16], pmod[:, 0:16], cc[:, V_ADA:V_ADA + 16], ALU.add)
                D_()
                stt(amix, mod[:, 8:16], 1.0, cc[:, V_NM:V_NM + KT], ALU.add, ALU.mult)
                D_()
                scale_x(0, amix)

                with dve.If(l < 1):
                    positions_and_angles()
                    bias_steps(1, B1)
                freed("q")
                freed("k")
                dve.tensor_reduce(ss[:, 0:32], sqqk.rearrange("p i t (g d) -> p (i t g) d", d=DA_D), AX, ALU.add).then_inc(qk_ss, 1)
                dve.wait_ge(qk_rt, l + 1)
                dve.reciprocal(rs[:, 0:32], rs[:, 0:32])
                D_()
                heads = qk.rearrange("p i t (g d) -> p (i t g) d", d=DA_D)
                tt(heads, heads, bc(rs[:, 0:32], 2, DA_D), ALU.mult).then_inc(qk_n, 1)
                with dve.If(l < 1):
                    bias_steps(B1, B2)
                dve.wait_ge(ml_rt, l + 1)
                dve.reciprocal(rsl[:, :, 0:2], rsl[:, :, 0:2])
                D_()
                for t in range(T):
                    ts(ml[:, t, 0:Q_RANK], ml[:, t, 0:Q_RANK], rsl[:, t, 0:1], None, ALU.mult)
                    last = ts(ml[:, t, Q_RANK:Q_RANK + KV_RANK], ml[:, t, Q_RANK:Q_RANK + KV_RANK], rsl[:, t, 1:2], None, ALU.mult)
                last.then_inc(c_n, 1)
                tt(dtn, ml[:, :, ML_W:ML_W + SM_H], bc(rc[:, R_DTB:R_DTB + SM_H], 1, T), ALU.add)
                D_()
                ts(dt, dtn, -1.0, None, ALU.mult)
                D_()
                tt(dt, dt, dtn, ALU.min).then_inc(dt_abs, 1)
                with dve.If(l < 1):
                    bias_steps(B2, B3)
                dve.wait_ge(dt_ln, l + 1)
                stt(dt, dtn, 0.0, dt, ALU.max, ALU.add)
                D_()
                tt(da, dt, bc(anega, 1, T), ALU.mult).then_inc(dt_ready, 1)
                dve.wait_ge(rope_done, 1)
                tt(krr, ml[:, :, Q_RANK + KV_RANK:ML_W], bc(rc[:, R_MK + ML_N:R_MK + ML_QK], 1, T), ALU.mult)
                D_()
                rope(krr[:, :, 0:16], krr[:, :, 16:32], rcos, rsin, tmp1[:, :, 0, :], tmp2[:, :, 0, :], rot1[:, :, 0, :])
                with dve.If(l < 1):
                    bias_steps(B3, B4)
                dve.wait_ge(cs_full, l + 1)
                dve.tensor_copy(csb, shaped(pmod[:, 48:80], T, SM_H)).then_inc(cs_out, 1)
                with dve.If(l < 1):
                    bias_steps(B4, BUCKETS)

                qheads, kheads = qb.rearrange("p t h n -> p (t h) n"), kb.rearrange("p t h n -> p (t h) n")

                def latent_sums():
                    dve.wait_ge(m_sq, l + 1)
                    dve.tensor_reduce(ss[:, 0:16], sqq.rearrange("p t h n -> p (t h) n"), AX, ALU.add)
                    dve.tensor_reduce(ss[:, 16:32], sqk.rearrange("p t h n -> p (t h) n"), AX, ALU.add)
                    D_()
                    for t in range(T):
                        last = ts(ss[:, 16 + 8 * t:24 + 8 * t], ss[:, 16 + 8 * t:24 + 8 * t], ssl[:, t, 2:3], None, ALU.add)
                    last.then_inc(m_ss, 1)

                def latent_norms():
                    dve.wait_ge(m_rt, l + 1)
                    dve.reciprocal(rs[:, 0:32], rs[:, 0:32])
                    D_()
                    tt(qheads, qheads, bc(rs[:, 0:16], 2, ML_QK), ALU.mult)
                    for t in range(T):
                        tt(kb[:, t, :, 0:ML_N], shaped_kv(kv)[:, t, :, 0:ML_N], bc(rs[:, 16 + 8 * t:24 + 8 * t], 2, ML_N), ALU.mult)
                        tt(kb[:, t, :, ML_N:], bc(krr[:, t, :], 1, ML_H), bc(rs[:, 16 + 8 * t:24 + 8 * t], 2, ML_R), ALU.mult)
                    D_()

                def latent_gains():
                    tt(qheads, qheads, bc(rc[:, R_MQ:R_MQ + ML_QK], 1, T * ML_H), ALU.mult)
                    tt(kheads[:, :, 0:ML_N], kheads[:, :, 0:ML_N], bc(rc[:, R_MK:R_MK + ML_N], 1, T * ML_H), ALU.mult)
                    D_()

                def latent_rope():
                    rope(qb[:, :, :, ML_N:ML_N + 16], qb[:, :, :, ML_N + 16:], bc(rcos, 2, ML_H), bc(rsin, 2, ML_H), tmp1, tmp2, rot1)
                    D_().then_inc(m_n, 1)

                latent_sums()

                for n in range(3):
                    t, h0, nh, nk = [(0, 0, 4, 1), (1, 0, 2, 2), (1, 2, 2, 2)][n]
                    K = P * nk
                    k0 = P if t else 0
                    dve.wait_ge(s_full, l * 6 + n + 1)
                    maps = [shaped(S[:, 512 * m:512 * m + K * nh], nh, K) for m in range(2)]
                    for m in range(2):
                        tt(maps[m], shaped(aux[:, 512 * m:512 * m + K * nh], nh, K), biasm[:, h0:h0 + nh, k0:k0 + K], ALU.add)
                    D_()
                    for m in range(2):
                        last = dve.tensor_reduce(nmx[:, nh * m:nh * m + nh], maps[m], AX, ALU.max, negate=True)
                    last.then_inc(s_max, 1)
                    dve.wait_ge(p_exp, l * 6 + n + 1)
                    dve.reciprocal(rps[:, 0:2 * nh], psums[:, 0:2 * nh])
                    D_()
                    ts(nlr[:, 0:nh], rps[:, nh:2 * nh], lamv[:, 7:8], None, ALU.mult)
                    D_()
                    for i in range(nh):
                        ts(maps[1][:, i, :], maps[1][:, i, :], nlr[:, i:i + 1], None, ALU.mult)
                    D_()
                    for i in range(nh):
                        last = stt(maps[0][:, i, :], maps[0][:, i, :], rps[:, i:i + 1], maps[1][:, i, :], ALU.mult, ALU.add)
                    last.then_inc(w_mix, 1)
                    (latent_norms, latent_gains, latent_rope)[n]()
                dve.wait_ge(oa_rt, l + 1)
                dve.reciprocal(sso, sso)
                D_()
                heads = o.rearrange("p t (h d) -> p (t h) d", d=2 * DA_D)
                tt(heads, heads, bc(sso.rearrange("p t h -> p (t h)"), 2, 2 * DA_D), ALU.mult).then_inc(oa_n, 1)
                dve.wait_ge(ada_done, 12 * l + ADA_AHEAD + ADA_POOL)
                tt(mod[:, 16:36], pmod[:, 16:36], cc[:, V_ADA + 16:V_ADA + 36], ALU.add)
                D_()
                ts(gmh, mod[:, 16:24], 0.5, None, ALU.mult)

                for n in range(3):
                    t, h0, nh, nk = [(0, 0, 8, 1), (1, 0, 4, 2), (1, 4, 4, 2)][n]
                    K = P * nk
                    dve.wait_ge(s_full, l * 6 + 3 + n + 1)
                    mask = kc[:, K_CM + (P if t else 0):K_CM + (P if t else 0) + K]
                    tt(shaped(S, nh, K), shaped(aux, nh, K), bc(mask, 1, nh), ALU.add)
                    D_()
                    dve.tensor_reduce(nmx[:, 0:nh], shaped(S, nh, K), AX, ALU.max, negate=True).then_inc(s_max, 1)
                    if n < 2:
                        for u in range(T):
                            dve.wait_ge(z_tanh, 4 * l + 2 * n + u + 1)
                            part = zb[:, u, 512 * n:512 * n + 512]
                            last = stt(part, part, 1.0, acc[LU.buf[f"z{n}"]][:, 512 * u:512 * u + 512], ALU.add, ALU.mult)
                        last.then_inc(*free(f"z{n}"))
                    else:
                        for u in range(2):
                            part = gates[:, 0, 4 * u:4 * u + 4, :].rearrange("p k n -> p (k n)")
                            stt(part, part, 1.0, full(f"ba{u}", 3), ALU.add, ALU.mult).then_inc(*free(f"ba{u}"))
                    dve.wait_ge(p_exp, l * 6 + 3 + n + 1)
                    dve.reciprocal(rps[:, 0:nh], psums[:, 0:nh])
                    D_()
                    dve.wait_ge(o_full, l * 6 + 3 + n + 1)
                    tt(shaped(o[:, t, ML_V * h0:ML_V * (h0 + nh)], nh, ML_V), shaped(aux2[:, 0:ML_V * nh], nh, ML_V),
                       bc(rps[:, 0:nh], 2, ML_V), ALU.mult).then_inc(o_out, 1)

                for c in range(4):
                    dve.wait_ge(tap0, 16 * l + 4 * c + 4)
                    for k in (2, 1, 0):
                        d = 3 - k
                        for j in range(4):
                            f = 4 * c + j
                            last = stt(xb[:, f, d:], acc[LU.buf[f"xbc{c}"]][:, SEQ * j:SEQ * j + SEQ - d], swh[:, 16 * k + f:16 * k + f + 1],
                                       xb[:, f, d:], ALU.mult, ALU.add)
                        if k:
                            D_()
                    last.then_inc(*free(f"xbc{c}"))
                    dve.wait_ge(c_tanh, 4 * l + c + 1)
                    part = xb[:, 4 * c:4 * c + 4, :].rearrange("p h n -> p (h n)")
                    stt(part, th, 1.0, part, ALU.add, ALU.mult).then_inc(xb_ready, 1)

                def decay_rows(hc):
                    t, h0 = hc // 2, 8 * (hc % 2)
                    tt(tria, bc(tri, 1, 8), bc(da[:, t, h0:h0 + 8], 2, P), ALU.mult).then_inc(tria_ready, 1)

                def take_cb(t):
                    dve.wait_ge(cb_full, 2 * l + t + 1)
                    tt(cbm, shaped(aux2, SM_G, P), bc(tri, 1, SM_G), ALU.mult).then_inc(cb_out, 1)

                def branch_b(u):
                    part = gates[:, 1, 4 * u:4 * u + 4, :].rearrange("p k n -> p (k n)")
                    stt(part, part, 1.0, full(f"bb{u}", 3), ALU.add, ALU.mult).then_inc(*free(f"bb{u}"))

                def gate_y(t):
                    stt(y[:, t, :], y[:, t, :], 0.5, zb[:, t, :], ALU.mult, ALU.mult).then_inc(y_gated, 1)

                def norm_y(t):
                    dve.wait_ge(y_rt, 2 * l + t + 1)
                    dve.reciprocal(rs[:, SM_G * t:SM_G * t + SM_G], rs[:, SM_G * t:SM_G * t + SM_G])
                    D_()
                    groups = y[:, t, :].rearrange("p (g n) -> p g n", g=SM_G)
                    tt(groups, groups, bc(rs[:, SM_G * t:SM_G * t + SM_G], 2, D // SM_G), ALU.mult).then_inc(y_n, 1)

                decay_rows(0)
                dve.wait_ge(xs_out, 2 * l + 2)
                for t in range(T):
                    tt(shaped(xdt[:, t, :], SM_H, SM_D), shaped(xs[:, t, :], SM_H, SM_D), bc(dt[:, t, :], 2, SM_D), ALU.mult)
                branch_b(0)
                take_cb(0)
                for hc in range(4):
                    t, h0 = hc // 2, 8 * (hc % 2)
                    dve.wait_ge(r_full, 4 * l + hc + 1)
                    tt(E, shaped(aux, 8, P), bc(csb[:, t, h0:h0 + 8], 2, P), ALU.subtract)
                    D_()
                    ts(E, E, 0.0, None, ALU.min).then_inc(seg_ready, 1)
                    if hc < 3:
                        decay_rows(hc + 1)
                    half_y, half_x = y[:, t, SM_D * h0:SM_D * (h0 + 8)], xs[:, t, SM_D * h0:SM_D * (h0 + 8)]
                    tt(shaped(half_y, 8, SM_D), shaped(half_x, 8, SM_D), bc(rc[:, R_SD + h0:R_SD + h0 + 8], 2, SM_D), ALU.mult)
                    D_()
                    dve.wait_ge(seg_exp, 4 * l + hc + 1)
                    if t == 0:
                        tt(xe[:, h0:h0 + 8, :], shaped(xdt[:, t, SM_D * h0:SM_D * (h0 + 8)], 8, SM_D),
                           E[:, :, P - 1:P].to_broadcast([P, 8, SM_D]), ALU.mult)
                        D_()
                    groups = E.rearrange("p (g r) n -> p g r n", g=2)
                    tt(groups, groups, bc(cbm[:, h0 // 4:h0 // 4 + 2, :], 2, 4), ALU.mult).then_inc(m_ready, 1)
                    if hc == 0:
                        branch_b(1)
                        D_()
                        g0, g1 = (gates[:, n].rearrange("p k n -> p (k n)") for n in range(2))
                        tt(g0, g0, g1, ALU.add).then_inc(merged_b, 1)
                    if hc == 2:
                        gate_y(0)
                    dve.wait_ge(y_full, 4 * l + hc + 1)
                    tt(half_y, half_y, aux2, ALU.add).then_inc(y_out, 1)
                    if hc == 1:
                        take_cb(1)
                norm_y(0)
                dve.wait_ge(yo_full, l + 1)
                dve.wait_ge(ecs_out, l + 1)
                off = E.rearrange("p h n -> p (h n)")
                tt(shaped(off, SM_H, SM_D), shaped(aux, SM_H, SM_D), bc(ecs[:, 1, :], 2, SM_D), ALU.mult).then_inc(yo_out, 1)
                D_()
                tt(y[:, 1, :], y[:, 1, :], off, ALU.add)
                D_()
                gate_y(1)
                norm_y(1)
                dve.wait_ge(ysT_t, 3 * l + 2)
                tt(ysT[:, 0:4, P:2 * P], shaped(aux[:, 0:512], 4, P), bc(cc[:, V_SN:V_SN + 4], 2, P), ALU.mult).then_inc(ysT_out, 1)
                ada(9)
                freed("gc0")
                freed("gc1")
                for i in range(2):
                    part, total = (gates[:, n, 4 * i:4 * i + 4, :].rearrange("p k n -> p (k n)") for n in (1, 0))
                    stt(part, part, 1.0, full(f"bc{i}", 3), ALU.add, ALU.mult).then_inc(*free(f"bc{i}"))
                    D_()
                    last = tt(total, total, part, ALU.add)
                    if i == 0:
                        ada(10)
                last.then_inc(merged, 1)
                ada(11)
                for i in range(2):
                    add_to_x(full(f"wo{i}", 3), 4 * i, gmh, f"wo{i}")
                    if i == 0:
                        dve.wait_ge(ada_done, 12 * l + 12)
                        tt(mod[:, 36:48], pmod[:, 36:48], cc[:, V_ADA + 36:V_ADA + 48], ALU.add)
                        D_()
                        stt(affn, mod[:, 32:40], 1.0, cc[:, V_NF:V_NF + KT], ALU.add, ALU.mult)

                scale_x(1, affn)
                for i in range(11):
                    dve.wait_ge(u_tap, 44 * l + 4 * i + 4)
                    for k in (1, 0):
                        d = 2 - k
                        for j in range(4):
                            f = (0, FT)[j // 2] + 2 * i + j % 2
                            last = stt(u4[:, i % 2, j, d:], acc[LU.buf[f"up{i}"]][:, SEQ * j:SEQ * j + SEQ - d],
                                       cc[:, V_FW + 2 * FT * k + f:V_FW + 2 * FT * k + f + 1], u4[:, i % 2, j, d:], ALU.mult, ALU.add)
                        if k:
                            D_()
                    last.then_inc(*free(f"up{i}"))
                    dve.wait_ge(u_silu, 11 * l + i + 1)
                    tt(act[:, 2 * i:2 * i + 2, :].rearrange("p h n -> p (h n)"), sl[:, i % 2, :],
                       u4[:, i % 2, 2:4, :].rearrange("p h n -> p (h n)"), ALU.mult).then_inc(act_ready, 1)
                for i in range(ADA_AHEAD):
                    ada(i)
                dve.wait_ge(dn_done, 6 * l + 12)
                add_to_x(acc[LU.buf["dn0"]], 0, mod[:, 40:48], "dn0")
                add_to_x(aux, 4, mod[:, 40:48])

            def norm_x(n, gain):
                dve.wait_ge(x_rt, 2 * DEPTH + n)
                dve.reciprocal(rstd, rstd)
                D_()
                for k in range(KT):
                    stt(hT[:, k, :], xT[:, k, :], gain[:, k:k + 1], rstd, ALU.mult, ALU.mult).then_inc(h_ready, 1)

            norm_x(1, cols2[:, W_N1:W_OA])
            dve.wait_ge(late_in, 16 * 6)
            ts(qn2, qn2, D2 ** -0.5, None, ALU.mult)
            for name in ("m_qa", "m_kva"):
                dve.wait_ge(acc_free[MU.buf[name]], MU.turn[name] + 1)
            dve.tensor_reduce(ss[:, 0:16], sqa2.rearrange("p t (h d) -> p (t h) d", d=D2), AX, ALU.add)
            dve.tensor_reduce(ss[:, 16:20], sqk2.rearrange("p t (h d) -> p (t h) d", d=D2), AX, ALU.add).then_inc(a2_ss, 1)
            dve.wait_ge(a2_rt, 1)
            dve.reciprocal(rs[:, 0:20], rs[:, 0:20])
            D_()
            qh, kh = qa2.rearrange("p t (h d) -> p (t h) d", d=D2), ka2.rearrange("p t (h d) -> p (t h) d", d=D2)
            tt(qh, qh, bc(rs[:, 0:16], 2, D2), ALU.mult)
            tt(kh, kh, bc(rs[:, 16:20], 2, D2), ALU.mult)
            D_()
            tt(qh, qh, bc(qn2, 1, 16), ALU.mult)
            tt(kh, kh, bc(kn2, 1, 4), ALU.mult)
            D_()

            def rope2(x, heads, cos, sin):
                v = x.rearrange("p t (h s d) -> p t h s d", s=2, d=32)
                c, s = (bc(shaped(kc[:, at:at + 64], T, 32), 2, heads) for at in (cos, sin))
                rope(v[:, :, :, 0, :], v[:, :, :, 1, :], c, s, rt1[:, :, 0:heads], rt2[:, :, 0:heads], rr1[:, :, 0:heads])

            rope2(qa2, H2, K_AC, K_AS)
            rope2(ka2, 2, K_AC, K_AS)
            for i in range(2):
                for t in range(T):
                    dve.tensor_copy(kd2[:, t, :, i, :], shaped(ka2[:, t, :], 2, D2))
            D_().then_inc(a2_n, 1)
            for name in ("m_qb", "m_kb"):
                dve.wait_ge(acc_free[MU.buf[name]], MU.turn[name] + 1)
            rope2(qb2, H2, K_LC, K_LS)
            rope2(kb2, H2, K_LC, K_LS)
            D_().then_inc(b2_n, 1)

            def take_output(u):
                t, n = u // 2 % 2, u // 4
                dve.wait_ge(o2_full, u + 1)
                dst = o2[n][:, t, 256 * (u % 2):256 * (u % 2) + 256].rearrange("p (i m d) -> p i m d", i=2, m=2)
                r = rps[:, 4 * (u % 2):4 * (u % 2) + 4].rearrange("p (m i) -> p i m", m=2)
                tt(dst, shaped(aux2[:, 0:256], 2, 2, D2), bc(r, 3, D2), ALU.mult).then_inc(o2_out, 1)

            def norm_output(n):
                D_().then_inc(on_ss, 1)
                dve.wait_ge(on_ss, 2 * n + 2)
                dve.reciprocal(ssq, ssq)
                D_()
                for t in range(T):
                    last = ts(o2[n][:, t, :], o2[n][:, t, :], ssq[:, t:t + 1], None, ALU.mult)
                last.then_inc(on_n, 1)

            def output_T(n):
                dve.wait_ge(oT_t, n + 1)
                gain = cols2[:, (W_OA, W_OB)[n]:(W_OA, W_OB)[n] + 4]
                tt(hT[:, 4 * n:4 * n + 4, :], shaped(aux, 4, SEQ), bc(gain, 2, SEQ), ALU.mult).then_inc(oT_out, 1)

            for u in range(8):
                b, t = u % 2, u // 2 % 2
                dve.wait_ge(s2_full, u + 1)
                src = shaped(acc[b], 4, SEQ)
                if u >= 4:
                    dst = shaped(S2[b], 4, SEQ)
                    tt(dst, src, bc(kc[:, K_LNC + SEQ * t:K_LNC + SEQ * (t + 1)], 1, 4), ALU.add)
                    D_()
                    src = dst
                dve.tensor_reduce(nmx[:, 4 * b:4 * b + 4], src, AX, ALU.max, negate=True).then_inc(s2_max, 1)
                if u:
                    take_output(u - 1)
                if u == 4:
                    norm_output(0)
                if u == 5:
                    output_T(0)
                dve.wait_ge(p2_exp, u + 1)
                dve.reciprocal(rps[:, 4 * b:4 * b + 4], psums[:, 4 * b:4 * b + 4])
                D_()
            take_output(7)
            norm_output(1)
            output_T(1)
            for i in range(2):
                name = f"m_wo{i}"
                dve.wait_ge(acc_full[MU.buf[name]], MU.full[name] + 4)
                part = xT[:, 4 * i:4 * i + 4, :].rearrange("p k n -> p (k n)")
                tt(part, part, acc[MU.buf[name]], ALU.add).then_inc(x_new, 1)

            norm_x(2, cols2[:, W_N2:W_FN])

            def first_of(dst, x, best, n):
                dve.tensor_reduce(best, x, AX, ALU.max)
                D_()
                tt(dst, x, bc(best, 2, n), ALU.is_equal)
                D_()
                tt(ev[:, :, 0:n], dst, bc(kc[:, K_TIE:K_TIE + n], 1, T), ALU.mult)
                D_()
                dve.tensor_reduce(vm, ev[:, :, 0:n], AX, ALU.max)
                D_()
                tt(dst, ev[:, :, 0:n], bc(vm, 2, n), ALU.is_equal)
                D_()

            dve.wait_ge(lg_full, 1)
            tt(lg, shaped(pmod[:, 128:200], T, 36), bc(rb2, 1, T), ALU.add)
            D_()
            first_of(og, lg[:, :, 0:GROUPS], gm, GROUPS)
            D_().then_inc(og_ready, 1)
            tt(ge, lg[:, :, 0:GROUPS], bc(gm, 2, GROUPS), ALU.subtract).then_inc(lg_sub, 1)
            tt(em, lg[:, :, GROUPS:].rearrange("p t (g e) -> p t g e", g=GROUPS), bc(og, 3, EPG), ALU.mult)
            D_()
            dve.tensor_reduce(ei, em.rearrange("p t g e -> p t e g"), AX, ALU.add)
            D_()
            first_of(o1, ei, m1, EPG)
            stt(ei, o1, NEG, ei, ALU.mult, ALU.add)
            D_()
            first_of(o2nd, ei, m2, EPG)
            tt(m2, m2, m1, ALU.subtract).then_inc(top_sub, 1)
            dve.wait_ge(lg_exp, 1)
            dve.tensor_reduce(gp, ge, AX, ALU.add)
            D_()
            dve.reciprocal(gp, gp)
            dve.wait_ge(top_exp, 1)
            ts(w1, w2, 1.0, None, ALU.add)
            D_()
            dve.reciprocal(w1, w1)
            D_()
            tt(w1, w1, gp, ALU.mult)
            D_()
            tt(w2, w2, w1, ALU.mult)
            tt(o1, o1, bc(w1, 2, EPG), ALU.mult)
            D_()
            tt(o2nd, o2nd, bc(w2, 2, EPG), ALU.mult)
            D_()
            tt(gate8, o1, o2nd, ALU.add)
            dve.wait_ge(pos_full, 1)
            tt(psl[:, :, 0:GROUPS], shaped(pmod[:, 256:264], T, GROUPS), og, ALU.mult)
            ts(over, pmod[:, 264:268], float(P), None, ALU.is_gt)
            D_()
            ts(psl[:, :, 0:GROUPS], psl[:, :, 0:GROUPS], -1.0, None, ALU.add)
            tt(metaf[:, 0:GROUPS], over, kc[:, K_IOTA:K_IOTA + GROUPS], ALU.mult)
            D_()
            ts(psl[:, :, GROUPS + 1], psl[:, :, 0], 0.0, -1.0, ALU.mult, ALU.add)
            dve.tensor_reduce(psl[:, :, GROUPS], psl[:, :, 0:GROUPS], AX, ALU.max)
            dve.tensor_reduce(metaf[:, 4:5], metaf[:, 0:GROUPS], AX, ALU.add)
            dve.tensor_reduce(metaf[:, 5:6], over, AX, ALU.add)
            D_()
            ts(psl[:, :, GROUPS], psl[:, :, GROUPS], -float(P), None, ALU.add)
            ts(metaf[:, 5:6], metaf[:, 5:6], float(GROUPS), None, ALU.add)
            dve.tensor_copy(metaf[:, 0:GROUPS], kc[:, K_IOTA:K_IOTA + GROUPS])
            D_()
            dve.tensor_copy(meta[:, 0:6], metaf[:, 0:6])
            D_().then_inc(routed, 1)
            D_().then_inc(x_added, 1)
            passes = dve.value_load(meta[0:1, 5:6], min_val=GROUPS, max_val=GROUPS + 1)

            def match_slots(p):
                for t in range(T):
                    last = ts(pm[:, t, :], kc[:, K_IOTA:K_IOTA + P], psl[:, t, bass.ds(p, 1)], None, ALU.is_equal)
                last.then_inc(pm_ready, 1)

            match_slots(0)
            with dve.Fori(0, passes) as p:
                dve.wait_ge(pt_full, p + 1)
                dve.tensor_copy(gsl, pmod[:, 300:300 + EPG])
                dve.tensor_copy(pmT, aux2[:, 0:SEQ]).then_inc(pt_out, 1)
                D_()
                for e in range(EPG):
                    dve.wait_ge(g_silu, p * EPG + e + 1)
                    dve.wait_ge(u_full, p * EPG + EPG + e + 1)
                    stt(he[:, e % 2, :], hs[:, e % 2, :], gsl[:, e:e + 1], acc[e % 2][:, DE:2 * DE], ALU.mult, ALU.mult)\
                        .then_inc(he_ready, 1)
                match_slots(p + 1)
                dve.wait_ge(sc_full, p + 1)
                for i in range(2):
                    part = xT[:, 4 * i:4 * i + 4, :].rearrange("p k n -> p (k n)")
                    last = tt(part, part, (acc[1], aux)[i], ALU.add)
                last.then_inc(x_added, 1)
            D_().then_inc(x_new, 2)
            norm_x(3, cols2[:, W_FN:W_END])


ARGS = [
    "x", "c", "positions", "rel_bias", "ada_w", "ada_b", "norm_mix", "norm_ffn", "w_in", "da_q_norm", "da_k_norm",
    "da_lambda", "da_subln", "mla_q_a_norm", "mla_kv_a_norm", "mla_w_uq", "mla_w_ukv", "mla_q_norm",
    "mla_k_norm", "ssm_conv_w", "ssm_conv_b", "ssm_dt_bias", "ssm_a_log", "ssm_d", "ssm_norm", "w_branch_a",
    "w_branch_b", "w_branch_c", "w_out", "ffn_w_up", "ffn_conv_w", "ffn_conv_b", "ffn_w_down", "norm1_g_2",
    "w_in_2", "q_norm_g_2", "k_norm_g_2", "out_norm_a_g_2", "out_norm_b_g_2", "w_out_2", "norm2_g_2",
    "router_group_w_2", "router_group_b_2", "router_expert_w_2", "router_expert_b_2", "w_gate_2", "w_up_2",
    "w_down_2", "final_norm_g_2",
]


def kernel(**inputs):
    import numpy as _np
    import concourse.bacc as _bacc
    from concourse.bass_utils import run_bass_kernel_spmd as _run

    nc = _bacc.Bacc("TRN2", target_bir_lowering=False, num_devices=1)
    arrays, args = {}, {}
    for name in ARGS:
        v = _np.ascontiguousarray(inputs[name])
        arrays[f"in_{name}"] = v
        args[name] = nc.dram_tensor(f"in_{name}", v.shape, mybir.dt.from_np(v.dtype), kind="ExternalInput").ap()
    arrays["shape_constants"] = shape_constants()
    consts = nc.dram_tensor("shape_constants", (P, K_END), F32, kind="ExternalInput").ap()
    out = nc.dram_tensor("out", (1, SEQ, D), F32, kind="ExternalOutput").ap()
    program(nc, args, consts, out)
    r = _run(nc, [arrays], core_ids=[0])
    return r.results[0]["out"]
```
